# Optimizing a Trainium2 kernel written in Bass

```python
import jax, jax.numpy as jnp
from jax import lax
import numpy as np

D_MODEL = 1024
BATCH = 1
SEQ = 512
DEPTH = 2

EPS = 1e-6
RWKV_HEADS = 8
RWKV_HEAD_DIM = 64
RWKV_DIM = RWKV_HEADS * RWKV_HEAD_DIM
DECAY_LORA = 64
AAA_LORA = 64
GATE_LORA = 160
RWKV_IN = 3 * RWKV_DIM + DECAY_LORA + AAA_LORA + GATE_LORA
GN_EPS = 64e-5
MLA_HEADS = 4
MLA_NOPE = 64
MLA_ROPE = 32
MLA_QK = MLA_NOPE + MLA_ROPE
MLA_V = 64
MLA_DIM = MLA_HEADS * MLA_V
Q_LORA = 192
KV_LORA = 128
MLA_IN = Q_LORA + KV_LORA + MLA_ROPE
ROPE_THETA = 10000.0
Q_BLOCK = 128
GMLP_GROUPS = 4
GMLP_GROUP_DIM = 64
GMLP_DIM = GMLP_GROUPS * GMLP_GROUP_DIM
CHUNK = 128
GMLP_IN = 2 * GMLP_DIM
N_IN = RWKV_IN + MLA_IN + GMLP_IN
D_MIX = RWKV_DIM + MLA_DIM + GMLP_DIM
MEM_TOKENS = 256
MEM_HEADS = 4
MEM_HEAD_DIM = 64
MEM_DIM = MEM_HEADS * MEM_HEAD_DIM
N_GROUPS = 4
EXPERTS_PER_GROUP = 8
N_EXPERTS = N_GROUPS * EXPERTS_PER_GROUP
TOP_K = 2
D_EXPERT = 512
MOE_BLOCK = 128

kernel_name = 'hybrid_rwkv7_mla_gmlp_memxattn_hmoe'

def rms_norm(x, g, eps=EPS):
    xf = x.astype(jnp.float32)
    y = xf * lax.rsqrt(jnp.mean(xf * xf, axis=-1, keepdims=True) + eps)
    return (y * g.astype(jnp.float32)).astype(x.dtype)

def token_shift(p, mu):
    prev = jnp.concatenate([jnp.zeros_like(p[:, :1]), p[:, :-1]], axis=1)
    return p + (prev - p) * mu

def rope(x, pos):
    half = x.shape[-1] // 2
    inv = ROPE_THETA ** (-jnp.arange(half, dtype=jnp.float32) * 2.0 / x.shape[-1])
    ang = pos.astype(jnp.float32)[..., None] * inv
    cos = jnp.cos(ang)[:, :, None, :]
    sin = jnp.sin(ang)[:, :, None, :]
    xf = x.astype(jnp.float32)
    x1, x2 = xf[..., :half], xf[..., half:]
    return jnp.concatenate([x1 * cos - x2 * sin, x2 * cos + x1 * sin], axis=-1).astype(x.dtype)

def rwkv7_scan(r, w, k, v, a_, b_):
    B, S, H, N = r.shape
    def step(state, inp):
        r_t, w_t, k_t, v_t, a_t, b_t = inp
        sa = jnp.einsum('bhvk,bhk->bhv', state, a_t)
        state = (state * w_t[:, :, None, :] + sa[..., None] * b_t[:, :, None, :]
                 + v_t[..., None] * k_t[:, :, None, :])
        return state, jnp.einsum('bhvk,bhk->bhv', state, r_t)
    init = jnp.zeros((B, H, N, N), jnp.float32)
    xs = tuple(jnp.moveaxis(t, 1, 0) for t in (r, w, k, v, a_, b_))
    _, ys = lax.scan(step, init, xs)
    return jnp.moveaxis(ys, 0, 1)

def rwkv7_mixer(p, w0, w_up, a0, a_up, g_up, k_k, k_a, r_k, ln_g, ln_b):
    B, S, _ = p.shape
    H, N = RWKV_HEADS, RWKV_HEAD_DIM
    r, k, v, wd, ad, gd = jnp.split(p, np.cumsum([RWKV_DIM, RWKV_DIM, RWKV_DIM, DECAY_LORA, AAA_LORA]).tolist(), axis=-1)
    f32 = jnp.float32
    w_pre = (w0 + jnp.tanh(wd) @ w_up).astype(f32)
    w_log = -jax.nn.softplus(-w_pre) - 0.5
    decay = jnp.exp(-jnp.exp(w_log))
    a = jax.nn.sigmoid((a0 + ad @ a_up).astype(f32))
    g = jax.nn.sigmoid(gd) @ g_up
    hs = lambda t: t.astype(f32).reshape(B, S, H, N)
    r, k, v, decay, a = hs(r), hs(k), hs(v), hs(decay), hs(a)
    kk = k * k_k.astype(f32).reshape(H, N)
    kk = kk / jnp.maximum(jnp.sqrt(jnp.sum(kk * kk, axis=-1, keepdims=True)), 1e-12)
    k = k * (1.0 + (a - 1.0) * k_a.astype(f32).reshape(H, N))
    y = rwkv7_scan(r, decay, k, v, -kk, kk * a)
    mean = jnp.mean(y, axis=-1, keepdims=True)
    var = jnp.mean(jnp.square(y - mean), axis=-1, keepdims=True)
    y = (y - mean) * lax.rsqrt(var + GN_EPS) * ln_g.astype(f32).reshape(H, N) + ln_b.astype(f32).reshape(H, N)
    y = y + jnp.sum(r * k * r_k.astype(f32), axis=-1, keepdims=True) * v
    return (y.reshape(B, S, RWKV_DIM) * g.astype(f32)).astype(p.dtype)

def causal_block_attention(q, k, v):
    B, S, H, Dq = q.shape
    Dv = v.shape[-1]
    nb = S // Q_BLOCK
    qb = q.reshape(B, nb, Q_BLOCK, H, Dq).transpose(1, 0, 2, 3, 4)
    k_pos = jnp.arange(S)
    scale = Dq ** -0.5
    def one(args):
        q_blk, i = args
        s = jnp.einsum('bqhd,bkhd->bhqk', q_blk, k).astype(jnp.float32) * scale
        q_pos = i * Q_BLOCK + jnp.arange(Q_BLOCK)
        s = jnp.where(k_pos[None, :] <= q_pos[:, None], s, -jnp.inf)
        pr = jax.nn.softmax(s, axis=-1).astype(v.dtype)
        return jnp.einsum('bhqk,bkhd->bqhd', pr, v)
    out = lax.map(one, (qb, jnp.arange(nb)))
    return out.transpose(1, 0, 2, 3, 4).reshape(B, S, H * Dv)

def mla_mixer(p, positions, q_norm_g, w_uq, kv_norm_g, w_ukv, q_g, k_g):
    B, S, _ = p.shape
    H = MLA_HEADS
    c_q, c_kv, k_r = jnp.split(p, [Q_LORA, Q_LORA + KV_LORA], axis=-1)
    q = (rms_norm(c_q, q_norm_g) @ w_uq).reshape(B, S, H, MLA_QK)
    kv = (rms_norm(c_kv, kv_norm_g) @ w_ukv).reshape(B, S, H, MLA_NOPE + MLA_V)
    k_nope, v = kv[..., :MLA_NOPE], kv[..., MLA_NOPE:]
    q = jnp.concatenate([q[..., :MLA_NOPE], rope(q[..., MLA_NOPE:], positions)], axis=-1)
    k_rope = jnp.broadcast_to(rope(k_r[:, :, None, :], positions), (B, S, H, MLA_ROPE))
    k = jnp.concatenate([k_nope, k_rope], axis=-1)
    q = rms_norm(q, q_g)
    k = rms_norm(k, k_g)
    return causal_block_attention(q, k, v)

def gmlp_mixer(p, v_norm_g, ws, b):
    B, S, _ = p.shape
    G, Dg = GMLP_GROUPS, GMLP_GROUP_DIM
    z = jax.nn.gelu(p)
    u, v = z[..., :GMLP_DIM], z[..., GMLP_DIM:]
    v = rms_norm(v.reshape(B, S, G, Dg), v_norm_g.reshape(G, Dg))
    v = v.reshape(B, S // CHUNK, CHUNK, G, Dg)
    ws_c = ws * jnp.tril(jnp.ones((CHUNK, CHUNK), ws.dtype))
    sv = jnp.einsum('gts,bcsgd->bctgd', ws_c, v) + b.T[None, None, :, :, None]
    return u * sv.reshape(B, S, GMLP_DIM)

def memory_cross_attention(h, mem_k, mem_v, w_q, q_g, w_o):
    B, S, _ = h.shape
    q = rms_norm((h @ w_q).reshape(B, S, MEM_HEADS, MEM_HEAD_DIM), q_g)
    s = jnp.einsum('bqhd,bkhd->bhqk', q, mem_k).astype(jnp.float32) * (MEM_HEAD_DIM ** -0.5)
    pr = jax.nn.softmax(s, axis=-1).astype(mem_v.dtype)
    o = jnp.einsum('bhqk,bkhd->bqhd', pr, mem_v).reshape(B, S, MEM_DIM)
    return o @ w_o

def grouped_expert_ffn(t, eid, gate, w1, w3, w2):
    N, D = t.shape
    M = eid.shape[0]
    E, BLK = N_EXPERTS, MOE_BLOCK
    tok = jnp.repeat(jnp.arange(N, dtype=jnp.int32), TOP_K)
    order = jnp.argsort(eid)
    s_eid, s_tok, s_gate = eid[order], tok[order], gate[order]
    counts = jnp.bincount(eid, length=E)
    offsets = jnp.cumsum(counts) - counts
    padded = ((counts + BLK - 1) // BLK) * BLK
    p_end = jnp.cumsum(padded)
    p_off = p_end - padded
    dest = p_off[s_eid] + (jnp.arange(M) - offsets[s_eid])
    n_blocks = (M + E * (BLK - 1) + BLK - 1) // BLK
    P = n_blocks * BLK
    row_tok = jnp.full((P,), N, jnp.int32).at[dest].set(s_tok)
    row_gate = jnp.zeros((P,), gate.dtype).at[dest].set(s_gate)
    blk_e = jnp.minimum(jnp.searchsorted(p_end, jnp.arange(n_blocks) * BLK, side='right'), E - 1)
    t_pad = jnp.concatenate([t, jnp.zeros((1, D), t.dtype)], axis=0)
    def one(args):
        rows, e = args
        xb = t_pad[rows]
        hb = jax.nn.silu(xb @ w1[e]) * (xb @ w3[e])
        return hb @ w2[e]
    yb = lax.map(one, (row_tok.reshape(n_blocks, BLK), blk_e)).reshape(P, D)
    yb = yb * row_gate[:, None]
    return jax.ops.segment_sum(yb, row_tok, num_segments=N + 1)[:N]

def hierarchical_moe(h, w_group, b_group, w_expert, b_expert, w1, w3, w2):
    B, S, D = h.shape
    N = B * S
    t = h.reshape(N, D)
    g_prob = jax.nn.softmax((t @ w_group).astype(jnp.float32) + b_group.astype(jnp.float32), axis=-1)
    g_idx = jnp.argmax(g_prob, axis=-1)
    g_w = jnp.take_along_axis(g_prob, g_idx[:, None], axis=-1)[:, 0]
    e_logits = ((t @ w_expert).astype(jnp.float32) + b_expert.astype(jnp.float32)).reshape(N, N_GROUPS, EXPERTS_PER_GROUP)
    e_logits = jnp.take_along_axis(e_logits, g_idx[:, None, None], axis=1)[:, 0]
    e_prob = jax.nn.softmax(e_logits, axis=-1)
    top_p, top_i = lax.top_k(e_prob, TOP_K)
    gate = g_w[:, None] * top_p / jnp.sum(top_p, axis=-1, keepdims=True)
    eid = (g_idx[:, None] * EXPERTS_PER_GROUP + top_i).astype(jnp.int32)
    y = grouped_expert_ffn(t, eid.reshape(-1), gate.reshape(-1), w1, w3, w2)
    return y.reshape(B, S, D).astype(h.dtype)

def setup_inputs(seed: int = 0) -> dict:
    key = jax.random.key(seed)
    ks = jax.random.split(key, 41)
    nrm = lambda k, shape, s: jax.random.normal(k, shape, jnp.float32) * s
    gain = lambda k, shape: 1.0 + 0.05 * jax.random.normal(k, shape, jnp.float32)
    L = DEPTH
    positions = (jax.random.randint(ks[2], (BATCH, 1), 0, 4096)
                 + jnp.arange(SEQ, dtype=jnp.int32)[None, :]).astype(jnp.int32)
    return {
        'x': nrm(ks[0], (BATCH, SEQ, D_MODEL), 1.0),
        'mem': nrm(ks[1], (BATCH, MEM_TOKENS, D_MODEL), 1.0),
        'positions': positions,
        'norm_mix_g': gain(ks[3], (L, D_MODEL)),
        'w_in': nrm(ks[4], (L, D_MODEL, N_IN), D_MODEL ** -0.5),
        'shift_mu': jax.random.uniform(ks[5], (L, RWKV_IN), jnp.float32),
        'rwkv_w0': -0.5 + nrm(ks[6], (L, RWKV_DIM), 0.5),
        'rwkv_w_up': nrm(ks[7], (L, DECAY_LORA, RWKV_DIM), 0.5 * DECAY_LORA ** -0.5),
        'rwkv_a0': nrm(ks[8], (L, RWKV_DIM), 0.1),
        'rwkv_a_up': nrm(ks[9], (L, AAA_LORA, RWKV_DIM), 0.5 * AAA_LORA ** -0.5),
        'rwkv_g_up': nrm(ks[10], (L, GATE_LORA, RWKV_DIM), GATE_LORA ** -0.5),
        'rwkv_k_k': 0.85 + nrm(ks[11], (L, RWKV_DIM), 0.05),
        'rwkv_k_a': gain(ks[12], (L, RWKV_DIM)),
        'rwkv_r_k': nrm(ks[13], (L, RWKV_HEADS, RWKV_HEAD_DIM), 0.1),
        'rwkv_ln_g': gain(ks[14], (L, RWKV_DIM)),
        'rwkv_ln_b': nrm(ks[15], (L, RWKV_DIM), 0.02),
        'mla_q_norm_g': gain(ks[16], (L, Q_LORA)),
        'mla_w_uq': nrm(ks[17], (L, Q_LORA, MLA_HEADS * MLA_QK), Q_LORA ** -0.5),
        'mla_kv_norm_g': gain(ks[18], (L, KV_LORA)),
        'mla_w_ukv': nrm(ks[19], (L, KV_LORA, MLA_HEADS * (MLA_NOPE + MLA_V)), KV_LORA ** -0.5),
        'mla_q_g': gain(ks[20], (L, MLA_QK)),
        'mla_k_g': gain(ks[21], (L, MLA_QK)),
        'gmlp_v_norm_g': gain(ks[22], (L, GMLP_DIM)),
        'gmlp_ws': nrm(ks[23], (L, GMLP_GROUPS, CHUNK, CHUNK), CHUNK ** -0.5),
        'gmlp_b': gain(ks[24], (L, GMLP_GROUPS, CHUNK)),
        'w_out': nrm(ks[25], (L, D_MIX, D_MODEL), D_MIX ** -0.5),
        'mem_norm_g': gain(ks[26], (D_MODEL,)),
        'mem_w_kv': nrm(ks[27], (D_MODEL, 2 * MEM_DIM), D_MODEL ** -0.5),
        'mem_k_g': gain(ks[28], (MEM_HEAD_DIM,)),
        'norm_mem_g': gain(ks[29], (L, D_MODEL)),
        'mem_w_q': nrm(ks[30], (L, D_MODEL, MEM_DIM), D_MODEL ** -0.5),
        'mem_q_g': gain(ks[31], (L, MEM_HEAD_DIM)),
        'mem_w_o': nrm(ks[32], (L, MEM_DIM, D_MODEL), MEM_DIM ** -0.5),
        'norm_ffn_g': gain(ks[33], (L, D_MODEL)),
        'moe_w_group': nrm(ks[34], (L, D_MODEL, N_GROUPS), D_MODEL ** -0.5),
        'moe_b_group': nrm(ks[35], (L, N_GROUPS), 0.01),
        'moe_w_expert': nrm(ks[36], (L, D_MODEL, N_EXPERTS), D_MODEL ** -0.5),
        'moe_b_expert': nrm(ks[37], (L, N_EXPERTS), 0.01),
        'moe_w1': nrm(ks[38], (L, N_EXPERTS, D_MODEL, D_EXPERT), D_MODEL ** -0.5),
        'moe_w3': nrm(ks[39], (L, N_EXPERTS, D_MODEL, D_EXPERT), D_MODEL ** -0.5),
        'moe_w2': nrm(ks[40], (L, N_EXPERTS, D_EXPERT, D_MODEL), D_EXPERT ** -0.5),
    }

def reference(x, mem, positions, norm_mix_g, w_in, shift_mu, rwkv_w0, rwkv_w_up, rwkv_a0, rwkv_a_up,
              rwkv_g_up, rwkv_k_k, rwkv_k_a, rwkv_r_k, rwkv_ln_g, rwkv_ln_b, mla_q_norm_g, mla_w_uq,
              mla_kv_norm_g, mla_w_ukv, mla_q_g, mla_k_g, gmlp_v_norm_g, gmlp_ws, gmlp_b, w_out,
              mem_norm_g, mem_w_kv, mem_k_g, norm_mem_g, mem_w_q, mem_q_g, mem_w_o, norm_ffn_g,
              moe_w_group, moe_b_group, moe_w_expert, moe_b_expert, moe_w1, moe_w3, moe_w2):
    B, S, _ = x.shape
    M = mem.shape[1]
    mkv = (rms_norm(mem, mem_norm_g) @ mem_w_kv).reshape(B, M, 2, MEM_HEADS, MEM_HEAD_DIM)
    mem_k = rms_norm(mkv[:, :, 0], mem_k_g)
    mem_v = mkv[:, :, 1]
    for l in range(DEPTH):
        h = rms_norm(x, norm_mix_g[l])
        proj = h @ w_in[l]
        p_r, p_m, p_g = jnp.split(proj, [RWKV_IN, RWKV_IN + MLA_IN], axis=-1)
        o_r = rwkv7_mixer(token_shift(p_r, shift_mu[l]), rwkv_w0[l], rwkv_w_up[l], rwkv_a0[l], rwkv_a_up[l],
                          rwkv_g_up[l], rwkv_k_k[l], rwkv_k_a[l], rwkv_r_k[l], rwkv_ln_g[l], rwkv_ln_b[l])
        o_m = mla_mixer(p_m, positions, mla_q_norm_g[l], mla_w_uq[l], mla_kv_norm_g[l], mla_w_ukv[l],
                        mla_q_g[l], mla_k_g[l])
        o_g = gmlp_mixer(p_g, gmlp_v_norm_g[l], gmlp_ws[l], gmlp_b[l])
        x = x + jnp.concatenate([o_r, o_m, o_g], axis=-1) @ w_out[l]
        h = rms_norm(x, norm_mem_g[l])
        x = x + memory_cross_attention(h, mem_k, mem_v, mem_w_q[l], mem_q_g[l], mem_w_o[l])
        h = rms_norm(x, norm_ffn_g[l])
        x = x + hierarchical_moe(h, moe_w_group[l], moe_b_group[l], moe_w_expert[l], moe_b_expert[l],
                                 moe_w1[l], moe_w3[l], moe_w2[l])
    return x


_drawn_inputs = setup_inputs


def setup_inputs(seed=0):
    import zlib

    import numpy as np

    out = dict(_drawn_inputs(seed))
    spreads = {}
    factors = {'rwkv_k_k': 3.087,
     'mla_q_norm_g': 3.313,
     'mla_q_g': 2.731,
     'norm_mem_g': 3.492,
     'mem_q_g': 3.064,
     'moe_b_group': 6.072}
    for name, (base, spread) in spreads.items():
        noise = np.random.default_rng([zlib.crc32(name.encode()), seed]).standard_normal(out[name].shape)
        drawn = base * np.exp(spread * noise) if base else spread * noise
        out[name] = __import__('jax').numpy.asarray(drawn.astype(out[name].dtype))
    for name, factor in factors.items():
        out[name] = (out[name] * factor).astype(out[name].dtype)
    return out
```

```python
import numpy as np
import concourse.bass as bass
from concourse import mybir
from contextlib import ExitStack

F32 = mybir.dt.float32
I32 = mybir.dt.int32
ALU = mybir.AluOpType
ACT = mybir.ActivationFunctionType
AX = mybir.AxisListType.X

P = 128
DEPTH, SEQ, D = 2, 512, 1024
NT = SEQ // P
KD = D // P
MEM = 256
RC = 4
RH, RN = 8, 64
HEADS = 4
QK, NOPE, HALF = 96, 64, 16
NG, NE, EPG = 4, 32, 8
DE = 512
HM = DE // P
CAP = 64
EPS, GN_EPS = 1e-6, 64e-5
HALF_DECAY = 0.5 * float(np.exp(-0.5))
BIG = 1e30
PI = float(np.pi)

UNIT_COLS = [(0, 512), (512, 512), (1024, 512), (1536, 480), (2016, 416), (2432, 256)]
TILE = [(P * j, P, j // 4, True) for j in range(15)] + [(1920, 96, 3, False), (2016, P, 4, False),
                                                        (2176, P, 4, False), (2304, P, 4, False)]
TILE_ORDER = [12, 13, 14, 15, 4, 5, 6, 7, 0, 1, 2, 3, 8, 9, 10, 11, 16, 17, 18]
KR_COL, GV_COL = 2144, 2432

COLS = {}
_at = 0
for _name, _n in [("g_mix", 8), ("g_mem", 8), ("g_ffn", 8), ("mu", 15), ("w0", 4), ("a0", 4), ("k_k", 4),
                  ("k_a", 4), ("r_k", 4), ("ln_g", 4), ("ln_b", 4), ("cq_g", 2), ("ckv_g", 1), ("q_g", 1),
                  ("k_g", 1), ("gv_g", 2), ("xq_g", 1)]:
    COLS[_name] = _at
    _at += _n
NCOL = _at


class Chain:

    def __init__(self, sem):
        self.sem, self.n = sem, 0

    def on(self, eng):
        def step(ins):
            self.n += 1
            ins.then_inc(self.sem, 1)
            eng.wait_ge(self.sem, self.n)
        return step


def build(nc, xT_d, memT_d, pos_d, inv_d, colp_d, memcol_d, w_in_d, lora_d, gup_d, gup2_d, wuq_d, wukv_d, wsT_d,
          gb_d, w_out_d, wkv_d, wmq_d, wmo_d, wr_d, br_d, w1_d, w3_d, w2_d, out_d):
    ctx = ExitStack()
    with ctx:
        ys_d = nc.dram_tensor("expert_rows", (NE * CAP, D), F32, kind="Internal").ap()

        def sb(name, shape, dt=F32):
            return ctx.enter_context(nc.sbuf_tensor(name, shape, dt))

        stage = []
        held = [ExitStack()]

        def sem(name):
            stage.append(held[0].enter_context(nc.semaphore(name)))
            return stage[-1]

        def clear(some):
            nums = sorted(x.num for x in some)
            first = nums[0]
            for a, b in zip(nums, nums[1:] + [None]):
                if b != a + 1:
                    nc.sync.sem_clear(range(first, a + 1))
                    first = b

        def end_stage():
            clear(stage)
            nc.all_engine_barrier()
            held[0].close()
            stage.clear()
            held[0] = ExitStack()

        s_ygs = [ctx.enter_context(nc.semaphore(f"rows_gathered{i}")) for i in range(NT)]
        layer_sems = []

        def layer_sem(name):
            layer_sems.append(ctx.enter_context(nc.semaphore(name)))
            return layer_sems[-1]

        B = [ctx.enter_context(nc.psum_tensor(f"bank{i}", [P, 512], F32)) for i in range(8)]

        xT = sb("xT", [P, KD, SEQ])
        hT = sb("hT", [P, KD, SEQ])
        ring = sb("ring", [P, 6, 4096])
        arena = sb("arena", [P, 10880])
        ident = sb("ident", [P, P])
        ones_mean = sb("ones_mean", [P, P])
        ones = sb("ones", [P, P])
        head_sum = sb("head_sum", [P, P])
        head_mean = sb("head_mean", [P, P])
        before = sb("before", [P, P])
        mask4 = sb("mask4", [P, 4, P])
        causal = sb("causal", [P, P])
        pair1 = sb("pair1", [P, P])
        lvl = sb("lvl", [P, 6, 64])
        scan_keep = sb("scan_keep", [P, SEQ])
        slot_iota = sb("slot_iota", [P, SEQ])
        slot0 = sb("slot0", [P, NE])
        epsc = sb("epsc", [P, 3])
        colp = sb("colp", [P, NCOL])
        half0 = sb("half0", [P, 12])
        lora_w = sb("lora_w", [P, 512])
        gup_w = sb("gup_w", [P, 512])
        gup2_w = sb("gup2_w", [32, 512])
        wuq = sb("wuq", [P, 2, HEADS * QK])
        wukv = sb("wukv", [P, 512])
        wr = sb("wr", [P, KD, NG + NE])
        brb = sb("brb", [P, NG + NE])
        memKT = sb("memKT", [P, 2, MEM])
        memV = sb("memV", [P, 2, MEM])
        cosT = sb("cosT", [P, NT, HALF])
        sinT = sb("sinT", [P, NT, HALF])
        shp = sb("shift_in", [P, 2, SEQ + 1])
        ST = sb("ST", [P, RC, RN])
        small = sb("small", [P, 640])
        smalli = sb("smalli", [P, 64], I32)

        rT = arena[:, 0:2048].rearrange("p (c t) -> p c t", c=RC)
        kT = arena[:, 2048:4096].rearrange("p (c t) -> p c t", c=RC)
        vT = arena[:, 4096:6144].rearrange("p (c t) -> p c t", c=RC)
        lora = arena[:, 6144:6656]
        gd = arena[:, 6656:7168]
        t14 = arena[:, 7168:7680]
        cq2 = arena[:, 7680:8192]
        ckv = arena[:, 8192:8704]
        uT = arena[:, 8704:9728].rearrange("p (c t) -> p c t", c=2)
        gv = arena[:, 9728:10752].rearrange("p (i n) -> p i n", i=NT)
        kr = arena[:, 10752:10880].rearrange("p (i n) -> p i n", i=NT)

        def ring_view(unit, first, n):
            return ring[:, unit, first:first + n]

        def fours(ap):
            return ap.rearrange("p (c t) -> p c t", c=RC)

        def col(name, i=0):
            return colp[:, COLS[name] + i:COLS[name] + i + 1]

        s_in = sem("inputs_loaded")
        s_gc = sem("pool_const")
        s_vc = sem("dve_order")
        s_ac = sem("act_order")
        s_gp = sem("pool_order")
        s_done = sem("setup_done")
        s_msq = sem("mem_squares")
        s_mms = sem("mem_mean")
        s_mrt = sem("mem_root")
        s_mh = sem("mem_normed")
        s_mkv = sem("mem_kv")
        s_mev = sem("mem_kv_copied")
        s_mk2 = sem("mem_k_mean")
        vch, ach, gch = Chain(s_vc), Chain(s_ac), Chain(s_gp)
        memx = ring[:, 1, 0:2048].rearrange("p (k t) -> p k t", k=KD)
        memh = ring[:, 1, 2048:4096].rearrange("p (k t) -> p k t", k=KD)
        wkv = ring[:, 2, :].rearrange("p (k n) -> p k n", k=KD)
        memcol = small[:, 600:609]

        with nc.Block() as block:
            @block.sync
            def _(eng):
                eng.dma_start(xT[:, :, :], xT_d).then_inc(s_in, 16)
                eng.dma_start(memx, memT_d).then_inc(s_in, 16)
                eng.dma_start(memcol, memcol_d).then_inc(s_in, 16)
                eng.dma_start(wkv, wkv_d.rearrange("(k p) n -> p k n", p=P)).then_inc(s_in, 16)
                eng.dma_start(smalli[:, 0:NT], pos_d).then_inc(s_in, 16)
                eng.dma_start(small[:, 0:HALF], inv_d).then_inc(s_in, 16)
                eng.wait_ge(s_in, 16 * 6)

            @block.gpsimd
            def _(eng):
                g = gch.on(eng)

                def fill(t, v):
                    g(eng.memset(t, v))

                def keep(t, pattern, base, cm, op, other):
                    g(eng.affine_select(out=t, in_=t, compare_op=op, fill=other, base=base, pattern=pattern,
                                        channel_multiplier=cm))
                fill(ident[:, :], 0.0)
                keep(ident[:, :], [[-1, P]], 0, 1, ALU.not_equal, 1.0)
                fill(ones[:, :], 1.0)
                fill(ones_mean[:, :], 1.0 / D)
                for t, v in ((head_sum, 1.0), (head_mean, 1.0 / RN)):
                    fill(t[:, :], 0.0)
                    fill(t[0:64, 0:64], v)
                    fill(t[64:128, 64:128], v)
                fill(before[:, :], 1.0)
                keep(before[:, :], [[1, P]], 0, -1, ALU.is_gt, 0.0)
                fill(mask4[:, :, :], 1.0)
                keep(mask4[:, 0, :], [[-1, P]], 0, 1, ALU.is_gt, 0.0)
                keep(mask4[:, 1, :], [[1, P]], 0, -1, ALU.is_gt, 0.0)
                keep(mask4[:, 2, :], [[1, P]], 0, -1, ALU.is_ge, 0.0)
                keep(mask4[:, 3, :], [[1, P]], 0, -1, ALU.is_ge, 0.0)
                fill(causal[:, :], 0.0)
                keep(causal[:, :], [[-1, P]], 0, 1, ALU.is_ge, -BIG)
                fill(pair1[:, :], 0.0)
                v = pair1[:, :].rearrange("p (a b) -> p a b", b=2)[:, :, 0]
                keep(v, [[-2, 64]], -1, 1, ALU.not_equal, 1.0)
                fill(lvl[:, :, :], 1.0)
                for L in range(6):
                    b = 2 << L
                    v = lvl[:, L, :].rearrange("p (a j) -> p a j", j=b)
                    keep(v, [[-2 * b, 64 // b], [0, b]], 0, 1, ALU.is_ge, 0.0)
                    keep(v, [[2 * b, 64 // b], [0, b]], b, -1, ALU.is_gt, 0.0)
                fill(scan_keep[:, :], 1.0)
                for n in range(NT):
                    fill(scan_keep[:, n * P:n * P + 1], 0.0)
                g(eng.iota(slot_iota[:, :], pattern=[[1, SEQ]], base=0, channel_multiplier=0,
                           allow_small_or_imprecise_dtypes=True))
                g(eng.iota(slot0[:, :], pattern=[[CAP, NE]], base=0, channel_multiplier=0,
                           allow_small_or_imprecise_dtypes=True))
                fill(epsc[:, 0:1], EPS)
                fill(epsc[:, 1:2], GN_EPS)
                fill(epsc[:, 2:3], 0.0)
                eng.sem_inc(s_gc, 1)

            @block.vector
            def _(eng):
                v = vch.on(eng)
                eng.wait_ge(s_in, 16 * 6)
                pf = small[:, 16:20]
                v(eng.tensor_copy(pf, smalli[:, 0:NT]))
                ang, kq, ang2 = small[:, 32:96], small[:, 96:160], small[:, 160:224]
                v(eng.tensor_tensor(ang.rearrange("p (i j) -> p i j", i=NT),
                                    pf.unsqueeze(2).to_broadcast([P, NT, HALF]),
                                    small[:, 0:HALF].unsqueeze(1).to_broadcast([P, NT, HALF]), ALU.mult))
                v(eng.tensor_scalar(kq, ang, float(1 / (2 * np.pi)), 12582912.0, ALU.mult, ALU.add))
                v(eng.tensor_scalar(kq, kq, -12582912.0, None, ALU.add))
                c1 = 6.28125
                c2 = float(np.float32(np.float64(2 * np.pi) - c1).view(np.uint32) & 0xFFFFF000)
                c2 = float(np.array([int(c2)], np.uint32).view(np.float32)[0])
                c3 = float(np.float64(2 * np.pi) - c1 - c2)
                for c in (c1, c2, c3):
                    v(eng.scalar_tensor_tensor(out=ang, in0=kq, scalar=-c, in1=ang, op0=ALU.mult, op1=ALU.add))
                v(eng.tensor_scalar(ang2, ang, PI / 2, None, ALU.add))
                v(eng.tensor_scalar(kq, ang2, PI, -2 * PI, ALU.is_gt, ALU.mult))
                v(eng.tensor_tensor(ang2, ang2, kq, ALU.add))
                for a in (ang, ang2):
                    v(eng.tensor_scalar(a, a, -PI, PI, ALU.max, ALU.min))
                eng.sem_inc(s_done, 1)
                eng.wait_ge(s_mrt, 1)
                rs = small[:, 256:512]
                v(eng.reciprocal(rs, rs))
                for k in range(KD):
                    eng.scalar_tensor_tensor(out=memh[:, k, :], in0=memx[:, k, :], scalar=memcol[:, k:k + 1],
                                             in1=rs, op0=ALU.mult, op1=ALU.mult).then_inc(s_mh, 1)
                eng.wait_ge(s_mrt, 2)
                krs = ring_view(3, 1024, 512).rearrange("p (c t) -> p c t", c=2)
                v(eng.reciprocal(krs, krs))
                for c in range(2):
                    eng.scalar_tensor_tensor(out=memKT[:, c, :], in0=B[c][:, 0:MEM], scalar=memcol[:, 8:9],
                                             in1=krs[:, c, :], op0=ALU.mult, op1=ALU.mult).then_inc(s_mev, 1)

            @block.scalar
            def _(eng):
                a = ach.on(eng)
                eng.wait_ge(s_in, 16 * 6)
                eng.wait_ge(s_gc, 1)
                msq = ring_view(3, 0, 512).rearrange("p (c t) -> p c t", c=2)
                for k in range(KD):
                    if k >= 2:
                        eng.wait_ge(s_mms, k - 1)
                    eng.activation(msq[:, k % 2, :], memx[:, k, :], ACT.Square).then_inc(s_msq, 1)
                eng.wait_ge(s_mms, KD)
                eng.activation(small[:, 256:512], B[0][:, 0:MEM], ACT.Sqrt, bias=epsc[:, 0:1]).then_inc(s_mrt, 1)
                ksq = ring_view(3, 512, 512).rearrange("p (c t) -> p c t", c=2)
                for c in range(2):
                    eng.wait_ge(s_mkv, c + 1)
                    eng.activation(ksq[:, c, :], B[c][:, 0:MEM], ACT.Square).then_inc(s_msq, 1)
                for i in range(2):
                    eng.wait_ge(s_mkv, 3 + i)
                    eng.activation(memV[:, i, :], B[2 + i][:, 0:MEM], ACT.Copy).then_inc(s_mev, 1)
                krs = ring_view(3, 1024, 512).rearrange("p (c t) -> p c t", c=2)
                eng.wait_ge(s_mk2, 2)
                eng.activation(krs[:, 0, :], B[4][:, 0:MEM], ACT.Sqrt, bias=epsc[:, 0:1])
                eng.activation(krs[:, 1, :], B[5][:, 0:MEM], ACT.Sqrt, bias=epsc[:, 0:1]).then_inc(s_mrt, 1)
                eng.wait_ge(s_done, 1)
                a(eng.activation(sinT[:, :, :], small[:, 32:96].rearrange("p (i j) -> p i j", i=NT), ACT.Sin))
                a(eng.activation(cosT[:, :, :], small[:, 160:224].rearrange("p (i j) -> p i j", i=NT), ACT.Sin))

            @block.tensor
            def _(eng):
                eng.wait_ge(s_gc, 1)
                msq = ring_view(3, 0, 512).rearrange("p (c t) -> p c t", c=2)
                for k in range(KD):
                    eng.wait_ge(s_msq, k + 1)
                    nc.tensor.matmul(B[0][:, 0:MEM], ones_mean[:, :], msq[:, k % 2, :], start=k == 0,
                                     stop=k == KD - 1).then_inc(s_mms, 1)
                eng.wait_ge(s_mh, KD)
                for c in range(2):
                    for k in range(KD):
                        last = nc.tensor.matmul(B[c][:, 0:MEM], wkv[:, k, c * P:(c + 1) * P], memh[:, k, :],
                                                start=k == 0, stop=k == KD - 1)
                    last.then_inc(s_mkv, 1)
                for i in range(2):
                    for k in range(KD):
                        last = nc.tensor.matmul(B[2 + i][:, 0:MEM], memh[:, k, i * P:(i + 1) * P],
                                                wkv[:, k, MEM:2 * MEM], start=k == 0, stop=k == KD - 1)
                    last.then_inc(s_mkv, 1)
                ksq = ring_view(3, 512, 512).rearrange("p (c t) -> p c t", c=2)
                eng.wait_ge(s_msq, KD + 2)
                for c in range(2):
                    nc.tensor.matmul(B[4 + c][:, 0:MEM], head_mean[:, :], ksq[:, c, :], start=True,
                                     stop=True).then_inc(s_mk2, 1)

        end_stage()
        s_vc, s_ac, s_gp = layer_sem("dve_order_l"), layer_sem("act_order_l"), layer_sem("pool_order_l")
        vch, ach, gch = Chain(s_vc), Chain(s_ac), Chain(s_gp)
        s_par = layer_sem("params_loaded")
        s_sq, s_sqd = layer_sem("squares"), layer_sem("squares_summed")
        s_rt, s_h = layer_sem("norm_root"), layer_sem("h_ready")
        s_wo = [layer_sem(f"w_out_loaded{z}") for z in range(2)]
        s_wm = layer_sem("w_mem_loaded")
        s_e = [layer_sem(f"expert_weights{u}") for u in range(6)]

        with nc.Fori(0, DEPTH) as layer:
            lay = bass.ds(layer, 1)

            def norm_act(eng, n0, bank, sqb, rs):
                for k in range(KD):
                    if n0 or k >= 2:
                        eng.wait_ge(s_sqd, n0 * KD + k - 1)
                    eng.activation(sqb[:, k % 2, :], xT[:, k, :], ACT.Square).then_inc(s_sq, 1)
                eng.wait_ge(s_sqd, (n0 + 1) * KD)
                eng.activation(rs, bank[:, :], ACT.Sqrt, bias=epsc[:, 0:1]).then_inc(s_rt, 1)

            def norm_pe(eng, n0, bank, sqb):
                for k in range(KD):
                    eng.wait_ge(s_sq, n0 * KD + k + 1)
                    nc.tensor.matmul(bank[:, :], ones_mean[:, :], sqb[:, k % 2, :], start=k == 0,
                                     stop=k == KD - 1).then_inc(s_sqd, 1)

            def norm_dve(eng, v, n0, gain, rs):
                eng.wait_ge(s_rt, n0 + 1)
                v(eng.reciprocal(rs, rs))
                for k in range(KD):
                    eng.scalar_tensor_tensor(out=hT[:, k, :], in0=xT[:, k, :], scalar=col(gain, k), in1=rs,
                                             op0=ALU.mult, op1=ALU.mult).then_inc(s_h, 1)

            s_win = [sem(f"w_in_loaded{c}") for c in range(6)]
            s_col = sem("columns_loaded")
            s_pj, s_pad, s_sh = sem("proj_done"), sem("proj_copied"), sem("proj_shifted")
            nrm_sq = arena[:, 8704:9728].rearrange("p (a t) -> p a t", a=2)
            nrm_rs = arena[:, 9728:10240]
            shd = nrm_rs
            ins_units = [ring[:, c, 0:KD * w].rearrange("p (k n) -> p k n", k=KD) for c, (_, w) in
                         enumerate(UNIT_COLS)]
            dest = {12: lora, 13: gd, 14: t14, 15: cq2, 16: ckv, 17: uT[:, 0, :], 18: uT[:, 1, :]}
            for c in range(RC):
                dest[c], dest[4 + c], dest[8 + c] = rT[:, c, :], kT[:, c, :], vT[:, c, :]
            NPAR = 7

            with nc.Block() as block:
                @block.sync
                def _(eng):
                    eng.dma_start(colp[:, :], colp_d[lay].rearrange("a p n -> p (a n)")).then_inc(s_col, 16)
                    for c in (3, 1, 0, 2, 4, 5):
                        c0, w = UNIT_COLS[c]
                        eng.dma_start(ins_units[c], w_in_d[lay, :, c0:c0 + w].rearrange("a (k p) n -> p (a k) n", p=P)
                                      ).then_inc(s_win[c], 16)
                    eng.dma_start(lora_w[:, :], lora_d[lay].rearrange("a p n -> p (a n)")).then_inc(s_par, 16)
                    eng.dma_start(gup_w[:, :], gup_d[lay].rearrange("a p n -> p (a n)")).then_inc(s_par, 16)
                    eng.dma_start(gup2_w[:, :], gup2_d[lay].rearrange("a p n -> p (a n)")).then_inc(s_par, 16)
                    eng.dma_start(wuq[:, :, :], wuq_d[lay].rearrange("a p k n -> p (a k) n")).then_inc(s_par, 16)
                    eng.dma_start(wukv[:, :], wukv_d[lay].rearrange("a p n -> p (a n)")).then_inc(s_par, 16)
                    eng.dma_start(wr[:, :, :], wr_d[lay].rearrange("a p k n -> p (a k) n")).then_inc(s_par, 16)
                    eng.dma_start(brb[:, :], br_d[lay].broadcast_to([P, NG + NE])).then_inc(s_par, 16)
                    eng.wait_ge(s_par, 16 * NPAR)

                @block.gpsimd
                def _(eng):
                    eng.memset(shp[:, :, 0:1], 0.0).then_inc(s_gp, 1)
                    gch.n += 1

                @block.scalar
                def _(eng):
                    norm_act(eng, 0, B[7], nrm_sq, nrm_rs)
                    for n, j in enumerate(TILE_ORDER):
                        c0, w, unit, shifted = TILE[j]
                        eng.wait_ge(s_pj, n + 1)
                        if shifted:
                            m = sum(TILE[x][3] for x in TILE_ORDER[:n])
                            if m >= 2:
                                eng.wait_ge(s_sh, m - 1)
                            eng.activation(shp[:, m % 2, 1:SEQ + 1], B[n % 4][:, :], ACT.Copy).then_inc(s_pad, 1)
                        else:
                            eng.activation(dest[j][0:w, :], B[n % 4][0:w, :], ACT.Copy).then_inc(s_pad, 1)
                    n0 = len(TILE_ORDER)
                    eng.wait_ge(s_sh, 15)
                    for i in range(NT):
                        eng.wait_ge(s_pj, n0 + i + 1)
                        eng.activation(gv[:, i, :], B[(n0 + i) % 4][:, 0:256], ACT.Copy)
                        eng.activation(kr[:, i, :], B[(n0 + i) % 4][:, 256:288], ACT.Copy).then_inc(s_pad, 1)

                @block.vector
                def _(eng):
                    v = vch.on(eng)
                    eng.wait_ge(s_col, 16)
                    norm_dve(eng, v, 0, "g_mix", nrm_rs)
                    eng.wait_ge(s_gp, 1)
                    m = 0
                    for n, j in enumerate(TILE_ORDER):
                        if not TILE[j][3]:
                            continue
                        eng.wait_ge(s_pad, n + 1)
                        v(eng.tensor_tensor(shd[:, :], shp[:, m % 2, 0:SEQ], shp[:, m % 2, 1:SEQ + 1],
                                            ALU.subtract))
                        eng.scalar_tensor_tensor(out=dest[j], in0=shd[:, :], scalar=col("mu", j),
                                                 in1=shp[:, m % 2, 1:SEQ + 1], op0=ALU.mult,
                                                 op1=ALU.add).then_inc(s_sh, 1)
                        m += 1
                        eng.wait_ge(s_sh, m)

                @block.tensor
                def _(eng):
                    norm_pe(eng, 0, B[7], nrm_sq)
                    for n, j in enumerate(TILE_ORDER):
                        c0, w, unit, _s = TILE[j]
                        u0 = c0 - UNIT_COLS[unit][0]
                        eng.wait_ge(s_win[unit], 16)
                        if n == 0:
                            eng.wait_ge(s_h, KD)
                        if n >= 4:
                            eng.wait_ge(s_pad, n - 3)
                        for k in range(KD):
                            last = nc.tensor.matmul(B[n % 4][0:w, :], ins_units[unit][:, k, u0:u0 + w], hT[:, k, :],
                                                    start=k == 0, stop=k == KD - 1)
                        last.then_inc(s_pj, 1)
                    n0 = len(TILE_ORDER)
                    eng.wait_ge(s_win[5], 16)
                    for i in range(NT):
                        n = n0 + i
                        eng.wait_ge(s_pad, n - 3)
                        for o, w, unit, u0 in ((256, 32, 4, KR_COL - UNIT_COLS[4][0]), (0, 256, 5, 0)):
                            for k in range(KD):
                                last = nc.tensor.matmul(B[n % 4][:, o:o + w], hT[:, k, i * P:(i + 1) * P],
                                                        ins_units[unit][:, k, u0:u0 + w], start=k == 0,
                                                        stop=k == KD - 1)
                        last.then_inc(s_pj, 1)

            X1, X2, X3, X4, X5, X6 = [fours(ring_view(i // 2, 2048 * (i % 2), 2048)) for i in range(6)]
            AT = fours(hT[:, 4:8, :].rearrange("p c t -> p (c t)"))
            BT = fours(ring_view(5, 0, 2048))
            bonus = fours(hT[:, 0:4, :].rearrange("p c t -> p (c t)"))
            mid = small[:, 0:16].rearrange("p (c n) -> p c n", c=RC)
            lastr = small[:, 16:32].rearrange("p (c n) -> p c n", c=RC)
            fexp = small[:, 32:44].rearrange("p (c n) -> p c n", c=RC)
            sg2 = small[0:32, 64:576]
            s_b1, s_b2, s_b3 = sem("kk_squared"), sem("kk_summed"), sem("kk_floored")
            s_b4, s_b5 = sem("kk_root"), sem("lora_tanh")
            s_wp, s_ap, s_th, s_ta = sem("decay_lora"), sem("a_lora"), sem("decay_tanh"), sem("a_tanh")
            s_cr, s_ex, s_bp, s_bs, s_el = (sem("cum_ready"), sem("decay_exps"), sem("bonus_product"),
                                            sem("bonus_summed"), sem("elementwise_done"))

            def flat(ap):
                return ap.rearrange("p c t -> p (c t)")

            def chunks(ap):
                return ap.rearrange("p c (n t) -> p (c n) t", t=P)

            with nc.Block() as block:
                @block.scalar
                def _(eng):
                    a = ach.on(eng)
                    eng.activation(half0[:, 0:8], colp[:, COLS["w0"]:COLS["w0"] + 8], ACT.Copy, scale=0.5)
                    eng.activation(gd, gd, ACT.Tanh, scale=0.5)
                    eng.activation(sg2, t14[0:32, :], ACT.Tanh, scale=0.5)
                    a(eng.activation(lora[0:64, :], lora[0:64, :], ACT.Tanh))
                    eng.sem_inc(s_b5, 1)
                    eng.wait_ge(s_b1, 4)
                    a(eng.activation(flat(X2), flat(X1), ACT.Square))
                    eng.sem_inc(s_b2, 1)
                    for c in range(RC):
                        eng.wait_ge(s_wp, c + 1)
                        eng.activation(X3[:, c, :], B[4 + c][:, :], ACT.Tanh, scale=0.5,
                                       bias=half0[:, c:c + 1]).then_inc(s_th, 1)
                    for c in range(RC):
                        eng.wait_ge(s_ap, c + 1)
                        eng.activation(X4[:, c, :], B[c][:, :], ACT.Tanh, scale=0.5,
                                       bias=half0[:, 4 + c:5 + c]).then_inc(s_ta, 1)
                    eng.wait_ge(s_b3, 4)
                    eng.activation(flat(X2), flat(X2), ACT.Sqrt).then_inc(s_b4, 1)
                    eng.wait_ge(s_cr, 1)
                    eng.activation(flat(X6), flat(X6), ACT.Exp).then_inc(s_ex, 1)
                    eng.activation(flat(X3), flat(X5), ACT.Exp).then_inc(s_ex, 1)
                    eng.activation(fexp, fexp, ACT.Exp).then_inc(s_ex, 1)
                    eng.wait_ge(s_cr, 2)
                    eng.activation(flat(X2), flat(X5), ACT.Exp, scale=-1.0).then_inc(s_ex, 1)

                @block.vector
                def _(eng):
                    v = vch.on(eng)
                    for c in range(RC):
                        eng.tensor_scalar(X1[:, c, :], kT[:, c, :], col("k_k", c), None, ALU.mult).then_inc(s_b1, 1)
                    v(eng.tensor_scalar(half0[:, 8:12], colp[:, COLS["k_a"]:COLS["k_a"] + 4], -1.0, 1.0,
                                        ALU.mult, ALU.add))
                    for c in range(RC):
                        eng.wait_ge(s_bs, c + 1)
                        eng.tensor_scalar(X2[:, c, :], B[c][:, :], 1e-24, None, ALU.max).then_inc(s_b3, 1)
                    eng.wait_ge(s_th, 4)
                    v(eng.tensor_scalar(flat(X3), flat(X3), -HALF_DECAY, -HALF_DECAY, ALU.mult, ALU.add))
                    for c in range(RC):
                        last = eng.tensor_tensor_scan(X5[:, c, :], scan_keep[:, :], X3[:, c, :], 0.0,
                                                      ALU.mult, ALU.add)
                    v(last)
                    cum = X5.rearrange("p c (n t) -> p c n t", t=P)
                    v(eng.tensor_copy(mid, cum[:, :, :, P // 2 - 1]))
                    v(eng.tensor_tensor(chunks(X5), chunks(X5),
                                        small[:, 0:16].unsqueeze(2).to_broadcast([P, 16, P]), ALU.subtract))
                    v(eng.tensor_copy(lastr, cum[:, :, :, P - 1]))
                    v(eng.tensor_tensor(fexp, lastr[:, :, 0:3], mid[:, :, 1:4], ALU.add))
                    eng.tensor_tensor(flat(X6), flat(X5), flat(X3), ALU.subtract).then_inc(s_cr, 1)
                    eng.wait_ge(s_ta, 4)
                    v(eng.tensor_scalar(flat(X4), flat(X4), 0.5, 0.5, ALU.mult, ALU.add))
                    v(eng.tensor_scalar(gd, gd, 0.5, 0.5, ALU.mult, ALU.add))
                    v(eng.tensor_scalar(sg2, sg2, 0.5, 0.5, ALU.mult, ALU.add))
                    eng.wait_ge(s_b4, 1)
                    v(eng.reciprocal(flat(X2), flat(X2)))
                    eng.tensor_tensor(flat(X1), flat(X1), flat(X2), ALU.mult).then_inc(s_cr, 1)
                    eng.wait_ge(s_cr, 2)
                    eng.wait_ge(s_ex, 1)
                    v(eng.scalar_tensor_tensor(out=flat(AT), in0=flat(X1), scalar=-1.0, in1=flat(X6),
                                               op0=ALU.mult, op1=ALU.mult))
                    v(eng.tensor_tensor(flat(X1), flat(X1), flat(X4), ALU.mult))
                    for c in range(RC):
                        last = eng.tensor_scalar(X6[:, c, :], X4[:, c, :], col("k_a", c), half0[:, 8 + c:9 + c],
                                                 ALU.mult, ALU.add)
                    v(last)
                    v(eng.tensor_tensor(flat(kT), flat(kT), flat(X6), ALU.mult))
                    for c in range(RC):
                        eng.scalar_tensor_tensor(out=X4[:, c, :], in0=rT[:, c, :], scalar=col("r_k", c),
                                                 in1=kT[:, c, :], op0=ALU.mult, op1=ALU.mult).then_inc(s_bp, 1)
                    eng.wait_ge(s_ex, 4)
                    eng.wait_ge(s_bp, 4)
                    v(eng.tensor_tensor(flat(BT), flat(X1), flat(X2), ALU.mult))
                    v(eng.tensor_tensor(flat(kT), flat(kT), flat(X2), ALU.mult))
                    v(eng.tensor_tensor(flat(rT), flat(rT), flat(X3), ALU.mult))
                    for c in range(RC):
                        eng.wait_ge(s_bs, 5 + c)
                        v(eng.tensor_tensor(bonus[:, c, :], B[4 + c][:, :], vT[:, c, :], ALU.mult))

                @block.tensor
                def _(eng):
                    eng.wait_ge(s_b2, 1)
                    for c in range(RC):
                        nc.tensor.matmul(B[c][:, :], head_sum[:, :], X2[:, c, :], start=True,
                                         stop=True).then_inc(s_bs, 1)
                    eng.wait_ge(s_b5, 1)
                    for c in range(RC):
                        nc.tensor.matmul(B[4 + c][:, :], lora_w[0:64, c * P:(c + 1) * P], lora[0:64, :], start=True,
                                         stop=True).then_inc(s_wp, 1)
                    for c in range(RC):
                        eng.wait_ge(s_b3, c + 1)
                        nc.tensor.matmul(B[c][:, :], lora_w[64:128, c * P:(c + 1) * P], lora[64:128, :], start=True,
                                         stop=True).then_inc(s_ap, 1)
                    for c in range(RC):
                        eng.wait_ge(s_bp, c + 1)
                        eng.wait_ge(s_th, c + 1)
                        nc.tensor.matmul(B[4 + c][:, :], head_sum[:, :], X4[:, c, :], start=True,
                                         stop=True).then_inc(s_bs, 1)

            big = [ring[:, n, :].rearrange("p (h m t) -> p h m t", h=RH, m=4) for n in range(2)]
            XL = [ring_view(2, 1024 * n, 1024).rearrange("p (h t) -> p h t", h=RH) for n in range(2)]
            XU = [ring_view(2, 2048 + 1024 * n, 1024).rearrange("p (h t) -> p h t", h=RH) for n in range(2)]
            Vt, Bt, Kt = [[ring_view(3, 512 * (3 * n + q), 512) for n in range(2)] for q in range(3)]
            T1 = [ring_view(3, 3072 + 512 * n, 512).rearrange("p (h t) -> p h t", h=RH) for n in range(2)]
            Wm = ring_view(4, 0, 512).rearrange("p (h t) -> p h t", h=RH)
            Um = ring_view(4, 512, 512).rearrange("p (h t) -> p h t", h=RH)
            Stmp = ring_view(4, 1024, 256).rearrange("p (c t) -> p c t", c=RC)
            s_tr, s_tc = sem("chunk_transposed"), sem("chunk_copied")
            s_g4, s_gm = sem("products_done"), sem("products_masked")
            s_x0, s_xt, s_xc = sem("inverse_start"), sem("inverse_flipped"), sem("inverse_flip_copied")
            s_t1, s_tm, s_u1, s_xa = sem("level_a"), sem("level_a_masked"), sem("level_b"), sem("level_added")
            s_w, s_wc, s_u, s_uc = sem("w_done"), sem("w_copied"), sem("u_done"), sem("u_copied")
            s_y, s_yc, s_st, s_stc = sem("y_done"), sem("y_copied"), sem("state_done"), sem("state_kept")

            def odd(ap, L):
                b = 2 << L
                return ap.rearrange("p (a two j) -> p a two j", two=2, j=b)[:, :, 1, :]

            def odd8(ap, L):
                b = 2 << L
                return ap.rearrange("p h (a two j) -> p (h a) two j", two=2, j=b)[:, :, 1, :]

            def split(ap, L):
                return ap.rearrange("p (a j) -> p a j", j=2 << L)

            def split8(ap, L):
                return ap.rearrange("p h (a j) -> p (h a) j", j=2 << L)

            with nc.Block() as block:
                @block.tensor
                def _(eng):
                    tcp, gcp, t1n, u1n, xtn = 0, 0, 0, 0, 0
                    for n0 in (0, 2):
                        for s in range(2):
                            n = n0 + s
                            tok = slice(n * P, (n + 1) * P)
                            for q, src in enumerate((vT, BT, kT)):
                                i = 3 * n + q
                                if i >= 2:
                                    eng.wait_ge(s_tc, i - 1)
                                if n0 and q == 0 and s == 0:
                                    eng.wait_ge(s_yc, 2)
                                    eng.wait_ge(s_stc, 2)
                                for c in range(RC):
                                    last = nc.tensor.transpose(B[i % 2][:, c * P:(c + 1) * P], src[:, c, tok],
                                                               ident[:, :])
                                last.then_inc(s_tr, 1)
                            for h in range(RH):
                                g = RH * n + h
                                rows = slice(64 * (h % 2), 64 * (h % 2) + 64)
                                if g >= 4:
                                    eng.wait_ge(s_gm, g - 3)
                                bank = B[2 + g % 4]
                                a_, b_ = AT[rows, h // 2, tok], BT[rows, h // 2, tok]
                                k_, r_ = kT[rows, h // 2, tok], rT[rows, h // 2, tok]
                                for m, (lt, rt) in enumerate(((a_, b_), (k_, a_), (b_, r_), (k_, r_))):
                                    last = nc.tensor.matmul(bank[:, m * P:(m + 1) * P], lt, rt, start=True, stop=True)
                                last.then_inc(s_g4, 1)
                        for s in range(2):
                            n = n0 + s
                            eng.wait_ge(s_x0, n + 1)
                            for h in range(RH):
                                nc.tensor.transpose(B[6 + h // 4][:, (h % 4) * P:(h % 4 + 1) * P], XL[s][:, h, :],
                                                    ident[:, :]).then_inc(s_xt, 1)
                            xtn += 1
                            eng.wait_ge(s_xc, xtn)
                        for L in range(6):
                            for s in range(2):
                                for h in range(RH):
                                    last = nc.tensor.matmul(B[s][:, h * 64:(h + 1) * 64], big[s][:, h, 0, :],
                                                            odd(XU[s][:, h, :], L), start=True, stop=True)
                                last.then_inc(s_t1, 1)
                            for s in range(2):
                                t1n += 1
                                eng.wait_ge(s_tm, t1n)
                                for h in range(RH):
                                    last = nc.tensor.matmul(B[2 + s][:, h * 64:(h + 1) * 64], XL[s][:, h, :],
                                                            T1[s][:, h, :], start=True, stop=True)
                                last.then_inc(s_u1, 1)
                            for s in range(2):
                                u1n += 1
                                eng.wait_ge(s_xa, u1n)
                                if L == 5:
                                    continue
                                for h in range(RH):
                                    nc.tensor.transpose(B[4 + 2 * s + h // 4][:, (h % 4) * P:(h % 4 + 1) * P],
                                                        XU[s][:, h, :], ident[:, :]).then_inc(s_xt, 1)
                                xtn += 1
                            if L < 5:
                                eng.wait_ge(s_xc, xtn)
                        for s in range(2):
                            n = n0 + s
                            tok = slice(n * P, (n + 1) * P)
                            eng.wait_ge(s_tc, 3 * n + 3)
                            if n:
                                eng.wait_ge(s_stc, n)
                            for h in range(RH):
                                rows = slice(64 * (h % 2), 64 * (h % 2) + 64)
                                o = B[4 * (h % 2)][:, (h // 2) * 64:(h // 2 + 1) * 64]
                                if n:
                                    nc.tensor.matmul(o, AT[rows, h // 2, tok], ST[rows, h // 2, :], start=True,
                                                     stop=False)
                                last = nc.tensor.matmul(o, big[s][:, h, 1, :], Vt[s][:, h * 64:(h + 1) * 64],
                                                        start=n == 0, stop=True)
                            last.then_inc(s_w, 1)
                            eng.wait_ge(s_wc, n + 1)
                            for h in range(RH):
                                last = nc.tensor.matmul(B[1][:, h * 64:(h + 1) * 64], XU[s][:, h, :], Wm[:, h, :],
                                                        start=True, stop=True)
                            last.then_inc(s_u, 1)
                            eng.wait_ge(s_uc, n + 1)
                            if n < NT - 1:
                                for h in range(RH):
                                    rows = slice(64 * (h % 2), 64 * (h % 2) + 64)
                                    o = B[2][rows, (h // 2) * 64:(h // 2) * 64 + 64]
                                    hs = slice(h * 64, (h + 1) * 64)
                                    nc.tensor.matmul(o, Bt[s][:, hs], Um[:, h, :], start=True, stop=False)
                                    last = nc.tensor.matmul(o, Kt[s][:, hs], Vt[s][:, hs], start=False, stop=True)
                                last.then_inc(s_st, 1)
                            if n:
                                eng.wait_ge(s_yc, n)
                            for h in range(RH):
                                rows = slice(64 * (h % 2), 64 * (h % 2) + 64)
                                o = B[3][rows, (h // 2) * P:(h // 2 + 1) * P]
                                hs = slice(h * 64, (h + 1) * 64)
                                if n:
                                    nc.tensor.matmul(o, ST[rows, h // 2, :], rT[rows, h // 2, tok], start=True,
                                                     stop=False)
                                nc.tensor.matmul(o, Um[:, h, :], big[s][:, h, 2, :], start=n == 0, stop=False)
                                last = nc.tensor.matmul(o, Vt[s][:, hs], big[s][:, h, 3, :], start=False, stop=True)
                            last.then_inc(s_y, 1)

                @block.scalar
                def _(eng):
                    xtn = 0
                    for n0 in (0, 2):
                        if n0:
                            eng.wait_ge(s_y, n0)
                        for i in range(3 * n0, 3 * n0 + 6):
                            dst = (Vt, Bt, Kt)[i % 3][(i // 3) % 2]
                            eng.wait_ge(s_tr, i + 1)
                            eng.activation(dst, B[i % 2][:, :], ACT.Copy).then_inc(s_tc, 1)
                        for s in range(2):
                            xtn += RH
                            eng.wait_ge(s_xt, xtn)
                            eng.activation(XU[s][:, 0:4, :], B[6][:, :].rearrange("p (h t) -> p h t", h=4), ACT.Copy)
                            eng.activation(XU[s][:, 4:8, :], B[7][:, :].rearrange("p (h t) -> p h t", h=4),
                                           ACT.Copy).then_inc(s_xc, 1)
                        for L in range(5):
                            for s in range(2):
                                xtn += RH
                                eng.wait_ge(s_xt, xtn)
                                for half in range(2):
                                    last = eng.activation(
                                        XL[s][:, 4 * half:4 * half + 4, :],
                                        B[4 + 2 * s + half][:, :].rearrange("p (h t) -> p h t", h=4), ACT.Copy)
                                last.then_inc(s_xc, 1)
                        for s in range(2):
                            n = n0 + s
                            eng.wait_ge(s_w, n + 1)
                            for odd_ in range(2):
                                last = eng.activation(Wm.rearrange("p (c two) t -> p c two t", two=2)[:, :, odd_, :],
                                                      B[4 * odd_][:, 0:256].rearrange("p (c t) -> p c t", c=RC),
                                                      ACT.Copy)
                            last.then_inc(s_wc, 1)
                            eng.wait_ge(s_u, n + 1)
                            if n:
                                eng.wait_ge(s_y, n)
                            eng.activation(flat(Um), B[1][:, :], ACT.Copy).then_inc(s_uc, 1)
                            eng.wait_ge(s_y, n + 1)
                            eng.activation(rT[:, :, n * P:(n + 1) * P], fours(B[3][:, :]), ACT.Copy).then_inc(s_yc, 1)

                @block.vector
                def _(eng):
                    v = vch.on(eng)
                    k = 0
                    for n0 in (0, 2):
                        if n0:
                            eng.wait_ge(s_y, n0)
                        for s in range(2):
                            n = n0 + s
                            for h in range(RH):
                                g = RH * n + h
                                eng.wait_ge(s_g4, g + 1)
                                eng.tensor_tensor(big[s][:, h, :, :],
                                                  B[2 + g % 4][:, :].rearrange("p (m t) -> p m t", m=4),
                                                  mask4[:, :, :], ALU.mult).then_inc(s_gm, 1)
                            eng.wait_ge(s_gm, RH * (n + 1))
                            v(eng.tensor_tensor(XL[s], big[s][:, :, 0, :],
                                                pair1[:, :].unsqueeze(1).to_broadcast([P, RH, P]), ALU.mult))
                            eng.tensor_tensor(XL[s], XL[s], ident[:, :].unsqueeze(1).to_broadcast([P, RH, P]),
                                              ALU.add).then_inc(s_x0, 1)
                        for L in range(6):
                            for s in range(2):
                                k += 1
                                eng.wait_ge(s_t1, k)
                                eng.tensor_tensor(T1[s], B[s][:, :].rearrange("p (h t) -> p h t", h=RH),
                                                  lvl[:, L, :].unsqueeze(1).to_broadcast([P, RH, 64]),
                                                  ALU.mult).then_inc(s_tm, 1)
                            for s in range(2):
                                eng.wait_ge(s_u1, k - 1 + s)
                                x = odd8(XU[s], L)
                                eng.tensor_tensor(x, split(B[2 + s][:, :], L), x, ALU.add).then_inc(s_xa, 1)
                        for s in range(2):
                            n = n0 + s
                            if n == NT - 1:
                                continue
                            eng.wait_ge(s_st, n + 1)
                            if n:
                                v(eng.tensor_tensor(Stmp, B[2][:, 0:256].rearrange("p (c t) -> p c t", c=RC),
                                                    ST[:, :, :], ALU.add))
                                eng.wait_ge(s_y, n + 1)
                                eng.tensor_tensor(ST[:, :, :], Stmp, fexp[:, :, n:n + 1].to_broadcast([P, RC, RN]),
                                                  ALU.mult).then_inc(s_stc, 1)
                            else:
                                eng.tensor_tensor(ST[:, :, :], B[2][:, 0:256].rearrange("p (c t) -> p c t", c=RC),
                                                  fexp[:, :, n:n + 1].to_broadcast([P, RC, RN]),
                                                  ALU.mult).then_inc(s_stc, 1)

            s_gn1, s_gn2, s_gn3, s_gn4 = sem("gn_mean"), sem("gn_centred"), sem("gn_squared"), sem("gn_var")
            s_gn5, s_gn6, s_gg = sem("gn_root"), sem("gn_var_read"), sem("gate_done")
            with nc.Block() as block:
                @block.tensor
                def _(eng):
                    for c in range(RC):
                        nc.tensor.matmul(B[c][:, :], head_mean[:, :], rT[:, c, :], start=True,
                                         stop=True).then_inc(s_gn1, 1)
                    for c in range(RC):
                        eng.wait_ge(s_gn3, c + 1)
                        nc.tensor.matmul(B[4 + c][:, :], head_mean[:, :], X1[:, c, :], start=True,
                                         stop=True).then_inc(s_gn4, 1)
                    for c in range(RC):
                        nc.tensor.matmul(B[c][:, :], gup_w[:, c * P:(c + 1) * P], gd, start=True, stop=False)
                        nc.tensor.matmul(B[c][:, :], gup2_w[:, c * P:(c + 1) * P], sg2, start=False,
                                         stop=True).then_inc(s_gg, 1)

                @block.scalar
                def _(eng):
                    for c in range(RC):
                        eng.wait_ge(s_gn2, c + 1)
                        eng.activation(X1[:, c, :], rT[:, c, :], ACT.Square).then_inc(s_gn3, 1)
                    for c in range(RC):
                        eng.wait_ge(s_gn4, c + 1)
                        eng.activation(X2[:, c, :], B[4 + c][:, :], ACT.Sqrt, bias=epsc[:, 1:2]).then_inc(s_gn5, 1)

                @block.vector
                def _(eng):
                    v = vch.on(eng)
                    for c in range(RC):
                        eng.wait_ge(s_gn1, c + 1)
                        eng.tensor_tensor(rT[:, c, :], rT[:, c, :], B[c][:, :], ALU.subtract).then_inc(s_gn2, 1)
                    for c in range(RC):
                        eng.wait_ge(s_gn5, c + 1)
                        v(eng.reciprocal(X2[:, c, :], X2[:, c, :]))
                        v(eng.scalar_tensor_tensor(out=X2[:, c, :], in0=rT[:, c, :], scalar=col("ln_g", c),
                                                   in1=X2[:, c, :], op0=ALU.mult, op1=ALU.mult))
                        v(eng.scalar_tensor_tensor(out=X2[:, c, :], in0=X2[:, c, :], scalar=col("ln_b", c),
                                                   in1=bonus[:, c, :], op0=ALU.add, op1=ALU.add))
                        eng.wait_ge(s_gg, c + 1)
                        v(eng.tensor_tensor(hT[:, c, :], X2[:, c, :], B[c][:, :], ALU.mult))

            end_stage()
            q_sb = ring_view(0, 0, 1536).rearrange("p (i h n) -> p i h n", i=NT, h=HEADS)
            k_sb = ring_view(0, 1536, 1536).rearrange("p (i h n) -> p i h n", i=NT, h=HEADS)
            v_sb = ring_view(0, 3072, 1024).rearrange("p (i n) -> p i n", i=NT)
            qT = ring_view(1, 0, 2048).rearrange("p (h t) -> p h t", h=HEADS)
            kTm = ring_view(1, 2048, 2048).rearrange("p (h t) -> p h t", h=HEADS)
            PT = [ring_view(2, 2048 * z, 2048).rearrange("p (j q) -> p j q", j=NT) for z in range(2)]
            sq14, sq15, sqkv = arena[:, 0:512], arena[:, 512:1024], arena[:, 1024:1536]
            qk_sq = arena[:, 0:1536].rearrange("p (i n) -> p i n", n=QK)
            rope_t = [arena[:, 1536 + 256 * z:1792 + 256 * z].rearrange("p (i h n) -> p i h n", i=NT, h=HEADS)
                      for z in range(4)]
            rope_k = [arena[:, 2560 + 64 * z:2624 + 64 * z].rearrange("p (i n) -> p i n", i=NT) for z in range(4)]
            Pm = [arena[:, 2816 + 512 * z:3328 + 512 * z] for z in range(2)]
            gsq = arena[:, 3840:4864].rearrange("p (i n) -> p i n", n=RN)
            wsm = arena[:, 4864:5376].rearrange("p (g t) -> p g t", g=4)
            gtmp = arena[:, 5376:5888]
            gbb = arena[:, 5888:6144].rearrange("p (c t) -> p c t", c=2)
            lat = small[:, 0:12]
            qk_rs = small[:, 16:48]
            g_rs = small[:, 48:64]
            mx, sm = small[:, 64:80], small[:, 80:96]
            lat_w = small[:, 100:103]
            s_lw = sem("latent_weights")
            s_l0, s_l1, s_l2 = sem("latent_gained"), sem("latent_squares"), sem("latent_means")
            s_l3, s_l4, s_up, s_upc = sem("latent_root"), sem("latent_rs"), sem("mla_up"), sem("mla_up_copied")
            s_r0, s_r1, s_r2, s_r3 = sem("rope_done"), sem("qk_squares"), sem("qk_sums"), sem("qk_root")
            s_qn, s_qt, s_qc = sem("qk_normed"), sem("qk_transposed"), sem("qk_copied")
            s_sc, s_mx, s_ex2, s_pn = sem("scores"), sem("score_max"), sem("probs"), sem("probs_normed")
            s_pt, s_pc, s_pv, s_oc = sem("probs_transposed"), sem("probs_copied"), sem("pv_done"), sem("mla_out")
            s_ge, s_gs, s_gr, s_gq = sem("gelu"), sem("gmlp_sums"), sem("gmlp_root"), sem("gmlp_squares")
            s_gn, s_sp, s_ws = sem("gmlp_normed"), sem("gmlp_mixed"), sem("gmlp_weights")
            s_gw, s_gb = sem("gmlp_w_loaded"), sem("gmlp_b_loaded")
            w_out = ring[:, 3:5, :].rearrange("p u (k n) -> p (u k) n", k=4)
            wmq = ring_view(5, 0, 2048).rearrange("p (k n) -> p k n", k=KD)
            wmo = ring_view(5, 2048, 2048).rearrange("p (k n) -> p k n", k=2)
            SC = float(QK) ** -0.5

            def copy_probs(eng, n):
                h, i = n // NT, n % NT
                eng.wait_ge(s_pt, n + 1)
                if i == 0 and h >= 2:
                    eng.wait_ge(s_pv, h - 1)
                eng.activation(PT[h % 2][:, 0:i + 1, i * P:(i + 1) * P],
                               B[2 + n % 2][:, 0:(i + 1) * P].rearrange("p (j q) -> p j q", q=P),
                               ACT.Copy).then_inc(s_pc, 1)

            def mla_out(eng, h):
                rows = slice(64 * (h % 2), 64 * (h % 2) + 64)
                eng.wait_ge(s_pv, h + 1)
                eng.activation(hT[rows, 4 + h // 2, :], B[4 + h % 2][rows, :], ACT.Copy).then_inc(s_oc, 1)

            def norm_probs(eng, v, n):
                w = (n % NT + 1) * P
                eng.wait_ge(s_ex2, n + 1)
                v(eng.reciprocal(sm[:, n:n + 1], sm[:, n:n + 1]))
                eng.tensor_scalar(Pm[n % 2][:, 0:w], Pm[n % 2][:, 0:w], sm[:, n:n + 1], None,
                                  ALU.mult).then_inc(s_pn, 1)

            def flip_probs(eng, n):
                eng.wait_ge(s_pn, n + 1)
                if n >= 2:
                    eng.wait_ge(s_pc, n - 1)
                for j in range(n % NT + 1):
                    last = nc.tensor.transpose(B[2 + n % 2][:, j * P:(j + 1) * P],
                                               Pm[n % 2][:, j * P:(j + 1) * P], ident[:, :])
                last.then_inc(s_pt, 1)

            def pv(eng, h):
                rows = slice(64 * (h % 2), 64 * (h % 2) + 64)
                eng.wait_ge(s_pc, NT * (h + 1))
                if h >= 2:
                    eng.wait_ge(s_oc, h - 1)
                for j in range(NT):
                    last = nc.tensor.matmul(B[4 + h % 2][rows, j * P:SEQ], v_sb[:, j, h * 64:(h + 1) * 64],
                                            PT[h % 2][:, j, j * P:SEQ], start=j == 0, stop=j == NT - 1)
                last.then_inc(s_pv, 1)

            with nc.Block() as block:
                @block.sync
                def _(eng):
                    eng.dma_start(wsm, wsT_d[lay].rearrange("a p g n -> p (a g) n")).then_inc(s_gw, 16)
                    for half in range(2):
                        for c in range(2):
                            eng.dma_start(gbb[64 * half:64 * half + 64, c, :],
                                          gb_d[lay, 2 * c + half, :].broadcast_to([64, P])).then_inc(s_gb, 16)
                    for z in range(2):
                        eng.dma_start(w_out[:, 4 * z:4 * z + 4, :],
                                      w_out_d[lay, 512 * z:512 * z + 512, :].rearrange("a (k p) n -> p (a k) n", p=P)
                                      ).then_inc(s_wo[z], 16)
                    eng.dma_start(wmq, wmq_d[lay].rearrange("a (k p) n -> p (a k) n", p=P)).then_inc(s_wm, 16)
                    eng.dma_start(wmo, wmo_d[lay].rearrange("a (k p) n -> p (a k) n", p=P)).then_inc(s_wm, 16)

                @block.gpsimd
                def _(eng):
                    g = gch.on(eng)
                    eng.memset(lat_w[:, 0:1], 1.0 / 192)
                    g(eng.memset(lat_w[:, 1:2], 1.0 / 192))
                    eng.memset(lat_w[0:32, 0:1], 0.0)
                    g(eng.memset(lat_w[:, 2:3], 1.0 / P))
                    eng.sem_inc(s_lw, 1)
                    eng.wait_ge(s_gw, 16)
                    eng.tensor_tensor(wsm, wsm, mask4[:, 2:3, :].to_broadcast([P, 4, P]),
                                      ALU.mult).then_inc(s_ws, 1)

                @block.scalar
                def _(eng):
                    a = ach.on(eng)
                    eng.activation(sq14, t14, ACT.Square).then_inc(s_l1, 1)
                    eng.activation(sq15[0:96, :], cq2[0:96, :], ACT.Square).then_inc(s_l1, 1)
                    eng.activation(sqkv, ckv, ACT.Square).then_inc(s_l1, 1)
                    eng.wait_ge(s_l2, 1)
                    eng.activation(lat[:, 0:8], B[0][:, 0:8], ACT.Sqrt, bias=epsc[:, 0:1]).then_inc(s_l3, 1)
                    for i in range(NT):
                        eng.wait_ge(s_up, i + 1)
                        eng.wait_ge(s_l4, 1)
                        eng.activation(q_sb[:, i, :, :], B[1 + i][:, 0:384].rearrange("p (h n) -> p h n", h=HEADS),
                                       ACT.Copy, scale=lat[:, 2 * i:2 * i + 1]).then_inc(s_upc, 1)
                    for i in range(NT):
                        eng.wait_ge(s_up, 4 + i + 1)
                        src = B[(5 + i) % 8][:, :].rearrange("p (h n) -> p h n", h=HEADS)
                        eng.activation(k_sb[:, i, :, 0:NOPE], src[:, :, 0:NOPE], ACT.Copy,
                                       scale=lat[:, 2 * i + 1:2 * i + 2])
                        eng.activation(v_sb[:, i, :].rearrange("p (h n) -> p h n", h=HEADS), src[:, :, NOPE:P],
                                       ACT.Copy, scale=lat[:, 2 * i + 1:2 * i + 2]).then_inc(s_upc, 1)
                    eng.activation(gv[:, :, :], gv[:, :, :], ACT.Gelu_apprx_tanh).then_inc(s_ge, 1)
                    eng.activation(uT[:, :, :], uT[:, :, :], ACT.Gelu_apprx_tanh).then_inc(s_ge, 1)
                    eng.wait_ge(s_ge, 2)
                    eng.activation(gsq, gv.rearrange("p i (g n) -> p (i g) n", n=RN), ACT.Square).then_inc(s_gq, 1)
                    for z, src in enumerate((q_sb, k_sb)):
                        eng.wait_ge(s_r0, z + 1)
                        if z:
                            eng.wait_ge(s_r2, 1)
                        eng.activation(qk_sq, src.rearrange("p i h n -> p (i h) n"), ACT.Square).then_inc(s_r1, 1)
                    eng.wait_ge(s_r2, 2)
                    a(eng.activation(qk_rs, qk_rs, ACT.Sqrt, scale=1.0 / QK, bias=epsc[:, 0:1]))
                    eng.wait_ge(s_gs, 1)
                    a(eng.activation(g_rs, g_rs, ACT.Sqrt, scale=1.0 / RN, bias=epsc[:, 0:1]))
                    eng.sem_inc(s_r3, 1)
                    for z in range(8):
                        eng.wait_ge(s_qt, z + 1)
                        dst = (qT if z < 4 else kTm)[0:QK, z % 4, :]
                        eng.activation(dst, B[z][0:QK, :], ACT.Copy,
                                       scale=col("q_g" if z < 4 else "k_g")[0:QK, :]).then_inc(s_qc, 1)
                    n = 0
                    for h in range(HEADS):
                        for i in range(NT):
                            w = (i + 1) * P
                            eng.wait_ge(s_mx, n + 1)
                            if n >= 2:
                                eng.wait_ge(s_pt, n - 1)
                            eng.activation(Pm[n % 2][:, 0:w], B[n % 2][:, 0:w], ACT.Exp, scale=SC,
                                           bias=mx[:, n:n + 1], accum_out=sm[:, n:n + 1]).then_inc(s_ex2, 1)
                            if n >= 1:
                                copy_probs(eng, n - 1)
                            n += 1
                        if h >= 1:
                            mla_out(eng, h - 1)
                    copy_probs(eng, n - 1)
                    mla_out(eng, HEADS - 1)

                @block.vector
                def _(eng):
                    v = vch.on(eng)
                    for z, (t, c) in enumerate(((t14, 0), (cq2, 1))):
                        n = P if z == 0 else 96
                        eng.wait_ge(s_l1, z + 1)
                        eng.tensor_scalar(t[0:n, :], t[0:n, :], col("cq_g", c)[0:n, :], None,
                                          ALU.mult).then_inc(s_l0, 1)
                    eng.wait_ge(s_l1, 3)
                    eng.tensor_scalar(ckv, ckv, col("ckv_g"), None, ALU.mult).then_inc(s_l0, 1)
                    eng.wait_ge(s_l3, 1)
                    eng.reciprocal(lat[:, 0:8], lat[:, 0:8]).then_inc(s_l4, 1)
                    cos_b = cosT[:, :, :].unsqueeze(2).to_broadcast([P, NT, HEADS, HALF])
                    sin_b = sinT[:, :, :].unsqueeze(2).to_broadcast([P, NT, HEADS, HALF])
                    k1, k2 = kr[:, :, 0:HALF], kr[:, :, HALF:2 * HALF]
                    for t, x, y in ((0, k1, cosT), (1, k2, sinT), (2, k2, cosT), (3, k1, sinT)):
                        last = eng.tensor_tensor(rope_k[t], x, y[:, :, :], ALU.mult)
                    v(last)
                    eng.tensor_tensor(k1, rope_k[0], rope_k[1], ALU.subtract)
                    v(eng.tensor_tensor(k2, rope_k[2], rope_k[3], ALU.add))
                    v(eng.tensor_copy(k_sb[:, :, :, NOPE:QK], kr[:, :, :].unsqueeze(2).to_broadcast(
                        [P, NT, HEADS, 2 * HALF])))
                    eng.wait_ge(s_upc, 4)
                    q1, q2 = q_sb[:, :, :, NOPE:NOPE + HALF], q_sb[:, :, :, NOPE + HALF:QK]
                    for t, x, y in ((0, q1, cos_b), (1, q2, sin_b), (2, q2, cos_b), (3, q1, sin_b)):
                        last = eng.tensor_tensor(rope_t[t], x, y, ALU.mult)
                    v(last)
                    eng.tensor_tensor(q1, rope_t[0], rope_t[1], ALU.subtract)
                    v(eng.tensor_tensor(q2, rope_t[2], rope_t[3], ALU.add))
                    eng.sem_inc(s_r0, 1)
                    eng.wait_ge(s_upc, 8)
                    eng.sem_inc(s_r0, 1)
                    eng.wait_ge(s_gq, 1)
                    v(eng.tensor_reduce(g_rs, gsq, AX, ALU.add))
                    eng.sem_inc(s_gs, 1)
                    for z in range(2):
                        eng.wait_ge(s_r1, z + 1)
                        v(eng.tensor_reduce(qk_rs[:, 16 * z:16 * z + 16], qk_sq, AX, ALU.add))
                        eng.sem_inc(s_r2, 1)
                    eng.wait_ge(s_r3, 1)
                    v(eng.reciprocal(qk_rs, qk_rs))
                    v(eng.reciprocal(g_rs, g_rs))
                    for z, t in enumerate((q_sb, k_sb)):
                        f = t.rearrange("p i h n -> p (i h) n")
                        eng.tensor_tensor(f, f, qk_rs[:, 16 * z:16 * z + 16].unsqueeze(2).to_broadcast(
                            [P, 16, QK]), ALU.mult).then_inc(s_qn, 1)
                    f = gv.rearrange("p i (g n) -> p (i g) n", n=RN)
                    eng.tensor_tensor(f, f, g_rs.unsqueeze(2).to_broadcast([P, 16, RN]), ALU.mult).then_inc(s_gn, 1)
                    n = 0
                    for h in range(HEADS):
                        for i in range(NT):
                            w = (i + 1) * P
                            eng.wait_ge(s_sc, n + 1)
                            d = B[n % 2][:, w - P:w]
                            v(eng.tensor_tensor(d, d, causal[:, :], ALU.add))
                            v(eng.tensor_reduce(mx[:, n:n + 1], B[n % 2][:, 0:w], AX, ALU.max))
                            eng.tensor_scalar(mx[:, n:n + 1], mx[:, n:n + 1], -SC, None, ALU.mult).then_inc(s_mx, 1)
                            if n >= 1:
                                norm_probs(eng, v, n - 1)
                            n += 1
                    norm_probs(eng, v, n - 1)
                    eng.wait_ge(s_gb, 64)
                    for c in range(2):
                        eng.wait_ge(s_sp, c + 1)
                        v(eng.scalar_tensor_tensor(out=gtmp.rearrange("p (n t) -> p n t", t=P),
                                                   in0=B[6 + c][:, :].rearrange("p (n t) -> p n t", t=P),
                                                   scalar=col("gv_g", c),
                                                   in1=gbb[:, c:c + 1, :].to_broadcast([P, NT, P]),
                                                   op0=ALU.mult, op1=ALU.add))
                        v(eng.tensor_tensor(hT[:, 6 + c, :], gtmp, uT[:, c, :], ALU.mult))

                @block.tensor
                def _(eng):
                    eng.wait_ge(s_lw, 1)
                    eng.wait_ge(s_l1, 3)
                    for i in range(NT):
                        t = slice(i * P, (i + 1) * P)
                        nc.tensor.matmul(B[0][:, 2 * i:2 * i + 1], sq14[:, t], lat_w[:, 0:1], start=True, stop=False)
                        nc.tensor.matmul(B[0][:, 2 * i:2 * i + 1], sq15[0:96, t], lat_w[0:96, 1:2], start=False,
                                         stop=True)
                        last = nc.tensor.matmul(B[0][:, 2 * i + 1:2 * i + 2], sqkv[:, t], lat_w[:, 2:3], start=True,
                                                stop=True)
                    last.then_inc(s_l2, 1)
                    eng.wait_ge(s_l0, 3)
                    for i in range(NT):
                        t = slice(i * P, (i + 1) * P)
                        nc.tensor.matmul(B[1 + i][:, 0:384], t14[:, t], wuq[:, 0, :], start=True, stop=False)
                        nc.tensor.matmul(B[1 + i][:, 0:384], cq2[0:96, t], wuq[0:96, 1, :], start=False,
                                         stop=True).then_inc(s_up, 1)
                    eng.wait_ge(s_l3, 1)
                    for i in range(NT):
                        nc.tensor.matmul(B[(5 + i) % 8][:, :], ckv[:, i * P:(i + 1) * P], wukv[:, :], start=True,
                                         stop=True).then_inc(s_up, 1)
                    eng.wait_ge(s_upc, 8)
                    for z in range(8):
                        eng.wait_ge(s_qn, z // 4 + 1)
                        src = (q_sb, k_sb)[z // 4]
                        for i in range(NT):
                            last = nc.tensor.transpose(B[z][0:QK, i * P:(i + 1) * P], src[:, i, z % 4, :], ident[:, :])
                        last.then_inc(s_qt, 1)
                    eng.wait_ge(s_qc, 8)
                    eng.wait_ge(s_gn, 1)
                    eng.wait_ge(s_ws, 1)
                    for c in range(2):
                        for half in range(2):
                            g_ = 2 * c + half
                            for n in range(NT):
                                last = nc.tensor.matmul(B[6 + c][64 * half:64 * half + 64, n * P:(n + 1) * P],
                                                        gv[:, n, g_ * 64:(g_ + 1) * 64], wsm[:, g_, :], start=True,
                                                        stop=True)
                        last.then_inc(s_sp, 1)
                    n = 0
                    for h in range(HEADS):
                        for i in range(NT):
                            w = (i + 1) * P
                            if n >= 2:
                                eng.wait_ge(s_ex2, n - 1)
                            nc.tensor.matmul(B[n % 2][:, 0:w], qT[0:QK, h, i * P:w], kTm[0:QK, h, 0:w], start=True,
                                             stop=True).then_inc(s_sc, 1)
                            if n >= 1:
                                flip_probs(eng, n - 1)
                            n += 1
                        if h >= 1:
                            pv(eng, h - 1)
                    flip_probs(eng, n - 1)
                    pv(eng, HEADS - 1)
            end_stage()
            nrm_sq = arena[:, 0:1024].rearrange("p (a t) -> p a t", a=2)
            nrm_rs = arena[:, 1024:1536]
            qx = arena[:, 1536:2560].rearrange("p (c t) -> p c t", c=2)
            qx_rs = arena[:, 2560:3584].rearrange("p (c t) -> p c t", c=2)
            Px = [arena[:, 3584 + 1024 * z:4608 + 1024 * z].rearrange("p (i m) -> p i m", i=NT) for z in range(2)]
            PXT = [arena[:, 5632 + 1024 * z:6656 + 1024 * z].rearrange("p (m q) -> p m q", m=2) for z in range(2)]
            oX = arena[:, 7680:8704].rearrange("p (c t) -> p c t", c=2)
            mxx, smx = small[:, 0:16], small[:, 16:32]
            s_o, s_or = sem("out_proj"), sem("out_added")
            s_q0, s_q1, s_q2, s_q3, s_q4 = (sem("xq_done"), sem("xq_squares"), sem("xq_mean"), sem("xq_root"),
                                            sem("xq_normed"))
            s_xs, s_xm, s_xe, s_xn = sem("x_scores"), sem("x_max"), sem("x_probs"), sem("x_probs_normed")
            s_xf, s_xg, s_xv, s_xo = sem("x_flipped"), sem("x_flip_copied"), sem("x_pv"), sem("x_out")
            SCX = float(RN) ** -0.5
            w1v = [ring[:, 3 * u, :].rearrange("p (k n) -> p k n", k=KD) for u in range(2)]
            w3v = [ring[:, 3 * u + 1, :].rearrange("p (k n) -> p k n", k=KD) for u in range(2)]
            w2v = [ring[:, 3 * u + 2, :].rearrange("p (k n) -> p k n", k=HM) for u in range(2)]

            def expert_row(e):
                return bass.ds(layer * NE + e, 1)

            def load_up(eng, u, e, done):
                eng.dma_start(w1v[u], w1_d[expert_row(e)].rearrange("a (k p) n -> p (a k) n", p=P)).then_inc(done[0], 16)
                eng.dma_start(w3v[u], w3_d[expert_row(e)].rearrange("a (k p) n -> p (a k) n", p=P)).then_inc(done[1], 16)

            def load_down(eng, u, e, done):
                eng.dma_start(w2v[u], w2_d[expert_row(e)].rearrange("a (k p) n -> p (a k) n", p=P)).then_inc(done, 16)

            def flip_x(eng, h):
                eng.wait_ge(s_xn, h + 1)
                if h:
                    eng.wait_ge(s_xg, 2 * h)
                for m in range(2):
                    for i in range(NT):
                        last = nc.tensor.transpose(B[4 + m][:, i * P:(i + 1) * P],
                                                   Px[h % 2][:, i, m * P:(m + 1) * P], ident[:, :])
                    last.then_inc(s_xf, 1)

            def pv_x(eng, h):
                rows = slice(64 * (h % 2), 64 * (h % 2) + 64)
                eng.wait_ge(s_xg, 2 * (h + 1))
                if h >= 2:
                    eng.wait_ge(s_xo, h - 1)
                for m in range(2):
                    last = nc.tensor.matmul(B[6 + h % 2][rows, :], memV[:, m, h * 64:(h + 1) * 64],
                                            PXT[h % 2][:, m, :], start=m == 0, stop=m == 1)
                last.then_inc(s_xv, 1)

            def copy_x(eng, h):
                rows = slice(64 * (h % 2), 64 * (h % 2) + 64)
                for m in range(2):
                    eng.wait_ge(s_xf, 2 * h + m + 1)
                    if h >= 2 and m == 0:
                        eng.wait_ge(s_xv, h - 1)
                    eng.activation(PXT[h % 2][:, m, :], B[4 + m][:, :], ACT.Copy).then_inc(s_xg, 1)
                eng.wait_ge(s_xv, h + 1)
                eng.activation(oX[rows, h // 2, :], B[6 + h % 2][rows, :], ACT.Copy).then_inc(s_xo, 1)

            def norm_x(eng, v, h):
                eng.wait_ge(s_xe, 4 * (h + 1))
                v(eng.reciprocal(smx[:, 4 * h:4 * h + 4], smx[:, 4 * h:4 * h + 4]))
                eng.tensor_tensor(Px[h % 2], Px[h % 2],
                                  smx[:, 4 * h:4 * h + 4].unsqueeze(2).to_broadcast([P, NT, MEM]),
                                  ALU.mult).then_inc(s_xn, 1)

            with nc.Block() as block:
                @block.sync
                def _(eng):
                    load_up(eng, 0, 0, s_e[0:2])
                    load_down(eng, 0, 0, s_e[2])

                @block.tensor
                def _(eng):
                    for z in range(2):
                        eng.wait_ge(s_wo[z], 16)
                    for c in range(KD):
                        if c >= 4:
                            eng.wait_ge(s_or, c - 3)
                        for k in range(KD):
                            last = nc.tensor.matmul(B[c % 4][:, :], w_out[:, k, c * P:(c + 1) * P], hT[:, k, :],
                                                    start=k == 0, stop=k == KD - 1)
                        last.then_inc(s_o, 1)
                    norm_pe(eng, 1, B[7], nrm_sq)
                    eng.wait_ge(s_wm, 32)
                    eng.wait_ge(s_h, 2 * KD)
                    for c in range(2):
                        for k in range(KD):
                            last = nc.tensor.matmul(B[c][:, :], wmq[:, k, c * P:(c + 1) * P], hT[:, k, :], start=k == 0,
                                                    stop=k == KD - 1)
                        last.then_inc(s_q0, 1)
                    for c in range(2):
                        eng.wait_ge(s_q1, c + 1)
                        nc.tensor.matmul(B[2 + c][:, :], head_mean[:, :], qx_rs[:, c, :], start=True,
                                         stop=True).then_inc(s_q2, 1)
                    eng.wait_ge(s_q4, 2)
                    for h in range(HEADS):
                        rows = slice(64 * (h % 2), 64 * (h % 2) + 64)
                        if h >= 2:
                            eng.wait_ge(s_xe, 4 * (h - 1))
                        for i in range(NT):
                            last = nc.tensor.matmul(B[2 * (h % 2) + i // 2][:, (i % 2) * MEM:(i % 2 + 1) * MEM],
                                                    qx[rows, h // 2, i * P:(i + 1) * P], memKT[rows, h // 2, :],
                                                    start=True, stop=True)
                        last.then_inc(s_xs, 1)
                        if h:
                            flip_x(eng, h - 1)
                            pv_x(eng, h - 1)
                    flip_x(eng, HEADS - 1)
                    pv_x(eng, HEADS - 1)
                    eng.wait_ge(s_xo, HEADS)
                    for c in range(KD):
                        if c >= 4:
                            eng.wait_ge(s_or, KD + c - 3)
                        for k in range(2):
                            last = nc.tensor.matmul(B[c % 4][:, :], wmo[:, k, c * P:(c + 1) * P], oX[:, k, :],
                                                    start=k == 0, stop=k == 1)
                        last.then_inc(s_o, 1)

                @block.scalar
                def _(eng):
                    a = ach.on(eng)
                    eng.wait_ge(s_or, KD)
                    norm_act(eng, 1, B[7], nrm_sq, nrm_rs)
                    for c in range(2):
                        eng.wait_ge(s_q0, c + 1)
                        eng.activation(qx_rs[:, c, :], B[c][:, :], ACT.Square).then_inc(s_q1, 1)
                    for c in range(2):
                        eng.wait_ge(s_q2, c + 1)
                        eng.activation(qx_rs[:, c, :], B[2 + c][:, :], ACT.Sqrt, bias=epsc[:, 0:1]).then_inc(s_q3, 1)
                    for h in range(HEADS):
                        eng.wait_ge(s_xm, h + 1)
                        if h >= 2:
                            eng.wait_ge(s_xf, 2 * (h - 1))
                        for i in range(NT):
                            n = 4 * h + i
                            eng.activation(Px[h % 2][:, i, :],
                                           B[2 * (h % 2) + i // 2][:, (i % 2) * MEM:(i % 2 + 1) * MEM], ACT.Exp,
                                           scale=SCX, bias=mxx[:, n:n + 1], accum_out=smx[:, n:n + 1]
                                           ).then_inc(s_xe, 1)
                        if h:
                            copy_x(eng, h - 1)
                    copy_x(eng, HEADS - 1)

                @block.vector
                def _(eng):
                    v = vch.on(eng)

                    def add_out(first):
                        for c in range(KD):
                            eng.wait_ge(s_o, first + c + 1)
                            eng.tensor_tensor(xT[:, c, :], xT[:, c, :], B[c % 4][:, :], ALU.add).then_inc(s_or, 1)
                    add_out(0)
                    norm_dve(eng, v, 1, "g_mem", nrm_rs)
                    for c in range(2):
                        eng.wait_ge(s_q3, c + 1)
                        v(eng.reciprocal(qx_rs[:, c, :], qx_rs[:, c, :]))
                        eng.scalar_tensor_tensor(out=qx[:, c, :], in0=B[c][:, :], scalar=col("xq_g"),
                                                 in1=qx_rs[:, c, :], op0=ALU.mult, op1=ALU.mult).then_inc(s_q4, 1)
                    for h in range(HEADS):
                        eng.wait_ge(s_xs, h + 1)
                        for z in range(2):
                            last = eng.tensor_reduce(mxx[:, 4 * h + 2 * z:4 * h + 2 * z + 2],
                                                     B[2 * (h % 2) + z][:, :].rearrange("p (i m) -> p i m", i=2),
                                                     AX, ALU.max)
                        v(last)
                        eng.tensor_scalar(mxx[:, 4 * h:4 * h + 4], mxx[:, 4 * h:4 * h + 4], -SCX, None,
                                          ALU.mult).then_inc(s_xm, 1)
                        if h:
                            norm_x(eng, v, h - 1)
                    norm_x(eng, v, HEADS - 1)
                    add_out(KD)

            end_stage()
            nrm_sq = arena[:, 4096:5120].rearrange("p (a t) -> p a t", a=2)
            nrm_rs = arena[:, 5120:5632]
            htok = arena[:, 0:4096].rearrange("p (i n) -> p i n", i=NT)
            xr = [arena[:, 4096 + 512 * u:4608 + 512 * u] for u in range(2)]
            sel = [arena[:, 5120 + 256 * u:5376 + 256 * u].rearrange("p (i s) -> p i s", i=NT) for u in range(2)]
            xg = [arena[:, 5632 + 512 * u:6144 + 512 * u] for u in range(2)]
            hr = [arena[:, 6656 + 512 * u:7168 + 512 * u] for u in range(2)]
            sg = [arena[:, 7680 + 256 * u:7936 + 256 * u].rearrange("p (m s) -> p m s", m=HM) for u in range(2)]
            hid = [arena[:, 8192 + 256 * u:8448 + 256 * u].rearrange("p (m s) -> p m s", m=HM) for u in range(2)]
            ysb = [arena[:, 8704 + 512 * u:9216 + 512 * u] for u in range(2)]
            lg = arena[:, 9728:9872].rearrange("p (i n) -> p i n", i=NT)
            em, oh1, oh2, M, tmp = [arena[:, 9872 + 128 * z:10000 + 128 * z].rearrange("p (i n) -> p i n", i=NT)
                                    for z in range(5)]
            rankm = arena[:, 10512:10644].rearrange("p (e i) -> p e i", i=NT)
            rank = arena[:, 10644:10772].rearrange("p (i n) -> p i n", i=NT)
            gmax, gsum, m1, m2, ratio, gate1, gate2, idx, slot = [small[:, 4 * z:4 * z + 4] for z in range(9)]
            eg, goh, gt = [small[:, 64 + 16 * z:80 + 16 * z].rearrange("p (i n) -> p i n", i=NT) for z in range(3)]
            gates = em
            spread = xr[1]
            cntf = small[:, 128:160]
            slots_i = [smalli[:, 4 * k:4 * k + 4] for k in range(2)]
            passes_i, most_i = smalli[0:1, 16:48], smalli[0:1, 48:49]
            s_lg, s_ht, s_htc = sem("logits"), sem("h_flipped"), sem("h_token_major")
            s_gd, s_ge2, s_rt2, s_rk = sem("group_logits"), sem("group_exps"), sem("chosen"), sem("ranks")
            s_ed, s_ee = sem("expert_difference"), sem("expert_ratio")
            s_sel, s_g, s_xr, s_tx = sem("selection"), sem("gathered"), sem("gather_copied"), sem("gather_flipped")
            s_xg, s_mu, s_hr, s_th = sem("tokens_ready"), sem("up_done"), sem("up_copied"), sem("up_flipped")
            s_sg, s_hd, s_dn, s_ys = sem("silu_done"), sem("hidden_ready"), sem("down_done"), sem("rows_ready")
            s_yo = [sem(f"rows_written{u}") for u in range(2)]
            s_cb, s_cf = sem("combined"), sem("combine_flipped")

            def bc(ap, n):
                return ap.unsqueeze(2).to_broadcast([P, NT, n])

            def row(ap, n):
                return ap.unsqueeze(1).to_broadcast([P, NT, n])

            with nc.Block() as block:
                @block.sync
                def _(eng):
                    load_up(eng, 1, 1, s_e[3:5])
                    load_down(eng, 1, 1, s_e[5])

                @block.tensor
                def _(eng):
                    norm_pe(eng, 2, B[7], nrm_sq)
                    eng.wait_ge(s_h, 3 * KD)
                    for i in range(NT):
                        for k in range(KD):
                            last = nc.tensor.matmul(B[0][:, i * 36:(i + 1) * 36], hT[:, k, i * P:(i + 1) * P],
                                                    wr[:, k, :], start=k == 0, stop=k == KD - 1)
                    last.then_inc(s_lg, 1)
                    for z in range(2 * NT):
                        if z >= 4:
                            eng.wait_ge(s_htc, z - 3)
                        for k in range(4):
                            kk = 4 * (z % 2) + k
                            last = nc.tensor.transpose(B[3 + z % 4][:, k * P:(k + 1) * P],
                                                       hT[:, kk, (z // 2) * P:(z // 2 + 1) * P], ident[:, :])
                        last.then_inc(s_ht, 1)
                    eng.wait_ge(s_rt2, 1)
                    for i in range(NT):
                        for j in range(i):
                            nc.tensor.matmul(B[1][:, i * NE:(i + 1) * NE], ones[:, :], M[:, j, :], start=j == 0,
                                             stop=False)
                        nc.tensor.matmul(B[1][:, i * NE:(i + 1) * NE], before[:, :], M[:, i, :], start=i == 0,
                                         stop=True)
                    for i in range(NT):
                        last = nc.tensor.matmul(B[2][:, 0:NE], ones[:, :], M[:, i, :], start=i == 0,
                                                stop=i == NT - 1)
                    last.then_inc(s_rk, 1)

                @block.scalar
                def _(eng):
                    norm_act(eng, 2, B[7], nrm_sq, nrm_rs)
                    for z in range(2 * NT):
                        eng.wait_ge(s_ht, z + 1)
                        eng.activation(htok[:, z // 2, 512 * (z % 2):512 * (z % 2) + 512], B[3 + z % 4][:, :],
                                       ACT.Copy).then_inc(s_htc, 1)
                    eng.wait_ge(s_gd, 1)
                    eng.activation(eg, eg, ACT.Exp).then_inc(s_ge2, 1)
                    eng.wait_ge(s_ed, 1)
                    eng.activation(ratio, ratio, ACT.Exp).then_inc(s_ee, 1)

                @block.vector
                def _(eng):
                    v = vch.on(eng)
                    norm_dve(eng, v, 2, "g_ffn", nrm_rs)
                    eng.wait_ge(s_lg, 1)
                    v(eng.tensor_tensor(lg, B[0][:, 0:144].rearrange("p (i n) -> p i n", i=NT), row(brb[:, :], 36),
                                        ALU.add))

                    def first_max(src, n, best, out, t):
                        v(eng.tensor_reduce(best, src, AX, ALU.max))
                        v(eng.tensor_tensor(out, src, bc(best, n), ALU.is_ge))
                        v(eng.scalar_tensor_tensor(out=t, in0=out, scalar=-1000.0, in1=row(slot_iota[:, 0:n], n),
                                                   op0=ALU.mult, op1=ALU.add))
                        v(eng.tensor_reduce(idx, t, AX, ALU.min))
                        v(eng.tensor_tensor(out, t, bc(idx, n), ALU.is_equal))
                    first_max(lg[:, :, 0:NG], NG, gmax, goh, gt)
                    v(eng.tensor_tensor(eg, lg[:, :, 0:NG], bc(gmax, NG), ALU.subtract))
                    eng.sem_inc(s_gd, 1)
                    v(eng.tensor_scalar(gt, goh, BIG, -BIG, ALU.mult, ALU.add))
                    v(eng.tensor_tensor(em.rearrange("p i (g n) -> p i g n", g=NG),
                                        lg[:, :, NG:NG + NE].rearrange("p i (g n) -> p i g n", g=NG),
                                        gt.unsqueeze(3).to_broadcast([P, NT, NG, EPG]), ALU.add))
                    first_max(em, NE, m1, oh1, tmp)
                    v(eng.scalar_tensor_tensor(out=em, in0=oh1, scalar=-2 * BIG, in1=em, op0=ALU.mult, op1=ALU.add))
                    first_max(em, NE, m2, oh2, tmp)
                    v(eng.tensor_tensor(M, oh1, oh2, ALU.add))
                    eng.sem_inc(s_rt2, 1)
                    v(eng.tensor_tensor(ratio, m2, m1, ALU.subtract))
                    eng.sem_inc(s_ed, 1)
                    eng.wait_ge(s_ge2, 1)
                    v(eng.tensor_reduce(gsum, eg, AX, ALU.add))
                    eng.wait_ge(s_ee, 1)
                    v(eng.scalar_tensor_tensor(out=gate1, in0=ratio, scalar=1.0, in1=gsum, op0=ALU.add, op1=ALU.mult))
                    v(eng.reciprocal(gate1, gate1))
                    v(eng.tensor_tensor(gate2, gate1, ratio, ALU.mult))
                    eng.wait_ge(s_rk, 1)
                    v(eng.tensor_scalar(tmp, M, 1e5, -1e5, ALU.mult, ALU.add))
                    v(eng.tensor_copy(rank, B[1][:, 0:128].rearrange("p (i n) -> p i n", i=NT)))
                    v(eng.tensor_tensor(rankm[:, 0:NE, :].rearrange("p e i -> p i e"), rank, tmp, ALU.add))
                    v(eng.memset(rankm[:, NE, :], -1e5))
                    v(eng.tensor_tensor(gates, oh1, bc(gate1, NE), ALU.mult))
                    v(eng.tensor_tensor(tmp, oh2, bc(gate2, NE), ALU.mult))
                    v(eng.tensor_tensor(gates, gates, tmp, ALU.add))
                    for k, (oh, gate) in enumerate(((oh1, gate1), (oh2, gate2))):
                        v(eng.tensor_tensor(tmp, rank, oh, ALU.mult))
                        v(eng.tensor_reduce(slot, tmp, AX, ALU.add))
                        v(eng.tensor_scalar(idx, slot, float(CAP), None, ALU.is_lt))
                        v(eng.tensor_tensor(gate, gate, idx, ALU.mult))
                        v(eng.tensor_tensor(tmp, oh, row(slot0[:, :], NE), ALU.mult))
                        v(eng.tensor_reduce(idx, tmp, AX, ALU.add))
                        v(eng.scalar_tensor_tensor(out=slot, in0=slot, scalar=float(CAP - 1), in1=idx,
                                                   op0=ALU.min, op1=ALU.add))
                        v(eng.tensor_copy(slots_i[k], slot))
                    passes = cntf[0:1, :]
                    v(eng.memset(passes, 1.0))
                    for b in range(1, SEQ // CAP):
                        v(eng.scalar_tensor_tensor(out=passes, in0=B[2][0:1, 0:NE], scalar=float(b * CAP), in1=passes,
                                                   op0=ALU.is_gt, op1=ALU.add))
                    v(eng.tensor_copy(passes_i, passes))
                    v(eng.tensor_reduce(passes[:, 0:1], passes, AX, ALU.max))
                    v(eng.tensor_copy(most_i, passes[:, 0:1]))

            def pe_gather(u):
                for i in range(NT):
                    for half in range(2):
                        last = nc.tensor.matmul(B[u][CAP * half:CAP * half + CAP, :], sel[u][:, i, :],
                                                htok[:, i, 512 * half:512 * half + 512], start=i == 0,
                                                stop=i == NT - 1)
                return last

            def pe_flip(bank, src):
                for j in range(4):
                    last = nc.tensor.transpose(bank[:, j * P:(j + 1) * P], src[:, j * P:(j + 1) * P], ident[:, :])
                return last

            def pe_up(u):
                for k in range(KD):
                    o = (k % 4) * P + (k // 4) * CAP
                    for half, w in enumerate((w1v[u], w3v[u])):
                        last = nc.tensor.matmul(B[3 + 3 * u][CAP * half:CAP * half + CAP, :], xg[u][:, o:o + CAP],
                                                w[:, k, :], start=k == 0, stop=k == KD - 1)
                return last

            def pe_down(u):
                for m in range(HM):
                    for half in range(2):
                        last = nc.tensor.matmul(B[5 + 2 * u][CAP * half:CAP * half + CAP, :], hid[u][:, m, :],
                                                w2v[u][:, m, 512 * half:512 * half + 512], start=m == 0,
                                                stop=m == HM - 1)
                return last

            def up_half(half):
                return B[4][:, :].rearrange("p (m a s) -> p m a s", m=HM, a=2)[:, :, half, :]

            def expert_rows(e):
                return ys_d[bass.ds(e * CAP, CAP), :].rearrange("s (a n) -> a s n", a=2)

            def select(eng, u, ranks):
                return eng.tensor_tensor(sel[u], slot_iota[:, 0:CAP].unsqueeze(1).to_broadcast([P, NT, CAP]),
                                         ranks.rearrange("p a i -> p (a i)").unsqueeze(2).to_broadcast([P, NT, CAP]),
                                         ALU.is_equal)

            with nc.Block() as block:
                @block.sync
                def _(eng):
                    eng.sem_inc(s_yo[0], 16)
                    eng.sem_inc(s_yo[1], 16)

                    def store_rows(u, i):
                        eng.wait_ge(s_ys, 2 * i + (u + 3))
                        eng.dma_start(expert_rows(2 * i + u), ysb[u]).then_inc(s_yo[u], 16)
                    with eng.Fori(0, NE // 2 - 1) as i:
                        for u in range(2):
                            eng.wait_ge(s_mu, 2 * i + (u + 1))
                            load_up(eng, u, 2 * i + (u + 2), s_e[3 * u:3 * u + 2])
                            eng.wait_ge(s_dn, 2 * i + (u + 1))
                            load_down(eng, u, 2 * i + (u + 2), s_e[3 * u + 2])
                            store_rows(u, i)
                    for u in range(2):
                        store_rows(u, NE // 2 - 1)
                    for u in range(2):
                        eng.wait_ge(s_yo[u], 16 * (NE // 2 + 1))

                @block.tensor
                def _(eng):
                    eng.wait_ge(s_sel, 1)
                    pe_gather(0).then_inc(s_g, 1)
                    eng.wait_ge(s_xr, 1)
                    pe_flip(B[2], xr[0]).then_inc(s_tx, 1)
                    with eng.Fori(0, NE // 2) as i:
                        for u in range(2):
                            eng.wait_ge(s_e[3 * u], 16 * i + 16)
                            eng.wait_ge(s_e[3 * u + 1], 16 * i + 16)
                            eng.wait_ge(s_xg, 2 * i + (u + 1))
                            pe_up(u).then_inc(s_mu, 1)
                            eng.wait_ge(s_sel, 2 * i + (u + 2))
                            pe_gather(1 - u).then_inc(s_g, 1)
                            eng.wait_ge(s_hr, 2 * i + (u + 1))
                            pe_flip(B[4], hr[u]).then_inc(s_th, 1)
                            eng.wait_ge(s_xr, 2 * i + (u + 2))
                            pe_flip(B[2], xr[1 - u]).then_inc(s_tx, 1)
                            eng.wait_ge(s_e[3 * u + 2], 16 * i + 16)
                            eng.wait_ge(s_ys, 2 * i + (u + 1))
                            eng.wait_ge(s_hd, 2 * i + (u + 1))
                            pe_down(u).then_inc(s_dn, 1)

                @block.scalar
                def _(eng):
                    eng.wait_ge(s_g, 1)
                    eng.activation(xr[0], B[0][:, :], ACT.Copy).then_inc(s_xr, 1)
                    with eng.Fori(0, NE // 2) as i:
                        for u in range(2):
                            eng.wait_ge(s_mu, 2 * i + (u + 1))
                            eng.activation(hr[u], B[3 + 3 * u][:, :], ACT.Copy).then_inc(s_hr, 1)
                            eng.wait_ge(s_g, 2 * i + (u + 2))
                            eng.activation(xr[1 - u], B[1 - u][:, :], ACT.Copy).then_inc(s_xr, 1)
                            eng.wait_ge(s_th, 2 * i + (u + 1))
                            eng.activation(sg[u], up_half(0), ACT.Silu).then_inc(s_sg, 1)

                @block.vector
                def _(eng):
                    eng.sem_inc(s_ys, 2)
                    select(eng, 0, rankm[:, 0:1, :]).then_inc(s_sel, 1)
                    eng.wait_ge(s_tx, 1)
                    eng.tensor_copy(xg[0], B[2][:, :]).then_inc(s_xg, 1)
                    with eng.Fori(0, NE // 2) as i:
                        for u in range(2):
                            eng.wait_ge(s_g, 2 * i + (u + 1))
                            select(eng, 1 - u, rankm[:, bass.ds(2 * i + (u + 1), 1), :]).then_inc(s_sel, 1)
                            eng.wait_ge(s_sg, 2 * i + (u + 1))
                            eng.tensor_tensor(hid[u], sg[u], up_half(1), ALU.mult).then_inc(s_hd, 1)
                            eng.wait_ge(s_tx, 2 * i + (u + 2))
                            eng.tensor_copy(xg[1 - u], B[2][:, :]).then_inc(s_xg, 1)
                            eng.wait_ge(s_dn, 2 * i + (u + 1))
                            eng.wait_ge(s_yo[u], 16 * i + 16)
                            eng.tensor_copy(ysb[u], B[5 + 2 * u][:, :]).then_inc(s_ys, 1)

            o_sem = {x: sem("more_" + x) for x in ("w", "sel", "g", "xr", "tx", "xg", "up", "hr", "th", "sg", "hid",
                                                   "dn", "ys", "sp", "spt", "spc", "add")}
            most = nc.values_load(most_i, min_val=1, max_val=SEQ // CAP)
            with nc.If(most > 1):
                with nc.Fori(0, NE) as e:
                    passes = nc.values_load(smalli[0:1, bass.ds(16 + e, 1)], min_val=1, max_val=SEQ // CAP)
                    with nc.If(passes > 1):
                        with nc.Fori(1, passes) as b:
                            with nc.Block() as block:
                                @block.sync
                                def _(eng):
                                    load_up(eng, 0, e, (o_sem["w"], o_sem["w"]))
                                    load_down(eng, 0, e, o_sem["w"])
                                    eng.wait_ge(o_sem["w"], 48)

                                @block.tensor
                                def _(eng):
                                    eng.wait_ge(o_sem["sel"], 1)
                                    pe_gather(0).then_inc(o_sem["g"], 1)
                                    eng.wait_ge(o_sem["xr"], 1)
                                    pe_flip(B[2], xr[0]).then_inc(o_sem["tx"], 1)
                                    eng.wait_ge(o_sem["w"], 48)
                                    eng.wait_ge(o_sem["xg"], 1)
                                    pe_up(0).then_inc(o_sem["up"], 1)
                                    eng.wait_ge(o_sem["hr"], 1)
                                    pe_flip(B[4], hr[0]).then_inc(o_sem["th"], 1)
                                    eng.wait_ge(o_sem["hid"], 1)
                                    pe_down(0).then_inc(o_sem["dn"], 1)
                                    eng.wait_ge(o_sem["sp"], 1)
                                    pe_flip(B[1], hr[1]).then_inc(o_sem["spt"], 1)
                                    eng.wait_ge(o_sem["spc"], 1)
                                    eng.wait_ge(o_sem["ys"], 1)
                                    for k in range(KD):
                                        rows = slice(CAP * (k // 4), CAP * (k // 4) + CAP)
                                        nc.tensor.matmul(B[k][:, :], ysb[0][rows, (k % 4) * P:(k % 4 + 1) * P],
                                                         spread[rows, :], start=True,
                                                         stop=True).then_inc(o_sem["add"], 1)

                                @block.scalar
                                def _(eng):
                                    eng.wait_ge(o_sem["g"], 1)
                                    eng.activation(xr[0], B[0][:, :], ACT.Copy).then_inc(o_sem["xr"], 1)
                                    eng.wait_ge(o_sem["up"], 1)
                                    eng.activation(hr[0], B[3][:, :], ACT.Copy).then_inc(o_sem["hr"], 1)
                                    eng.wait_ge(o_sem["th"], 1)
                                    eng.activation(sg[0], up_half(0), ACT.Silu).then_inc(o_sem["sg"], 1)
                                    eng.wait_ge(o_sem["spt"], 1)
                                    eng.activation(spread, B[1][:, :], ACT.Copy).then_inc(o_sem["spc"], 1)

                                @block.vector
                                def _(eng):
                                    eng.tensor_tensor(
                                        sel[0],
                                        slot_iota[:, bass.ds(b * CAP, CAP)].unsqueeze(1).to_broadcast([P, NT, CAP]),
                                        rankm[:, bass.ds(e, 1), :].rearrange("p a i -> p (a i)").unsqueeze(2)
                                        .to_broadcast([P, NT, CAP]), ALU.is_equal).then_inc(o_sem["sel"], 1)
                                    eng.wait_ge(o_sem["sel"], 1)
                                    for half in range(2):
                                        last = eng.tensor_tensor(
                                            hr[1].rearrange("p (i a s) -> p i a s", i=NT, a=2)[:, :, half, :], sel[0],
                                            gates[:, :, bass.ds(e, 1)].to_broadcast([P, NT, CAP]), ALU.mult)
                                    last.then_inc(o_sem["sp"], 1)
                                    eng.wait_ge(o_sem["tx"], 1)
                                    eng.tensor_copy(xg[0], B[2][:, :]).then_inc(o_sem["xg"], 1)
                                    eng.wait_ge(o_sem["sg"], 1)
                                    eng.tensor_tensor(hid[0], sg[0], up_half(1), ALU.mult).then_inc(o_sem["hid"], 1)
                                    eng.wait_ge(o_sem["dn"], 1)
                                    eng.tensor_copy(ysb[0], B[5][:, :]).then_inc(o_sem["ys"], 1)
                                    for k in range(KD):
                                        eng.wait_ge(o_sem["add"], k + 1)
                                        eng.tensor_tensor(xT[:, k, :], xT[:, k, :], B[k][:, :], ALU.add)
                            clear(o_sem.values())
                            nc.all_engine_barrier()
                        for eng in (nc.sync, nc.gpsimd, nc.scalar, nc.vector, nc.tensor):
                            eng.nop()
                    for eng in (nc.sync, nc.gpsimd, nc.scalar, nc.vector, nc.tensor):
                        eng.nop()
                for eng in (nc.sync, nc.gpsimd, nc.scalar, nc.vector, nc.tensor):
                    eng.nop()

            def add_rows(eng, i):
                eng.wait_ge(s_cf, i + 1)
                for half in range(2):
                    x = xT[:, 4 * half:4 * half + 4, i * P:(i + 1) * P]
                    eng.tensor_tensor(x, x, B[2 * i + half][:, :].rearrange("p (k t) -> p k t", k=4), ALU.add)

            yg = [[ring_view(2 * k + i // 2, 2048 * (i % 2), 1024) for i in range(NT)] for k in range(2)]
            with nc.Block() as block:
                @block.gpsimd
                def _(eng):
                    for i in range(NT):
                        for k in range(2):
                            eng.indirect_dma_start(out=yg[k][i], out_offset=None, in_=ys_d,
                                                   in_offset=bass.IndirectOffsetOnAxis(ap=slots_i[k][:, i:i + 1],
                                                                                       axis=0)).then_inc(s_ygs[i], 16)

                @block.vector
                def _(eng):
                    v = vch.on(eng)
                    for i in range(NT):
                        eng.wait_ge(s_ygs[i], 32 * layer + 32)
                        v(eng.tensor_scalar(yg[0][i], yg[0][i], gate1[:, i:i + 1], None, ALU.mult))
                        eng.scalar_tensor_tensor(out=yg[0][i], in0=yg[1][i], scalar=gate2[:, i:i + 1], in1=yg[0][i],
                                                 op0=ALU.mult, op1=ALU.add).then_inc(s_cb, 1)
                        if i:
                            add_rows(eng, i - 1)
                    add_rows(eng, NT - 1)

                @block.tensor
                def _(eng):
                    for i in range(NT):
                        eng.wait_ge(s_cb, i + 1)
                        for half in range(2):
                            for k in range(4):
                                kk = 4 * half + k
                                last = nc.tensor.transpose(B[2 * i + half][:, k * P:(k + 1) * P],
                                                           yg[0][i][:, kk * P:(kk + 1) * P], ident[:, :])
                        last.then_inc(s_cf, 1)

            clear(layer_sems)
            end_stage()

        s_out = ctx.enter_context(nc.semaphore("out_written"))
        with nc.Block() as block:
            @block.sync
            def _(eng):
                eng.dma_start(out_d, xT[:, :, :]).then_inc(s_out, 16)
                eng.wait_ge(s_out, 16)


_F = np.float32


def pack(inputs):
    c = np.ascontiguousarray
    L = DEPTH

    def cols(a, n):
        return a.reshape(L, n, P).transpose(0, 2, 1)

    def zeros(*s):
        return np.zeros(s, _F)
    i = {k: np.asarray(v) for k, v in inputs.items()}
    mu = np.concatenate([i["shift_mu"], zeros(L, 15 * P - i["shift_mu"].shape[1])], 1)
    qn = i["mla_q_norm_g"]
    cq = np.stack([np.concatenate([zeros(L, 32), qn[:, :96]], 1), np.concatenate([qn[:, 96:], zeros(L, 32)], 1)], 2)
    pad32 = zeros(L, 32)
    colp = np.concatenate([
        cols(i["norm_mix_g"], 8), cols(i["norm_mem_g"], 8), cols(i["norm_ffn_g"], 8), cols(mu, 15),
        cols(i["rwkv_w0"], 4), cols(i["rwkv_a0"], 4), cols(i["rwkv_k_k"], 4), cols(i["rwkv_k_a"], 4),
        cols(i["rwkv_r_k"].reshape(L, 512), 4), cols(i["rwkv_ln_g"], 4), cols(i["rwkv_ln_b"], 4), cq,
        i["mla_kv_norm_g"][:, :, None], np.concatenate([i["mla_q_g"], pad32], 1)[:, :, None],
        np.concatenate([i["mla_k_g"], pad32], 1)[:, :, None], cols(i["gmlp_v_norm_g"], 2),
        np.concatenate([i["mem_q_g"], i["mem_q_g"]], 1)[:, :, None]], 2)
    memcol = np.concatenate([i["mem_norm_g"].reshape(8, P).T,
                             np.concatenate([i["mem_k_g"], i["mem_k_g"]])[:, None]], 1)
    wuq = i["mla_w_uq"]
    wuq = np.stack([np.concatenate([zeros(L, 32, 384), wuq[:, :96]], 1),
                    np.concatenate([wuq[:, 96:], zeros(L, 32, 384)], 1)], 2)
    wr = np.concatenate([i["moe_w_group"], i["moe_w_expert"]], 2).reshape(L, 8, P, NG + NE).transpose(0, 2, 1, 3)
    inv = np.power(_F(10000.0), -np.arange(HALF, dtype=_F) * _F(2.0) / _F(32)).astype(_F)
    gup = i["rwkv_g_up"]
    out = {
        "xT": i["x"][0].T.reshape(KD, P, SEQ).transpose(1, 0, 2),
        "memT": i["mem"][0].T.reshape(KD, P, MEM).transpose(1, 0, 2),
        "pos": i["positions"][0].reshape(NT, P).T,
        "inv": np.repeat(inv[None], P, 0),
        "colp": colp, "memcol": memcol, "w_in": i["w_in"],
        "lora": np.concatenate([i["rwkv_w_up"], i["rwkv_a_up"]], 1),
        "gup": gup[:, :P], "gup2": gup[:, P:], "wuq": wuq, "wukv": i["mla_w_ukv"],
        "wsT": i["gmlp_ws"].transpose(0, 3, 1, 2), "gb": i["gmlp_b"], "w_out": i["w_out"], "wkv": i["mem_w_kv"],
        "wmq": i["mem_w_q"], "wmo": i["mem_w_o"], "wr": wr,
        "br": np.concatenate([i["moe_b_group"], i["moe_b_expert"]], 1),
        "w1": i["moe_w1"].reshape(L * NE, D, DE), "w3": i["moe_w3"].reshape(L * NE, D, DE),
        "w2": i["moe_w2"].reshape(L * NE, DE, D),
    }
    return {k: c(a) for k, a in out.items()}


def kernel(**inputs):
    import concourse.bacc as _bacc
    from concourse.bass_utils import run_bass_kernel_spmd as _run

    nc = _bacc.Bacc("TRN2", target_bir_lowering=False, num_devices=1)
    arrays, args = {}, []
    for name, a in pack(inputs).items():
        arrays[f"in_{name}"] = a
        args.append(nc.dram_tensor(f"in_{name}", a.shape, mybir.dt.from_np(a.dtype), kind="ExternalInput").ap())
    out = nc.dram_tensor("out_xT", (P, KD, SEQ), F32, kind="ExternalOutput").ap()
    build(nc, *args, out)
    r = _run(nc, [arrays], core_ids=[0])
    got = r.results[0]["out_xT"]
    return np.ascontiguousarray(got.transpose(1, 0, 2).reshape(D, SEQ).T)[None]
```

```python
import numpy as np
import concourse.bass as bass
from concourse import mybir
from contextlib import ExitStack

F32 = mybir.dt.float32
I32 = mybir.dt.int32
ALU = mybir.AluOpType
ACT = mybir.ActivationFunctionType
AX = mybir.AxisListType.X

P = 128
DEPTH, SEQ, D = 2, 512, 1024
NT = SEQ // P
KD = D // P
MEM = 256
RC = 4
RH, RN = 8, 64
HEADS = 4
QK, NOPE, HALF = 96, 64, 16
NG, NE, EPG = 4, 32, 8
DE = 512
HM = DE // P
CAP = 64
EPS, GN_EPS = 1e-6, 64e-5
HALF_DECAY = 0.5 * float(np.exp(-0.5))
BIG = 1e30
PI = float(np.pi)

UNIT_COLS = [(0, 512), (512, 512), (1024, 512), (1536, 480), (2016, 416), (2432, 256)]
TILE = [(P * j, P, j // 4, True) for j in range(15)] + [(1920, 96, 3, False), (2016, P, 4, False),
                                                        (2176, P, 4, False), (2304, P, 4, False)]
TILE_ORDER = [12, 13, 14, 15, 4, 5, 6, 7, 0, 1, 2, 3, 8, 9, 10, 11, 16, 17, 18]
KR_COL, GV_COL = 2144, 2432

COLS = {}
_at = 0
for _name, _n in [("g_mix", 8), ("g_mem", 8), ("g_ffn", 8), ("mu", 15), ("w0", 4), ("a0", 4), ("k_k", 4),
                  ("k_a", 4), ("r_k", 4), ("ln_g", 4), ("ln_b", 4), ("cq_g", 2), ("ckv_g", 1), ("q_g", 1),
                  ("k_g", 1), ("gv_g", 2), ("xq_g", 1)]:
    COLS[_name] = _at
    _at += _n
NCOL = _at


class Chain:

    def __init__(self, sem):
        self.sem, self.n = sem, 0

    def on(self, eng):
        def step(ins):
            self.n += 1
            ins.then_inc(self.sem, 1)
            eng.wait_ge(self.sem, self.n)
        return step


def build(nc, xT_d, memT_d, pos_d, inv_d, colp_d, memcol_d, w_in_d, lora_d, gup_d, gup2_d, wuq_d, wukv_d, wsT_d,
          gb_d, w_out_d, wkv_d, wmq_d, wmo_d, wr_d, br_d, w1_d, w3_d, w2_d, out_d):
    ctx = ExitStack()
    with ctx:
        ys_d = nc.dram_tensor("expert_rows", (NE * CAP, D), F32, kind="Internal").ap()

        def sb(name, shape, dt=F32):
            return ctx.enter_context(nc.sbuf_tensor(name, shape, dt))

        stage = []
        held = [ExitStack()]

        def sem(name):
            stage.append(held[0].enter_context(nc.semaphore(name)))
            return stage[-1]

        def clear(some):
            nums = sorted(x.num for x in some)
            first = nums[0]
            for a, b in zip(nums, nums[1:] + [None]):
                if b != a + 1:
                    nc.sync.sem_clear(range(first, a + 1))
                    first = b

        def end_stage():
            clear(stage)
            nc.all_engine_barrier()
            held[0].close()
            stage.clear()
            held[0] = ExitStack()

        s_ygs = [ctx.enter_context(nc.semaphore(f"rows_gathered{i}")) for i in range(NT)]
        layer_sems = []

        def layer_sem(name):
            layer_sems.append(ctx.enter_context(nc.semaphore(name)))
            return layer_sems[-1]

        B = [ctx.enter_context(nc.psum_tensor(f"bank{i}", [P, 512], F32)) for i in range(8)]

        xT = sb("xT", [P, KD, SEQ])
        hT = sb("hT", [P, KD, SEQ])
        ring = sb("ring", [P, 6, 4096])
        arena = sb("arena", [P, 10880])
        ident = sb("ident", [P, P])
        ones_mean = sb("ones_mean", [P, P])
        ones = sb("ones", [P, P])
        head_sum = sb("head_sum", [P, P])
        head_mean = sb("head_mean", [P, P])
        before = sb("before", [P, P])
        mask4 = sb("mask4", [P, 4, P])
        causal = sb("causal", [P, P])
        pair1 = sb("pair1", [P, P])
        lvl = sb("lvl", [P, 6, 64])
        scan_keep = sb("scan_keep", [P, SEQ])
        slot_iota = sb("slot_iota", [P, SEQ])
        slot0 = sb("slot0", [P, NE])
        epsc = sb("epsc", [P, 3])
        colp = sb("colp", [P, NCOL])
        half0 = sb("half0", [P, 12])
        lora_w = sb("lora_w", [P, 512])
        gup_w = sb("gup_w", [P, 512])
        gup2_w = sb("gup2_w", [32, 512])
        wuq = sb("wuq", [P, 2, HEADS * QK])
        wukv = sb("wukv", [P, 512])
        wr = sb("wr", [P, KD, NG + NE])
        brb = sb("brb", [P, NG + NE])
        memKT = sb("memKT", [P, 2, MEM])
        memV = sb("memV", [P, 2, MEM])
        cosT = sb("cosT", [P, NT, HALF])
        sinT = sb("sinT", [P, NT, HALF])
        shp = sb("shift_in", [P, 2, SEQ + 1])
        ST = sb("ST", [P, RC, RN])
        small = sb("small", [P, 640])
        smalli = sb("smalli", [P, 64], I32)

        rT = arena[:, 0:2048].rearrange("p (c t) -> p c t", c=RC)
        kT = arena[:, 2048:4096].rearrange("p (c t) -> p c t", c=RC)
        vT = arena[:, 4096:6144].rearrange("p (c t) -> p c t", c=RC)
        lora = arena[:, 6144:6656]
        gd = arena[:, 6656:7168]
        t14 = arena[:, 7168:7680]
        cq2 = arena[:, 7680:8192]
        ckv = arena[:, 8192:8704]
        uT = arena[:, 8704:9728].rearrange("p (c t) -> p c t", c=2)
        gv = arena[:, 9728:10752].rearrange("p (i n) -> p i n", i=NT)
        kr = arena[:, 10752:10880].rearrange("p (i n) -> p i n", i=NT)

        def ring_view(unit, first, n):
            return ring[:, unit, first:first + n]

        def fours(ap):
            return ap.rearrange("p (c t) -> p c t", c=RC)

        def col(name, i=0):
            return colp[:, COLS[name] + i:COLS[name] + i + 1]

        s_in = sem("inputs_loaded")
        s_gc = sem("pool_const")
        s_vc = sem("dve_order")
        s_ac = sem("act_order")
        s_gp = sem("pool_order")
        s_done = sem("setup_done")
        s_msq = sem("mem_squares")
        s_mms = sem("mem_mean")
        s_mrt = sem("mem_root")
        s_mh = sem("mem_normed")
        s_mkv = sem("mem_kv")
        s_mev = sem("mem_kv_copied")
        s_mk2 = sem("mem_k_mean")
        vch, ach, gch = Chain(s_vc), Chain(s_ac), Chain(s_gp)
        memx = ring[:, 1, 0:2048].rearrange("p (k t) -> p k t", k=KD)
        memh = ring[:, 1, 2048:4096].rearrange("p (k t) -> p k t", k=KD)
        wkv = ring[:, 2, :].rearrange("p (k n) -> p k n", k=KD)
        memcol = small[:, 600:609]

        with nc.Block() as block:
            @block.sync
            def _(eng):
                eng.dma_start(xT[:, :, :], xT_d).then_inc(s_in, 16)
                eng.dma_start(memx, memT_d).then_inc(s_in, 16)
                eng.dma_start(memcol, memcol_d).then_inc(s_in, 16)
                eng.dma_start(wkv, wkv_d.rearrange("(k p) n -> p k n", p=P)).then_inc(s_in, 16)
                eng.dma_start(smalli[:, 0:NT], pos_d).then_inc(s_in, 16)
                eng.dma_start(small[:, 0:HALF], inv_d).then_inc(s_in, 16)
                eng.wait_ge(s_in, 16 * 6)

            @block.gpsimd
            def _(eng):
                g = gch.on(eng)

                def fill(t, v):
                    g(eng.memset(t, v))

                def keep(t, pattern, base, cm, op, other):
                    g(eng.affine_select(out=t, in_=t, compare_op=op, fill=other, base=base, pattern=pattern,
                                        channel_multiplier=cm))
                fill(ident[:, :], 0.0)
                keep(ident[:, :], [[-1, P]], 0, 1, ALU.not_equal, 1.0)
                fill(ones[:, :], 1.0)
                fill(ones_mean[:, :], 1.0 / D)
                for t, v in ((head_sum, 1.0), (head_mean, 1.0 / RN)):
                    fill(t[:, :], 0.0)
                    fill(t[0:64, 0:64], v)
                    fill(t[64:128, 64:128], v)
                fill(before[:, :], 1.0)
                keep(before[:, :], [[1, P]], 0, -1, ALU.is_gt, 0.0)
                fill(mask4[:, :, :], 1.0)
                keep(mask4[:, 0, :], [[-1, P]], 0, 1, ALU.is_gt, 0.0)
                keep(mask4[:, 1, :], [[1, P]], 0, -1, ALU.is_gt, 0.0)
                keep(mask4[:, 2, :], [[1, P]], 0, -1, ALU.is_ge, 0.0)
                keep(mask4[:, 3, :], [[1, P]], 0, -1, ALU.is_ge, 0.0)
                fill(causal[:, :], 0.0)
                keep(causal[:, :], [[-1, P]], 0, 1, ALU.is_ge, -BIG)
                fill(pair1[:, :], 0.0)
                v = pair1[:, :].rearrange("p (a b) -> p a b", b=2)[:, :, 0]
                keep(v, [[-2, 64]], -1, 1, ALU.not_equal, 1.0)
                fill(lvl[:, :, :], 1.0)
                for L in range(6):
                    b = 2 << L
                    v = lvl[:, L, :].rearrange("p (a j) -> p a j", j=b)
                    keep(v, [[-2 * b, 64 // b], [0, b]], 0, 1, ALU.is_ge, 0.0)
                    keep(v, [[2 * b, 64 // b], [0, b]], b, -1, ALU.is_gt, 0.0)
                fill(scan_keep[:, :], 1.0)
                for n in range(NT):
                    fill(scan_keep[:, n * P:n * P + 1], 0.0)
                g(eng.iota(slot_iota[:, :], pattern=[[1, SEQ]], base=0, channel_multiplier=0,
                           allow_small_or_imprecise_dtypes=True))
                g(eng.iota(slot0[:, :], pattern=[[CAP, NE]], base=0, channel_multiplier=0,
                           allow_small_or_imprecise_dtypes=True))
                fill(epsc[:, 0:1], EPS)
                fill(epsc[:, 1:2], GN_EPS)
                fill(epsc[:, 2:3], 0.0)
                eng.sem_inc(s_gc, 1)

            @block.vector
            def _(eng):
                v = vch.on(eng)
                eng.wait_ge(s_in, 16 * 6)
                pf = small[:, 16:20]
                v(eng.tensor_copy(pf, smalli[:, 0:NT]))
                ang, kq, ang2 = small[:, 32:96], small[:, 96:160], small[:, 160:224]
                v(eng.tensor_tensor(ang.rearrange("p (i j) -> p i j", i=NT),
                                    pf.unsqueeze(2).to_broadcast([P, NT, HALF]),
                                    small[:, 0:HALF].unsqueeze(1).to_broadcast([P, NT, HALF]), ALU.mult))
                v(eng.tensor_scalar(kq, ang, float(1 / (2 * np.pi)), 12582912.0, ALU.mult, ALU.add))
                v(eng.tensor_scalar(kq, kq, -12582912.0, None, ALU.add))
                c1 = 6.28125
                c2 = float(np.float32(np.float64(2 * np.pi) - c1).view(np.uint32) & 0xFFFFF000)
                c2 = float(np.array([int(c2)], np.uint32).view(np.float32)[0])
                c3 = float(np.float64(2 * np.pi) - c1 - c2)
                for c in (c1, c2, c3):
                    v(eng.scalar_tensor_tensor(out=ang, in0=kq, scalar=-c, in1=ang, op0=ALU.mult, op1=ALU.add))
                v(eng.tensor_scalar(ang2, ang, PI / 2, None, ALU.add))
                v(eng.tensor_scalar(kq, ang2, PI, -2 * PI, ALU.is_gt, ALU.mult))
                v(eng.tensor_tensor(ang2, ang2, kq, ALU.add))
                for a in (ang, ang2):
                    v(eng.tensor_scalar(a, a, -PI, PI, ALU.max, ALU.min))
                eng.sem_inc(s_done, 1)
                eng.wait_ge(s_mrt, 1)
                rs = small[:, 256:512]
                v(eng.reciprocal(rs, rs))
                for k in range(KD):
                    eng.scalar_tensor_tensor(out=memh[:, k, :], in0=memx[:, k, :], scalar=memcol[:, k:k + 1],
                                             in1=rs, op0=ALU.mult, op1=ALU.mult).then_inc(s_mh, 1)
                eng.wait_ge(s_mrt, 2)
                krs = ring_view(3, 1024, 512).rearrange("p (c t) -> p c t", c=2)
                v(eng.reciprocal(krs, krs))
                for c in range(2):
                    eng.scalar_tensor_tensor(out=memKT[:, c, :], in0=B[c][:, 0:MEM], scalar=memcol[:, 8:9],
                                             in1=krs[:, c, :], op0=ALU.mult, op1=ALU.mult).then_inc(s_mev, 1)

            @block.scalar
            def _(eng):
                a = ach.on(eng)
                eng.wait_ge(s_in, 16 * 6)
                eng.wait_ge(s_gc, 1)
                msq = ring_view(3, 0, 512).rearrange("p (c t) -> p c t", c=2)
                for k in range(KD):
                    if k >= 2:
                        eng.wait_ge(s_mms, k - 1)
                    eng.activation(msq[:, k % 2, :], memx[:, k, :], ACT.Square).then_inc(s_msq, 1)
                eng.wait_ge(s_mms, KD)
                eng.activation(small[:, 256:512], B[0][:, 0:MEM], ACT.Sqrt, bias=epsc[:, 0:1]).then_inc(s_mrt, 1)
                ksq = ring_view(3, 512, 512).rearrange("p (c t) -> p c t", c=2)
                for c in range(2):
                    eng.wait_ge(s_mkv, c + 1)
                    eng.activation(ksq[:, c, :], B[c][:, 0:MEM], ACT.Square).then_inc(s_msq, 1)
                for i in range(2):
                    eng.wait_ge(s_mkv, 3 + i)
                    eng.activation(memV[:, i, :], B[2 + i][:, 0:MEM], ACT.Copy).then_inc(s_mev, 1)
                krs = ring_view(3, 1024, 512).rearrange("p (c t) -> p c t", c=2)
                eng.wait_ge(s_mk2, 2)
                eng.activation(krs[:, 0, :], B[4][:, 0:MEM], ACT.Sqrt, bias=epsc[:, 0:1])
                eng.activation(krs[:, 1, :], B[5][:, 0:MEM], ACT.Sqrt, bias=epsc[:, 0:1]).then_inc(s_mrt, 1)
                eng.wait_ge(s_done, 1)
                a(eng.activation(sinT[:, :, :], small[:, 32:96].rearrange("p (i j) -> p i j", i=NT), ACT.Sin))
                a(eng.activation(cosT[:, :, :], small[:, 160:224].rearrange("p (i j) -> p i j", i=NT), ACT.Sin))

            @block.tensor
            def _(eng):
                eng.wait_ge(s_gc, 1)
                msq = ring_view(3, 0, 512).rearrange("p (c t) -> p c t", c=2)
                for k in range(KD):
                    eng.wait_ge(s_msq, k + 1)
                    nc.tensor.matmul(B[0][:, 0:MEM], ones_mean[:, :], msq[:, k % 2, :], start=k == 0,
                                     stop=k == KD - 1).then_inc(s_mms, 1)
                eng.wait_ge(s_mh, KD)
                for c in range(2):
                    for k in range(KD):
                        last = nc.tensor.matmul(B[c][:, 0:MEM], wkv[:, k, c * P:(c + 1) * P], memh[:, k, :],
                                                start=k == 0, stop=k == KD - 1)
                    last.then_inc(s_mkv, 1)
                for i in range(2):
                    for k in range(KD):
                        last = nc.tensor.matmul(B[2 + i][:, 0:MEM], memh[:, k, i * P:(i + 1) * P],
                                                wkv[:, k, MEM:2 * MEM], start=k == 0, stop=k == KD - 1)
                    last.then_inc(s_mkv, 1)
                ksq = ring_view(3, 512, 512).rearrange("p (c t) -> p c t", c=2)
                eng.wait_ge(s_msq, KD + 2)
                for c in range(2):
                    nc.tensor.matmul(B[4 + c][:, 0:MEM], head_mean[:, :], ksq[:, c, :], start=True,
                                     stop=True).then_inc(s_mk2, 1)

        end_stage()
        s_vc, s_ac, s_gp = layer_sem("dve_order_l"), layer_sem("act_order_l"), layer_sem("pool_order_l")
        vch, ach, gch = Chain(s_vc), Chain(s_ac), Chain(s_gp)
        s_par = layer_sem("params_loaded")
        s_sq, s_sqd = layer_sem("squares"), layer_sem("squares_summed")
        s_rt, s_h = layer_sem("norm_root"), layer_sem("h_ready")
        s_rr, s_rb = layer_sem("norm_factors"), layer_sem("norm_factors_spread")
        s_nm = layer_sem("norm_means")
        s_wo = [layer_sem(f"w_out_loaded{z}") for z in range(2)]
        s_wm = layer_sem("w_mem_loaded")
        s_e = [layer_sem(f"expert_weights{u}") for u in range(6)]

        with nc.Fori(0, DEPTH) as layer:
            lay = bass.ds(layer, 1)

            rs4 = small[:, 624:628]

            def norm_squares(eng, n0, sqb, grown=None):
                for k in range(KD):
                    if grown is not None:
                        eng.wait_ge(s_or, grown + k + 1)
                    if n0 or k >= 2:
                        eng.wait_ge(s_sqd, n0 * KD + k - 1)
                    eng.activation(sqb[:, k % 2, :], xT[:, k, :], ACT.Square).then_inc(s_sq, 1)
                eng.activation(small[:, 628:629], epsc[:, 0:1], ACT.Sqrt)

            def norm_add(eng, n0, k, sqb, acc):
                eng.wait_ge(s_sq, n0 * KD + k + 1)
                if k:
                    eng.wait_ge(s_sqd, n0 * KD + k)
                    eng.tensor_tensor(acc, acc, sqb[:, k % 2, :], ALU.add).then_inc(s_sqd, 1)
                else:
                    eng.tensor_copy(acc, sqb[:, 0, :]).then_inc(s_sqd, 1)

            def norm_mean(eng, n0, acc):
                eng.wait_ge(s_sqd, (n0 + 1) * KD)
                for i in range(NT):
                    last = nc.tensor.matmul(B[7][:, i:i + 1], acc[:, i * P:(i + 1) * P], ones_mean[:, 0:1],
                                            start=True, stop=True)
                last.then_inc(s_nm, 1)

            def norm_root(eng, n0):
                eng.wait_ge(s_nm, n0 + 1)
                eng.activation(rs4, B[7][:, 0:NT], ACT.Sqrt, bias=epsc[:, 0:1]).then_inc(s_rt, 1)

            def norm_spread(eng, n0):
                eng.wait_ge(s_rr, n0 + 1)
                for i in range(NT):
                    last = nc.tensor.transpose(B[4][:, i * P:(i + 1) * P],
                                               rs4[:, i:i + 1].to_broadcast([P, P]), ident[:, :])
                last.then_inc(s_rb, 1)

            def norm_scale(eng, n0, gain):
                eng.wait_ge(s_rt, n0 + 1)
                eng.reciprocal(rs4, rs4).then_inc(s_rr, 1)
                eng.wait_ge(s_rb, n0 + 1)
                for k in range(KD):
                    eng.scalar_tensor_tensor(out=hT[:, k, :], in0=xT[:, k, :], scalar=col(gain, k), in1=B[4][:, :],
                                             op0=ALU.mult, op1=ALU.mult).then_inc(s_h, 1)

            def head_sums(bank, j, src, weight):
                return nc.tensor.matmul(bank[:, 2 * j:2 * j + 2], src, weight.rearrange("p (e n) -> p e n", e=2)
                                        [:, :, 0], start=True, stop=True)

            def head_spread(out, src):
                for e in range(2):
                    last = nc.tensor.matmul(out[RN * e:RN * (e + 1), :], src[:, e:e + 1].to_broadcast([P, RN]),
                                            ident[:, :], start=True, stop=True)
                return last

            s_win = [sem(f"w_in_loaded{c}") for c in range(6)]
            s_col = sem("columns_loaded")
            s_pj, s_pad, s_sh = sem("proj_done"), sem("proj_copied"), sem("proj_shifted")
            nrm_sq = arena[:, 8704:9728].rearrange("p (a t) -> p a t", a=2)
            nrm_acc = arena[:, 9728:10240]
            shd = nrm_acc
            ins_units = [ring[:, c, 0:KD * w].rearrange("p (k n) -> p k n", k=KD) for c, (_, w) in
                         enumerate(UNIT_COLS)]
            dest = {12: lora, 13: gd, 14: t14, 15: cq2, 16: ckv, 17: uT[:, 0, :], 18: uT[:, 1, :]}
            for c in range(RC):
                dest[c], dest[4 + c], dest[8 + c] = rT[:, c, :], kT[:, c, :], vT[:, c, :]
            NPAR = 7

            with nc.Block() as block:
                @block.sync
                def _(eng):
                    eng.dma_start(colp[:, :], colp_d[lay].rearrange("a p n -> p (a n)")).then_inc(s_col, 16)
                    for c in (3, 1, 0, 2, 4, 5):
                        c0, w = UNIT_COLS[c]
                        eng.dma_start(ins_units[c], w_in_d[lay, :, c0:c0 + w].rearrange("a (k p) n -> p (a k) n", p=P)
                                      ).then_inc(s_win[c], 16)
                    eng.dma_start(lora_w[:, :], lora_d[lay].rearrange("a p n -> p (a n)")).then_inc(s_par, 16)
                    eng.dma_start(gup_w[:, :], gup_d[lay].rearrange("a p n -> p (a n)")).then_inc(s_par, 16)
                    eng.dma_start(gup2_w[:, :], gup2_d[lay].rearrange("a p n -> p (a n)")).then_inc(s_par, 16)
                    eng.dma_start(wuq[:, :, :], wuq_d[lay].rearrange("a p k n -> p (a k) n")).then_inc(s_par, 16)
                    eng.dma_start(wukv[:, :], wukv_d[lay].rearrange("a p n -> p (a n)")).then_inc(s_par, 16)
                    eng.dma_start(wr[:, :, :], wr_d[lay].rearrange("a p k n -> p (a k) n")).then_inc(s_par, 16)
                    eng.dma_start(brb[:, :], br_d[lay].broadcast_to([P, NG + NE])).then_inc(s_par, 16)
                    eng.wait_ge(s_par, 16 * NPAR)

                @block.gpsimd
                def _(eng):
                    eng.memset(shp[:, :, 0:1], 0.0).then_inc(s_gp, 1)
                    gch.n += 1

                @block.scalar
                def _(eng):
                    norm_squares(eng, 0, nrm_sq)
                    norm_root(eng, 0)
                    for n, j in enumerate(TILE_ORDER):
                        c0, w, unit, shifted = TILE[j]
                        eng.wait_ge(s_pj, n + 1)
                        if shifted:
                            m = sum(TILE[x][3] for x in TILE_ORDER[:n])
                            if m >= 2:
                                eng.wait_ge(s_sh, m - 1)
                            eng.activation(shp[:, m % 2, 1:SEQ + 1], B[n % 4][:, :], ACT.Copy).then_inc(s_pad, 1)
                        else:
                            eng.activation(dest[j][0:w, :], B[n % 4][0:w, :], ACT.Copy).then_inc(s_pad, 1)
                    n0 = len(TILE_ORDER)
                    eng.wait_ge(s_sh, 15)
                    for i in range(NT):
                        eng.wait_ge(s_pj, n0 + i + 1)
                        eng.activation(gv[:, i, :], B[(n0 + i) % 4][:, 0:256], ACT.Copy)
                        eng.activation(kr[:, i, :], B[(n0 + i) % 4][:, 256:288], ACT.Copy).then_inc(s_pad, 1)

                @block.vector
                def _(eng):
                    v = vch.on(eng)
                    eng.wait_ge(s_col, 16)
                    for k in range(KD):
                        norm_add(eng, 0, k, nrm_sq, nrm_acc)
                    norm_scale(eng, 0, "g_mix")
                    eng.wait_ge(s_gp, 1)
                    m = 0
                    for n, j in enumerate(TILE_ORDER):
                        if not TILE[j][3]:
                            continue
                        eng.wait_ge(s_pad, n + 1)
                        v(eng.tensor_tensor(shd[:, :], shp[:, m % 2, 0:SEQ], shp[:, m % 2, 1:SEQ + 1],
                                            ALU.subtract))
                        eng.scalar_tensor_tensor(out=dest[j], in0=shd[:, :], scalar=col("mu", j),
                                                 in1=shp[:, m % 2, 1:SEQ + 1], op0=ALU.mult,
                                                 op1=ALU.add).then_inc(s_sh, 1)
                        m += 1
                        eng.wait_ge(s_sh, m)

                @block.tensor
                def _(eng):
                    norm_mean(eng, 0, nrm_acc)
                    norm_spread(eng, 0)
                    for n, j in enumerate(TILE_ORDER):
                        c0, w, unit, _s = TILE[j]
                        u0 = c0 - UNIT_COLS[unit][0]
                        eng.wait_ge(s_win[unit], 16)
                        if n >= 4:
                            eng.wait_ge(s_pad, n - 3)
                        for k in range(KD):
                            if n == 0:
                                eng.wait_ge(s_h, k + 1)
                            last = nc.tensor.matmul(B[n % 4][0:w, :], ins_units[unit][:, k, u0:u0 + w], hT[:, k, :],
                                                    start=k == 0, stop=k == KD - 1)
                        last.then_inc(s_pj, 1)
                    n0 = len(TILE_ORDER)
                    eng.wait_ge(s_win[5], 16)
                    for i in range(NT):
                        n = n0 + i
                        eng.wait_ge(s_pad, n - 3)
                        for o, w, unit, u0 in ((256, 32, 4, KR_COL - UNIT_COLS[4][0]), (0, 256, 5, 0)):
                            for k in range(KD):
                                last = nc.tensor.matmul(B[n % 4][:, o:o + w], hT[:, k, i * P:(i + 1) * P],
                                                        ins_units[unit][:, k, u0:u0 + w], start=k == 0,
                                                        stop=k == KD - 1)
                        last.then_inc(s_pj, 1)

            X1, X2, X3, X4, X5, X6 = [fours(ring_view(i // 2, 2048 * (i % 2), 2048)) for i in range(6)]
            AT = fours(hT[:, 4:8, :].rearrange("p c t -> p (c t)"))
            BT = fours(ring_view(5, 0, 2048))
            bonus = fours(hT[:, 0:4, :].rearrange("p c t -> p (c t)"))
            mid = small[:, 0:16].rearrange("p (c n) -> p c n", c=RC)
            lastr = small[:, 16:32].rearrange("p (c n) -> p c n", c=RC)
            fexp = small[:, 32:44].rearrange("p (c n) -> p c n", c=RC)
            sg2 = small[0:32, 64:576]
            s_b1, s_b2, s_b3 = sem("kk_squared"), sem("kk_summed"), sem("kk_floored")
            s_b4, s_b5 = sem("kk_root"), sem("lora_tanh")
            s_b6, s_b7, s_b8 = sem("kk_factors"), sem("kk_factors_spread"), sem("gate_tanh")
            hf = small[:, 576:608]
            s_wp, s_ap, s_th, s_ta = sem("decay_lora"), sem("a_lora"), sem("decay_tanh"), sem("a_tanh")
            s_cr, s_ex, s_bp, s_bs, s_el = (sem("cum_ready"), sem("decay_exps"), sem("bonus_product"),
                                            sem("bonus_summed"), sem("elementwise_done"))

            def flat(ap):
                return ap.rearrange("p c t -> p (c t)")

            def chunks(ap):
                return ap.rearrange("p c (n t) -> p (c n) t", t=P)

            with nc.Block() as block:
                @block.scalar
                def _(eng):
                    a = ach.on(eng)
                    eng.activation(half0[:, 0:8], colp[:, COLS["w0"]:COLS["w0"] + 8], ACT.Copy, scale=0.5)
                    a(eng.activation(lora[0:64, :], lora[0:64, :], ACT.Tanh))
                    eng.sem_inc(s_b5, 1)
                    for c in range(RC):
                        eng.wait_ge(s_ap, c + 1)
                        eng.activation(X4[:, c, :], B[c][:, :], ACT.Tanh, scale=0.5,
                                       bias=half0[:, 4 + c:5 + c]).then_inc(s_ta, 1)
                    for c in range(RC):
                        eng.wait_ge(s_wp, c + 1)
                        eng.activation(X3[:, c, :], B[4 + c][:, :], ACT.Tanh, scale=0.5,
                                       bias=half0[:, c:c + 1]).then_inc(s_th, 1)
                    eng.wait_ge(s_b1, 4)
                    a(eng.activation(flat(X2), flat(X1), ACT.Square))
                    eng.sem_inc(s_b2, 1)
                    eng.activation(gd, gd, ACT.Tanh, scale=0.5)
                    a(eng.activation(sg2, t14[0:32, :], ACT.Tanh, scale=0.5))
                    eng.sem_inc(s_b8, 1)
                    eng.wait_ge(s_b3, 1)
                    eng.activation(hf, hf, ACT.Sqrt).then_inc(s_b4, 1)
                    eng.wait_ge(s_cr, 1)
                    eng.activation(flat(X6), flat(X6), ACT.Exp).then_inc(s_ex, 1)
                    eng.activation(flat(X3), flat(X5), ACT.Exp).then_inc(s_ex, 1)
                    eng.activation(fexp, fexp, ACT.Exp).then_inc(s_ex, 1)
                    eng.wait_ge(s_cr, 2)
                    eng.activation(flat(X2), flat(X5), ACT.Exp, scale=-1.0).then_inc(s_ex, 1)

                @block.vector
                def _(eng):
                    v = vch.on(eng)
                    for c in range(RC):
                        eng.tensor_scalar(X1[:, c, :], kT[:, c, :], col("k_k", c), None, ALU.mult).then_inc(s_b1, 1)
                    v(eng.tensor_scalar(half0[:, 8:12], colp[:, COLS["k_a"]:COLS["k_a"] + 4], -1.0, 1.0,
                                        ALU.mult, ALU.add))
                    eng.wait_ge(s_th, 4)
                    v(eng.tensor_scalar(flat(X3), flat(X3), -HALF_DECAY, -HALF_DECAY, ALU.mult, ALU.add))
                    for c in range(RC):
                        last = eng.tensor_tensor_scan(X5[:, c, :], scan_keep[:, :], X3[:, c, :], 0.0,
                                                      ALU.mult, ALU.add)
                    v(last)
                    eng.wait_ge(s_bs, 1)
                    eng.tensor_scalar(hf, B[0][:, 0:32], 1e-24, None, ALU.max).then_inc(s_b3, 1)
                    cum = X5.rearrange("p c (n t) -> p c n t", t=P)
                    v(eng.tensor_copy(mid, cum[:, :, :, P // 2 - 1]))
                    v(eng.tensor_tensor(chunks(X5), chunks(X5),
                                        small[:, 0:16].unsqueeze(2).to_broadcast([P, 16, P]), ALU.subtract))
                    v(eng.tensor_copy(lastr, cum[:, :, :, P - 1]))
                    v(eng.tensor_tensor(fexp, lastr[:, :, 0:3], mid[:, :, 1:4], ALU.add))
                    eng.tensor_tensor(flat(X6), flat(X5), flat(X3), ALU.subtract).then_inc(s_cr, 1)
                    eng.wait_ge(s_ta, 4)
                    v(eng.tensor_scalar(flat(X4), flat(X4), 0.5, 0.5, ALU.mult, ALU.add))
                    eng.wait_ge(s_b4, 1)
                    eng.reciprocal(hf, hf).then_inc(s_b6, 1)
                    eng.wait_ge(s_b8, 1)
                    v(eng.tensor_scalar(gd, gd, 0.5, 0.5, ALU.mult, ALU.add))
                    v(eng.tensor_scalar(sg2, sg2, 0.5, 0.5, ALU.mult, ALU.add))
                    for c in range(RC):
                        eng.wait_ge(s_b7, c + 1)
                        last = eng.tensor_tensor(X1[:, c, :], X1[:, c, :], B[c][:, :], ALU.mult)
                    last.then_inc(s_cr, 1)
                    eng.wait_ge(s_cr, 2)
                    eng.wait_ge(s_ex, 1)
                    v(eng.scalar_tensor_tensor(out=flat(AT), in0=flat(X1), scalar=-1.0, in1=flat(X6),
                                               op0=ALU.mult, op1=ALU.mult))
                    v(eng.tensor_tensor(flat(X1), flat(X1), flat(X4), ALU.mult))
                    for c in range(RC):
                        last = eng.tensor_scalar(X6[:, c, :], X4[:, c, :], col("k_a", c), half0[:, 8 + c:9 + c],
                                                 ALU.mult, ALU.add)
                    v(last)
                    v(eng.tensor_tensor(flat(kT), flat(kT), flat(X6), ALU.mult))
                    for c in range(RC):
                        eng.scalar_tensor_tensor(out=X4[:, c, :], in0=rT[:, c, :], scalar=col("r_k", c),
                                                 in1=kT[:, c, :], op0=ALU.mult, op1=ALU.mult).then_inc(s_bp, 1)
                    eng.wait_ge(s_ex, 4)
                    eng.wait_ge(s_bp, 4)
                    v(eng.tensor_tensor(flat(BT), flat(X1), flat(X2), ALU.mult))
                    v(eng.tensor_tensor(flat(kT), flat(kT), flat(X2), ALU.mult))
                    v(eng.tensor_tensor(flat(rT), flat(rT), flat(X3), ALU.mult))
                    for c in range(RC):
                        eng.wait_ge(s_bs, 2 + c)
                        v(eng.tensor_tensor(bonus[:, c, :], B[4 + c][:, :], vT[:, c, :], ALU.mult))

                @block.tensor
                def _(eng):
                    for c in range(RC):
                        nc.tensor.matmul(B[c][:, :], lora_w[64:128, c * P:(c + 1) * P], lora[64:128, :], start=True,
                                         stop=True).then_inc(s_ap, 1)
                    eng.wait_ge(s_b5, 1)
                    for c in range(RC):
                        nc.tensor.matmul(B[4 + c][:, :], lora_w[0:64, c * P:(c + 1) * P], lora[0:64, :], start=True,
                                         stop=True).then_inc(s_wp, 1)
                    eng.wait_ge(s_b2, 1)
                    eng.wait_ge(s_ta, 4)
                    for c in range(RC):
                        for i in range(NT):
                            last = head_sums(B[0], 4 * c + i, X2[:, c, i * P:(i + 1) * P], head_sum)
                    last.then_inc(s_bs, 1)
                    eng.wait_ge(s_b6, 1)
                    for c in range(RC):
                        for i in range(NT):
                            j = 2 * (4 * c + i)
                            last = head_spread(B[c][:, i * P:(i + 1) * P], hf[:, j:j + 2])
                        last.then_inc(s_b7, 1)
                    for c in range(RC):
                        eng.wait_ge(s_bp, c + 1)
                        nc.tensor.matmul(B[4 + c][:, :], head_sum[:, :], X4[:, c, :], start=True,
                                         stop=True).then_inc(s_bs, 1)

            big = [ring[:, n, :].rearrange("p (h m t) -> p h m t", h=RH, m=4) for n in range(2)]
            XL = [ring_view(2, 1024 * n, 1024).rearrange("p (h t) -> p h t", h=RH) for n in range(2)]
            XU = [ring_view(2, 2048 + 1024 * n, 1024).rearrange("p (h t) -> p h t", h=RH) for n in range(2)]
            Vt, Bt, Kt = [[ring_view(3, 512 * (3 * n + q), 512) for n in range(2)] for q in range(3)]
            T1 = [ring_view(4, 1280 + 1024 * n, 1024).rearrange("p (h t) -> p h t", h=RH) for n in range(2)]
            Wm = [ring_view(4 - n, 3584 * n, 512).rearrange("p (h t) -> p h t", h=RH) for n in range(2)]
            Um = ring_view(4, 512, 512).rearrange("p (h t) -> p h t", h=RH)
            Stmp = ring_view(4, 1024, 256).rearrange("p (c t) -> p c t", c=RC)
            STb = [ring_view(4 - n, 3328 - 256 * n, 512).rearrange("p (c t) -> p c t", c=RC) for n in range(2)]
            s_bz, s_wb, s_kv = sem("state_blocks_zeroed"), sem("tril_ak_v"), sem("state_kv")
            s_wbc = sem("tril_ak_v_copied")
            s_tr, s_tc = sem("chunk_transposed"), sem("chunk_copied")
            s_g4, s_gm = sem("products_done"), sem("products_masked")
            s_x0, s_xt, s_xc = sem("inverse_start"), sem("inverse_flipped"), sem("inverse_flip_copied")
            s_t1, s_tm, s_u1, s_xa = sem("level_a"), sem("level_a_masked"), sem("level_b"), sem("level_added")
            s_w, s_wc, s_u, s_uc = sem("w_done"), sem("w_copied"), sem("u_done"), sem("u_copied")
            s_y, s_yc, s_st, s_stc = sem("y_done"), sem("y_copied"), sem("state_done"), sem("state_kept")

            def odd4(ap, L):
                return ap.rearrange("p h (a two j) -> p h a two j", two=2, j=2 << L)[:, :, :, 1, :]

            def four(ap):
                return ap.rearrange("p (h t) -> p h t", h=4)

            def quarter(ap, q):
                return ap[q // 2][:, 4 * (q % 2):4 * (q % 2) + 4, :]

            def level_rows(L):
                return slice(0, 64) if L == 5 else slice(0, P)

            with nc.Block() as block:
                @block.tensor
                def _(eng):
                    def outputs(n):
                        s, tok = n % 2, slice(n * P, (n + 1) * P)
                        for c in range(RC):
                            o = slice(c * P, (c + 1) * P)
                            if n:
                                nc.tensor.matmul(B[6 + s][:, o], STb[s][:, c, :], rT[:, c, tok], start=True,
                                                 stop=False)
                            for m, Z in ((3, fours(Vt[s])), (2, fours(flat(Um)))):
                                for e in range(2):
                                    rows = slice(64 * e, 64 * e + 64)
                                    last = nc.tensor.matmul(B[6 + s][rows, o], Z[:, c, rows],
                                                            big[s][:, 2 * c + e, m, :], start=n == 0 and m == 3,
                                                            stop=m == 2)
                        last.then_inc(s_y, 1)

                    for n0 in (0, 2):
                        flips, levels = 24 * (n0 // 2), 24 * (n0 // 2)

                        for s in range(2):
                            n = n0 + s
                            tok = slice(n * P, (n + 1) * P)
                            for q, src in enumerate((vT, BT, kT)):
                                i = 3 * n + q
                                if i >= 2:
                                    eng.wait_ge(s_tc, i - 1)
                                if n0 and q == 0 and s == 0:
                                    eng.wait_ge(s_wbc, 2)
                                    eng.wait_ge(s_stc, 2)
                                for c in range(RC):
                                    last = nc.tensor.transpose(B[i % 2][:, c * P:(c + 1) * P], src[:, c, tok],
                                                               ident[:, :])
                                last.then_inc(s_tr, 1)
                            for h in range(RH):
                                g = RH * n + h
                                rows = slice(64 * (h % 2), 64 * (h % 2) + 64)
                                if g >= 4:
                                    eng.wait_ge(s_gm, g - 3)
                                bank = B[2 + g % 4]
                                a_, b_ = AT[rows, h // 2, tok], BT[rows, h // 2, tok]
                                k_, r_ = kT[rows, h // 2, tok], rT[rows, h // 2, tok]
                                for m, (lt, rt) in enumerate(((a_, b_), (k_, a_), (b_, r_), (k_, r_))):
                                    last = nc.tensor.matmul(bank[:, m * P:(m + 1) * P], lt, rt, start=True, stop=True)
                                last.then_inc(s_g4, 1)
                        eng.wait_ge(s_x0, n0 + 2)
                        if n0:
                            eng.wait_ge(s_yc, 2)
                        for q in range(4):
                            for h in range(4):
                                last = nc.tensor.transpose(B[4 + (q + 2) % 4][:, h * P:(h + 1) * P],
                                                           quarter(XL, q)[:, h, :], ident[:, :])
                            last.then_inc(s_xt, 1)
                        eng.wait_ge(s_tc, 3 * n0 + 6)
                        for L in range(6):
                            m = level_rows(L)
                            for q in range(4):
                                if L:
                                    eng.wait_ge(s_xa, levels + 4 * (L - 1) + q + 1)
                                    for h in range(4):
                                        last = nc.tensor.transpose(B[4 + q][:, h * P:(h + 1) * P],
                                                                   quarter(XU, q)[:, h, :], ident[:, :])
                                    last.then_inc(s_xt, 1)
                                else:
                                    eng.wait_ge(s_xc, flips + q + 1)
                                for h in range(4):
                                    last = nc.tensor.matmul(B[q][m, h * P:(h + 1) * P],
                                                            big[q // 2][:, 4 * (q % 2) + h, 0, m],
                                                            quarter(XU, q)[:, h, :], start=True, stop=True)
                                last.then_inc(s_t1, 1)
                            for q in range(4):
                                eng.wait_ge(s_tm, levels + 4 * L + q + 1)
                                eng.wait_ge(s_xc, flips + 4 * max(L, 1) + (q + 1 if L else 0))
                                for h in range(4):
                                    last = nc.tensor.matmul(B[4 + q][m, h * P:(h + 1) * P],
                                                            quarter(XL, q)[m, h, m],
                                                            quarter(T1, q)[m, h, :], start=True, stop=True)
                                last.then_inc(s_u1, 1)
                        for s in range(2):
                            for h in range(RH):
                                last = nc.tensor.matmul(B[s][:, h * 64:(h + 1) * 64], big[s][:, h, 1, :],
                                                        Vt[s][:, h * 64:(h + 1) * 64], start=True, stop=True)
                            last.then_inc(s_wb, 1)
                        for s in range(2):
                            n = n0 + s
                            tok = slice(n * P, (n + 1) * P)
                            eng.wait_ge(s_xa, levels + 20 + 2 * (s + 1))
                            if n:
                                eng.wait_ge(s_stc, n)
                                for c in range(RC):
                                    last = nc.tensor.matmul(B[4][:, c * P:(c + 1) * P], AT[:, c, tok],
                                                            STb[n % 2][:, c, :], start=True, stop=True)
                                last.then_inc(s_w, 1)
                            if s:
                                outputs(n - 1)
                            if n < NT - 1:
                                for h in range(RH):
                                    rows = slice(64 * (h % 2), 64 * (h % 2) + 64)
                                    hs = slice(h * 64, (h + 1) * 64)
                                    last = nc.tensor.matmul(B[5][rows, (h // 2) * 64:(h // 2) * 64 + 64],
                                                            Kt[s][:, hs], Vt[s][:, hs], start=True, stop=True)
                                last.then_inc(s_kv, 1)
                            if n:
                                eng.wait_ge(s_wc, n)
                            else:
                                eng.wait_ge(s_wbc, 1)
                            for h in range(RH):
                                last = nc.tensor.matmul(B[2][:, h * 64:(h + 1) * 64], XU[s][:, h, :], Wm[s][:, h, :],
                                                        start=True, stop=True)
                            last.then_inc(s_u, 1)
                            eng.wait_ge(s_uc, n + 1)
                            if n < NT - 1:
                                for h in range(RH):
                                    rows = slice(64 * (h % 2), 64 * (h % 2) + 64)
                                    last = nc.tensor.matmul(B[3][rows, (h // 2) * 64:(h // 2) * 64 + 64],
                                                            Bt[s][:, h * 64:(h + 1) * 64], Um[:, h, :], start=True,
                                                            stop=True)
                                last.then_inc(s_st, 1)
                        outputs(n0 + 1)

                @block.gpsimd
                def _(eng):
                    eng.memset(STb[0], 0.0).then_inc(s_bz, 1)
                    eng.memset(STb[1], 0.0).then_inc(s_bz, 1)

                @block.scalar
                def _(eng):
                    for n0 in (0, 2):
                        if n0:
                            eng.wait_ge(s_y, n0)
                        for i in range(3 * n0, 3 * n0 + 6):
                            dst = (Vt, Bt, Kt)[i % 3][(i // 3) % 2]
                            eng.wait_ge(s_tr, i + 1)
                            eng.activation(dst, B[i % 2][:, :], ACT.Copy).then_inc(s_tc, 1)
                        for q in range(4):
                            eng.wait_ge(s_xt, 12 * n0 + q + 1)
                            eng.activation(quarter(XU, q), four(B[4 + (q + 2) % 4][:, :]),
                                           ACT.Copy).then_inc(s_xc, 1)
                        for L in range(1, 6):
                            for q in range(4):
                                eng.wait_ge(s_xt, 12 * n0 + 4 * L + q + 1)
                                eng.activation(quarter(XL, q), four(B[4 + q][:, :]), ACT.Copy).then_inc(s_xc, 1)
                        for s in range(2):
                            eng.wait_ge(s_wb, n0 + s + 1)
                            eng.activation(flat(Wm[s]), B[s][:, :], ACT.Copy).then_inc(s_wbc, 1)
                        for s in range(2):
                            n = n0 + s
                            eng.wait_ge(s_u, n + 1)
                            eng.activation(flat(Um), B[2][:, :], ACT.Copy).then_inc(s_uc, 1)
                            if s:
                                eng.wait_ge(s_y, n)
                                eng.activation(rT[:, :, (n - 1) * P:n * P], fours(B[6][:, :]),
                                               ACT.Copy).then_inc(s_yc, 1)
                        eng.wait_ge(s_y, n0 + 2)
                        eng.activation(rT[:, :, (n0 + 1) * P:(n0 + 2) * P], fours(B[7][:, :]),
                                       ACT.Copy).then_inc(s_yc, 1)

                @block.vector
                def _(eng):
                    v = vch.on(eng)
                    k = 0
                    for n0 in (0, 2):
                        if n0:
                            eng.wait_ge(s_y, n0)
                        for s in range(2):
                            n = n0 + s
                            for h in range(RH):
                                g = RH * n + h
                                eng.wait_ge(s_g4, g + 1)
                                eng.tensor_tensor(big[s][:, h, :, :],
                                                  B[2 + g % 4][:, :].rearrange("p (m t) -> p m t", m=4),
                                                  mask4[:, :, :], ALU.mult).then_inc(s_gm, 1)
                            eng.wait_ge(s_gm, RH * (n + 1))
                            v(eng.tensor_tensor(XL[s], big[s][:, :, 0, :],
                                                pair1[:, :].unsqueeze(1).to_broadcast([P, RH, P]), ALU.mult))
                            eng.tensor_tensor(XL[s], XL[s], ident[:, :].unsqueeze(1).to_broadcast([P, RH, P]),
                                              ALU.add).then_inc(s_x0, 1)
                        for L in range(6):
                            m = level_rows(L)
                            shape = [m.stop, 4, 32 >> L, 2 << L]
                            for q in range(4):
                                k += 1
                                eng.wait_ge(s_t1, k)
                                eng.tensor_tensor(odd4(quarter(T1, q)[m], L), odd4(four(B[q][m, :]), L),
                                                  lvl[m, L, :].rearrange("p (a j) -> p a j", j=2 << L)
                                                  .unsqueeze(1).to_broadcast(shape), ALU.mult).then_inc(s_tm, 1)
                            for q in range(4):
                                eng.wait_ge(s_u1, k - 3 + q)
                                x = odd4(quarter(XU, q)[m], L)
                                eng.tensor_tensor(x, odd4(four(B[4 + q][m, :]), L), x, ALU.add).then_inc(s_xa, 1)
                        for s in range(2):
                            n = n0 + s
                            if n:
                                eng.wait_ge(s_w, n)
                                eng.wait_ge(s_wbc, n + 1)
                                eng.tensor_tensor(flat(Wm[s]), B[4][:, :], flat(Wm[s]), ALU.add).then_inc(s_wc, 1)
                            if n == NT - 1:
                                continue
                            eng.wait_ge(s_kv, n + 1)
                            kv, bu = [B[b][:, 0:256].rearrange("p (c t) -> p c t", c=RC) for b in (5, 3)]
                            if n:
                                v(eng.tensor_tensor(Stmp, kv, ST[:, :, :], ALU.add))
                            else:
                                v(eng.tensor_copy(Stmp, kv))
                                eng.wait_ge(s_bz, 2)
                            eng.wait_ge(s_st, n + 1)
                            v(eng.tensor_tensor(Stmp, bu, Stmp, ALU.add))
                            for e in range(2):
                                rows = slice(64 * e, 64 * e + 64)
                                last = eng.tensor_tensor(STb[(n + 1) % 2][rows, :, 64 * e:64 * e + 64], Stmp[rows],
                                                         fexp[rows, :, n:n + 1].to_broadcast([64, RC, RN]), ALU.mult)
                            last.then_inc(s_stc, 1)
                            if n < NT - 2:
                                v(eng.tensor_tensor(ST[:, :, :], Stmp,
                                                    fexp[:, :, n:n + 1].to_broadcast([P, RC, RN]), ALU.mult))

            s_gn1, s_gn2, s_gn3, s_gn4 = sem("gn_mean"), sem("gn_centred"), sem("gn_squared"), sem("gn_var")
            s_gn5, s_gn6, s_gg = sem("gn_root"), sem("gn_factors"), sem("gate_done")
            s_gn7 = sem("gn_factors_spread")
            with nc.Block() as block:
                @block.tensor
                def _(eng):
                    for c in range(RC):
                        nc.tensor.matmul(B[c][:, :], head_mean[:, :], rT[:, c, :], start=True,
                                         stop=True).then_inc(s_gn1, 1)
                    for c in range(RC):
                        eng.wait_ge(s_gn3, c + 1)
                        for i in range(NT):
                            last = head_sums(B[4], 4 * c + i, X1[:, c, i * P:(i + 1) * P], head_mean)
                    last.then_inc(s_gn4, 1)
                    eng.wait_ge(s_gn6, 1)
                    for c in range(RC):
                        for i in range(NT):
                            j = 2 * (4 * c + i)
                            last = head_spread(B[4 + c][:, i * P:(i + 1) * P], hf[:, j:j + 2])
                        last.then_inc(s_gn7, 1)
                        nc.tensor.matmul(B[c][:, :], gup_w[:, c * P:(c + 1) * P], gd, start=True, stop=False)
                        nc.tensor.matmul(B[c][:, :], gup2_w[:, c * P:(c + 1) * P], sg2, start=False,
                                         stop=True).then_inc(s_gg, 1)

                @block.scalar
                def _(eng):
                    for c in range(RC):
                        eng.wait_ge(s_gn2, c + 1)
                        eng.activation(X1[:, c, :], rT[:, c, :], ACT.Square).then_inc(s_gn3, 1)
                    eng.activation(small[:, 628:629], epsc[:, 0:1], ACT.Sqrt)
                    eng.wait_ge(s_gn4, 1)
                    eng.activation(hf, B[4][:, 0:32], ACT.Sqrt, bias=epsc[:, 1:2]).then_inc(s_gn5, 1)

                @block.vector
                def _(eng):
                    v = vch.on(eng)
                    for c in range(RC):
                        eng.wait_ge(s_gn1, c + 1)
                        eng.tensor_tensor(rT[:, c, :], rT[:, c, :], B[c][:, :], ALU.subtract).then_inc(s_gn2, 1)
                    for c in range(RC):
                        if c == 0:
                            eng.wait_ge(s_gn5, 1)
                            eng.reciprocal(hf, hf).then_inc(s_gn6, 1)
                        eng.wait_ge(s_gn7, c + 1)
                        v(eng.scalar_tensor_tensor(out=X2[:, c, :], in0=rT[:, c, :], scalar=col("ln_g", c),
                                                   in1=B[4 + c][:, :], op0=ALU.mult, op1=ALU.mult))
                        v(eng.scalar_tensor_tensor(out=X2[:, c, :], in0=X2[:, c, :], scalar=col("ln_b", c),
                                                   in1=bonus[:, c, :], op0=ALU.add, op1=ALU.add))
                        eng.wait_ge(s_gg, c + 1)
                        v(eng.tensor_tensor(hT[:, c, :], X2[:, c, :], B[c][:, :], ALU.mult))

            end_stage()
            q_sb = ring_view(0, 0, 1536).rearrange("p (i h n) -> p i h n", i=NT, h=HEADS)
            k_sb = ring_view(0, 1536, 1536).rearrange("p (i h n) -> p i h n", i=NT, h=HEADS)
            v_sb = ring_view(0, 3072, 1024).rearrange("p (i n) -> p i n", i=NT)
            qT = ring_view(1, 0, 2048).rearrange("p (h t) -> p h t", h=HEADS)
            kTm = ring_view(1, 2048, 2048).rearrange("p (h t) -> p h t", h=HEADS)
            PT = [ring_view(2, 2048 * z, 2048).rearrange("p (j q) -> p j q", j=NT) for z in range(2)]
            sq14, sq15, sqkv = arena[:, 0:512], arena[:, 512:1024], arena[:, 1024:1536]
            qk_sq = arena[:, 0:1536].rearrange("p (i n) -> p i n", n=QK)
            rope_t = [arena[:, 1536 + 256 * z:1792 + 256 * z].rearrange("p (i h n) -> p i h n", i=NT, h=HEADS)
                      for z in range(4)]
            rope_k = [arena[:, 2560 + 64 * z:2624 + 64 * z].rearrange("p (i n) -> p i n", i=NT) for z in range(4)]
            Pm = [arena[:, 2816 + 512 * z:3328 + 512 * z] for z in range(2)]
            gsq = arena[:, 3840:4864].rearrange("p (i n) -> p i n", n=RN)
            wsm = arena[:, 4864:5376].rearrange("p (g t) -> p g t", g=4)
            gtmp = arena[:, 5376:5888]
            gbb = arena[:, 5888:6144].rearrange("p (c t) -> p c t", c=2)
            lat = small[:, 0:12]
            qk_rs = small[:, 16:48]
            g_rs = small[:, 48:64]
            mx, sm = small[:, 64:80], small[:, 80:96]
            lat_w = small[:, 100:103]
            s_lw = sem("latent_weights")
            s_l0, s_l1, s_l2 = sem("latent_gained"), sem("latent_squares"), sem("latent_means")
            s_l3, s_l4, s_up, s_upc = sem("latent_root"), sem("latent_rs"), sem("mla_up"), sem("mla_up_copied")
            s_r0, s_r1, s_r2, s_r3 = sem("rope_done"), sem("qk_squares"), sem("qk_sums"), sem("qk_root")
            s_qn, s_qt, s_qc = sem("qk_normed"), sem("qk_transposed"), sem("qk_copied")
            s_sc, s_mx, s_ex2, s_pn = sem("scores"), sem("score_max"), sem("probs"), sem("probs_normed")
            s_pt, s_pc, s_pv, s_oc = sem("probs_transposed"), sem("probs_copied"), sem("pv_done"), sem("mla_out")
            s_ge, s_gs, s_gr, s_gq = sem("gelu"), sem("gmlp_sums"), sem("gmlp_root"), sem("gmlp_squares")
            s_gn, s_sp, s_ws = sem("gmlp_normed"), sem("gmlp_mixed"), sem("gmlp_weights")
            s_gw, s_gb = sem("gmlp_w_loaded"), sem("gmlp_b_loaded")
            w_out = ring[:, 3:5, :].rearrange("p u (k n) -> p (u k) n", k=4)
            wmq = ring_view(5, 0, 2048).rearrange("p (k n) -> p k n", k=KD)
            wmo = ring_view(5, 2048, 2048).rearrange("p (k n) -> p k n", k=2)
            SC = float(QK) ** -0.5

            def copy_probs(eng, n):
                h, i = n // NT, n % NT
                eng.wait_ge(s_pt, n + 1)
                if i == 0 and h >= 2:
                    eng.wait_ge(s_pv, h - 1)
                eng.activation(PT[h % 2][:, 0:i + 1, i * P:(i + 1) * P],
                               B[2 + n % 2][:, 0:(i + 1) * P].rearrange("p (j q) -> p j q", q=P),
                               ACT.Copy).then_inc(s_pc, 1)

            def mla_out(eng, h):
                rows = slice(64 * (h % 2), 64 * (h % 2) + 64)
                eng.wait_ge(s_pv, h + 1)
                eng.activation(hT[rows, 4 + h // 2, :], B[4 + h % 2][rows, :], ACT.Copy).then_inc(s_oc, 1)

            def norm_probs(eng, v, n):
                w = (n % NT + 1) * P
                eng.wait_ge(s_ex2, n + 1)
                v(eng.reciprocal(sm[:, n:n + 1], sm[:, n:n + 1]))
                eng.tensor_scalar(Pm[n % 2][:, 0:w], Pm[n % 2][:, 0:w], sm[:, n:n + 1], None,
                                  ALU.mult).then_inc(s_pn, 1)

            def flip_probs(eng, n):
                eng.wait_ge(s_pn, n + 1)
                if n >= 2:
                    eng.wait_ge(s_pc, n - 1)
                for j in range(n % NT + 1):
                    last = nc.tensor.transpose(B[2 + n % 2][:, j * P:(j + 1) * P],
                                               Pm[n % 2][:, j * P:(j + 1) * P], ident[:, :])
                last.then_inc(s_pt, 1)

            def pv(eng, h):
                rows = slice(64 * (h % 2), 64 * (h % 2) + 64)
                eng.wait_ge(s_pc, NT * (h + 1))
                if h >= 2:
                    eng.wait_ge(s_oc, h - 1)
                for j in range(NT):
                    last = nc.tensor.matmul(B[4 + h % 2][rows, j * P:SEQ], v_sb[:, j, h * 64:(h + 1) * 64],
                                            PT[h % 2][:, j, j * P:SEQ], start=j == 0, stop=j == NT - 1)
                last.then_inc(s_pv, 1)

            with nc.Block() as block:
                @block.sync
                def _(eng):
                    eng.dma_start(wsm, wsT_d[lay].rearrange("a p g n -> p (a g) n")).then_inc(s_gw, 16)
                    for half in range(2):
                        for c in range(2):
                            eng.dma_start(gbb[64 * half:64 * half + 64, c, :],
                                          gb_d[lay, 2 * c + half, :].broadcast_to([64, P])).then_inc(s_gb, 16)
                    for z in range(2):
                        eng.dma_start(w_out[:, 4 * z:4 * z + 4, :],
                                      w_out_d[lay, 512 * z:512 * z + 512, :].rearrange("a (k p) n -> p (a k) n", p=P)
                                      ).then_inc(s_wo[z], 16)
                    eng.dma_start(wmq, wmq_d[lay].rearrange("a (k p) n -> p (a k) n", p=P)).then_inc(s_wm, 16)
                    eng.dma_start(wmo, wmo_d[lay].rearrange("a (k p) n -> p (a k) n", p=P)).then_inc(s_wm, 16)

                @block.gpsimd
                def _(eng):
                    g = gch.on(eng)
                    eng.memset(lat_w[:, 0:1], 1.0 / 192)
                    g(eng.memset(lat_w[:, 1:2], 1.0 / 192))
                    eng.memset(lat_w[0:32, 0:1], 0.0)
                    g(eng.memset(lat_w[:, 2:3], 1.0 / P))
                    eng.sem_inc(s_lw, 1)
                    eng.wait_ge(s_gw, 16)
                    eng.tensor_tensor(wsm, wsm, mask4[:, 2:3, :].to_broadcast([P, 4, P]),
                                      ALU.mult).then_inc(s_ws, 1)

                @block.scalar
                def _(eng):
                    a = ach.on(eng)
                    eng.activation(sq14, t14, ACT.Square).then_inc(s_l1, 1)
                    eng.activation(sq15[0:96, :], cq2[0:96, :], ACT.Square).then_inc(s_l1, 1)
                    eng.activation(sqkv, ckv, ACT.Square).then_inc(s_l1, 1)
                    eng.wait_ge(s_l2, 1)
                    eng.activation(lat[:, 0:8], B[0][:, 0:8], ACT.Sqrt, bias=epsc[:, 0:1]).then_inc(s_l3, 1)
                    for i in range(NT):
                        eng.wait_ge(s_up, i + 1)
                        eng.wait_ge(s_l4, 1)
                        eng.activation(q_sb[:, i, :, :], B[1 + i][:, 0:384].rearrange("p (h n) -> p h n", h=HEADS),
                                       ACT.Copy, scale=lat[:, 2 * i:2 * i + 1]).then_inc(s_upc, 1)
                    for i in range(NT):
                        eng.wait_ge(s_up, 4 + i + 1)
                        src = B[(5 + i) % 8][:, :].rearrange("p (h n) -> p h n", h=HEADS)
                        eng.activation(k_sb[:, i, :, 0:NOPE], src[:, :, 0:NOPE], ACT.Copy,
                                       scale=lat[:, 2 * i + 1:2 * i + 2])
                        eng.activation(v_sb[:, i, :].rearrange("p (h n) -> p h n", h=HEADS), src[:, :, NOPE:P],
                                       ACT.Copy, scale=lat[:, 2 * i + 1:2 * i + 2]).then_inc(s_upc, 1)
                    eng.activation(gv[:, :, :], gv[:, :, :], ACT.Gelu_apprx_tanh).then_inc(s_ge, 1)
                    eng.activation(uT[:, :, :], uT[:, :, :], ACT.Gelu_apprx_tanh).then_inc(s_ge, 1)
                    eng.wait_ge(s_ge, 2)
                    eng.activation(gsq, gv.rearrange("p i (g n) -> p (i g) n", n=RN), ACT.Square).then_inc(s_gq, 1)
                    for z, src in enumerate((q_sb, k_sb)):
                        eng.wait_ge(s_r0, z + 1)
                        if z:
                            eng.wait_ge(s_r2, 1)
                        eng.activation(qk_sq, src.rearrange("p i h n -> p (i h) n"), ACT.Square).then_inc(s_r1, 1)
                    eng.wait_ge(s_r2, 2)
                    a(eng.activation(qk_rs, qk_rs, ACT.Sqrt, scale=1.0 / QK, bias=epsc[:, 0:1]))
                    eng.wait_ge(s_gs, 1)
                    a(eng.activation(g_rs, g_rs, ACT.Sqrt, scale=1.0 / RN, bias=epsc[:, 0:1]))
                    eng.sem_inc(s_r3, 1)
                    for z in range(8):
                        eng.wait_ge(s_qt, z + 1)
                        dst = (qT if z < 4 else kTm)[0:QK, z % 4, :]
                        eng.activation(dst, B[z][0:QK, :], ACT.Copy,
                                       scale=col("q_g" if z < 4 else "k_g")[0:QK, :]).then_inc(s_qc, 1)
                    n = 0
                    for h in range(HEADS):
                        for i in range(NT):
                            w = (i + 1) * P
                            eng.wait_ge(s_mx, n + 1)
                            if n >= 2:
                                eng.wait_ge(s_pt, n - 1)
                            eng.activation(Pm[n % 2][:, 0:w], B[n % 2][:, 0:w], ACT.Exp, scale=SC,
                                           bias=mx[:, n:n + 1], accum_out=sm[:, n:n + 1]).then_inc(s_ex2, 1)
                            if n >= 1:
                                copy_probs(eng, n - 1)
                            n += 1
                        if h >= 1:
                            mla_out(eng, h - 1)
                    copy_probs(eng, n - 1)
                    mla_out(eng, HEADS - 1)

                @block.vector
                def _(eng):
                    v = vch.on(eng)
                    for z, (t, c) in enumerate(((t14, 0), (cq2, 1))):
                        n = P if z == 0 else 96
                        eng.wait_ge(s_l1, z + 1)
                        eng.tensor_scalar(t[0:n, :], t[0:n, :], col("cq_g", c)[0:n, :], None,
                                          ALU.mult).then_inc(s_l0, 1)
                    eng.wait_ge(s_l1, 3)
                    eng.tensor_scalar(ckv, ckv, col("ckv_g"), None, ALU.mult).then_inc(s_l0, 1)
                    eng.wait_ge(s_l3, 1)
                    eng.reciprocal(lat[:, 0:8], lat[:, 0:8]).then_inc(s_l4, 1)
                    cos_b = cosT[:, :, :].unsqueeze(2).to_broadcast([P, NT, HEADS, HALF])
                    sin_b = sinT[:, :, :].unsqueeze(2).to_broadcast([P, NT, HEADS, HALF])
                    k1, k2 = kr[:, :, 0:HALF], kr[:, :, HALF:2 * HALF]
                    for t, x, y in ((0, k1, cosT), (1, k2, sinT), (2, k2, cosT), (3, k1, sinT)):
                        last = eng.tensor_tensor(rope_k[t], x, y[:, :, :], ALU.mult)
                    v(last)
                    eng.tensor_tensor(k1, rope_k[0], rope_k[1], ALU.subtract)
                    v(eng.tensor_tensor(k2, rope_k[2], rope_k[3], ALU.add))
                    v(eng.tensor_copy(k_sb[:, :, :, NOPE:QK], kr[:, :, :].unsqueeze(2).to_broadcast(
                        [P, NT, HEADS, 2 * HALF])))
                    eng.wait_ge(s_upc, 4)
                    q1, q2 = q_sb[:, :, :, NOPE:NOPE + HALF], q_sb[:, :, :, NOPE + HALF:QK]
                    for t, x, y in ((0, q1, cos_b), (1, q2, sin_b), (2, q2, cos_b), (3, q1, sin_b)):
                        last = eng.tensor_tensor(rope_t[t], x, y, ALU.mult)
                    v(last)
                    eng.tensor_tensor(q1, rope_t[0], rope_t[1], ALU.subtract)
                    v(eng.tensor_tensor(q2, rope_t[2], rope_t[3], ALU.add))
                    eng.sem_inc(s_r0, 1)
                    eng.wait_ge(s_upc, 8)
                    eng.sem_inc(s_r0, 1)
                    eng.wait_ge(s_gq, 1)
                    v(eng.tensor_reduce(g_rs, gsq, AX, ALU.add))
                    eng.sem_inc(s_gs, 1)
                    for z in range(2):
                        eng.wait_ge(s_r1, z + 1)
                        v(eng.tensor_reduce(qk_rs[:, 16 * z:16 * z + 16], qk_sq, AX, ALU.add))
                        eng.sem_inc(s_r2, 1)
                    eng.wait_ge(s_r3, 1)
                    v(eng.reciprocal(qk_rs, qk_rs))
                    v(eng.reciprocal(g_rs, g_rs))
                    for z, t in enumerate((q_sb, k_sb)):
                        f = t.rearrange("p i h n -> p (i h) n")
                        eng.tensor_tensor(f, f, qk_rs[:, 16 * z:16 * z + 16].unsqueeze(2).to_broadcast(
                            [P, 16, QK]), ALU.mult).then_inc(s_qn, 1)
                    f = gv.rearrange("p i (g n) -> p (i g) n", n=RN)
                    eng.tensor_tensor(f, f, g_rs.unsqueeze(2).to_broadcast([P, 16, RN]), ALU.mult).then_inc(s_gn, 1)
                    n = 0
                    for h in range(HEADS):
                        for i in range(NT):
                            w = (i + 1) * P
                            eng.wait_ge(s_sc, n + 1)
                            v(eng.tensor_reduce(mx[:, n:n + 1], B[n % 2][:, 0:w], AX, ALU.max))
                            eng.tensor_scalar(mx[:, n:n + 1], mx[:, n:n + 1], -SC, None, ALU.mult).then_inc(s_mx, 1)
                            if n >= 1:
                                norm_probs(eng, v, n - 1)
                            n += 1
                    norm_probs(eng, v, n - 1)
                    eng.wait_ge(s_gb, 64)
                    for c in range(2):
                        eng.wait_ge(s_sp, c + 1)
                        v(eng.scalar_tensor_tensor(out=gtmp.rearrange("p (n t) -> p n t", t=P),
                                                   in0=B[6 + c][:, :].rearrange("p (n t) -> p n t", t=P),
                                                   scalar=col("gv_g", c),
                                                   in1=gbb[:, c:c + 1, :].to_broadcast([P, NT, P]),
                                                   op0=ALU.mult, op1=ALU.add))
                        v(eng.tensor_tensor(hT[:, 6 + c, :], gtmp, uT[:, c, :], ALU.mult))

                @block.tensor
                def _(eng):
                    eng.wait_ge(s_lw, 1)
                    eng.wait_ge(s_l1, 3)
                    for i in range(NT):
                        t = slice(i * P, (i + 1) * P)
                        nc.tensor.matmul(B[0][:, 2 * i:2 * i + 1], sq14[:, t], lat_w[:, 0:1], start=True, stop=False)
                        nc.tensor.matmul(B[0][:, 2 * i:2 * i + 1], sq15[0:96, t], lat_w[0:96, 1:2], start=False,
                                         stop=True)
                        last = nc.tensor.matmul(B[0][:, 2 * i + 1:2 * i + 2], sqkv[:, t], lat_w[:, 2:3], start=True,
                                                stop=True)
                    last.then_inc(s_l2, 1)
                    eng.wait_ge(s_l0, 3)
                    for i in range(NT):
                        t = slice(i * P, (i + 1) * P)
                        nc.tensor.matmul(B[1 + i][:, 0:384], t14[:, t], wuq[:, 0, :], start=True, stop=False)
                        nc.tensor.matmul(B[1 + i][:, 0:384], cq2[0:96, t], wuq[0:96, 1, :], start=False,
                                         stop=True).then_inc(s_up, 1)
                    eng.wait_ge(s_l3, 1)
                    for i in range(NT):
                        nc.tensor.matmul(B[(5 + i) % 8][:, :], ckv[:, i * P:(i + 1) * P], wukv[:, :], start=True,
                                         stop=True).then_inc(s_up, 1)
                    eng.wait_ge(s_upc, 8)
                    for z in range(8):
                        eng.wait_ge(s_qn, z // 4 + 1)
                        src = (q_sb, k_sb)[z // 4]
                        for i in range(NT):
                            last = nc.tensor.transpose(B[z][0:QK, i * P:(i + 1) * P], src[:, i, z % 4, :], ident[:, :])
                        last.then_inc(s_qt, 1)
                    eng.wait_ge(s_qc, 8)
                    eng.wait_ge(s_gn, 1)
                    eng.wait_ge(s_ws, 1)
                    for c in range(2):
                        for half in range(2):
                            g_ = 2 * c + half
                            for n in range(NT):
                                last = nc.tensor.matmul(B[6 + c][64 * half:64 * half + 64, n * P:(n + 1) * P],
                                                        gv[:, n, g_ * 64:(g_ + 1) * 64], wsm[:, g_, :], start=True,
                                                        stop=True)
                        last.then_inc(s_sp, 1)
                    n = 0
                    for h in range(HEADS):
                        for i in range(NT):
                            w = (i + 1) * P
                            if n >= 2:
                                eng.wait_ge(s_ex2, n - 1)
                            nc.tensor.matmul(B[n % 2][:, 0:w], qT[0:QK, h, i * P:w], kTm[0:QK, h, 0:w], start=True,
                                             stop=False)
                            nc.tensor.matmul(B[n % 2][:, w - P:w], ident[:, :], causal[:, :], start=False,
                                             stop=True).then_inc(s_sc, 1)
                            if n >= 2:
                                flip_probs(eng, n - 2)
                            n += 1
                        if h >= 1:
                            pv(eng, h - 1)
                    flip_probs(eng, n - 2)
                    flip_probs(eng, n - 1)
                    pv(eng, HEADS - 1)
            end_stage()
            nrm_sq = arena[:, 0:1024].rearrange("p (a t) -> p a t", a=2)
            nrm_acc = arena[:, 1024:1536]
            qx = arena[:, 1536:2560].rearrange("p (c t) -> p c t", c=2)
            qx_rs = arena[:, 2560:3584].rearrange("p (c t) -> p c t", c=2)
            Px = [arena[:, 3584 + 1024 * z:4608 + 1024 * z].rearrange("p (i m) -> p i m", i=NT) for z in range(2)]
            PXT = [arena[:, 5632 + 1024 * z:6656 + 1024 * z].rearrange("p (m q) -> p m q", m=2) for z in range(2)]
            oX = arena[:, 7680:8704].rearrange("p (c t) -> p c t", c=2)
            mxx, smx = small[:, 0:16], small[:, 16:32]
            xf = small[:, 32:48]
            s_o, s_or = sem("out_proj"), sem("out_added")
            s_q0, s_q1, s_q2, s_q3, s_q4 = (sem("xq_done"), sem("xq_squares"), sem("xq_mean"), sem("xq_root"),
                                            sem("xq_normed"))
            s_xs, s_xm, s_xe, s_xn = sem("x_scores"), sem("x_max"), sem("x_probs"), sem("x_probs_normed")
            s_q5, s_q6, s_q7 = sem("xq_factors"), sem("xq_factors_spread"), sem("xq_factors_copied")
            s_xf, s_xg, s_xv, s_xo = sem("x_flipped"), sem("x_flip_copied"), sem("x_pv"), sem("x_out")
            SCX = float(RN) ** -0.5
            w1v = [ring[:, 3 * u, :].rearrange("p (k n) -> p k n", k=KD) for u in range(2)]
            w3v = [ring[:, 3 * u + 1, :].rearrange("p (k n) -> p k n", k=KD) for u in range(2)]
            w2v = [ring[:, 3 * u + 2, :].rearrange("p (k n) -> p k n", k=HM) for u in range(2)]

            def expert_row(e):
                return bass.ds(layer * NE + e, 1)

            def load_up(eng, u, e, done):
                eng.dma_start(w1v[u], w1_d[expert_row(e)].rearrange("a (k p) n -> p (a k) n", p=P)).then_inc(done[0], 16)
                eng.dma_start(w3v[u], w3_d[expert_row(e)].rearrange("a (k p) n -> p (a k) n", p=P)).then_inc(done[1], 16)

            def load_down(eng, u, e, done):
                eng.dma_start(w2v[u], w2_d[expert_row(e)].rearrange("a (k p) n -> p (a k) n", p=P)).then_inc(done, 16)

            def flip_x(eng, h):
                eng.wait_ge(s_xn, h + 1)
                if h:
                    eng.wait_ge(s_xg, 2 * h)
                for m in range(2):
                    for i in range(NT):
                        last = nc.tensor.transpose(B[4 + m][:, i * P:(i + 1) * P],
                                                   Px[h % 2][:, i, m * P:(m + 1) * P], ident[:, :])
                    last.then_inc(s_xf, 1)

            def pv_x(eng, h):
                rows = slice(64 * (h % 2), 64 * (h % 2) + 64)
                eng.wait_ge(s_xg, 2 * (h + 1))
                if h >= 2:
                    eng.wait_ge(s_xo, h - 1)
                for m in range(2):
                    last = nc.tensor.matmul(B[6 + h % 2][rows, :], memV[:, m, h * 64:(h + 1) * 64],
                                            PXT[h % 2][:, m, :], start=m == 0, stop=m == 1)
                last.then_inc(s_xv, 1)

            def copy_x(eng, h):
                for m in range(2):
                    eng.wait_ge(s_xf, 2 * h + m + 1)
                    if h >= 2 and m == 0:
                        eng.wait_ge(s_xv, h - 1)
                    eng.activation(PXT[h % 2][:, m, :], B[4 + m][:, :], ACT.Copy).then_inc(s_xg, 1)

            def out_x(eng, h):
                rows = slice(64 * (h % 2), 64 * (h % 2) + 64)
                eng.wait_ge(s_xv, h + 1)
                eng.activation(oX[rows, h // 2, :], B[6 + h % 2][rows, :], ACT.Copy).then_inc(s_xo, 1)

            def norm_x(eng, v, h):
                eng.wait_ge(s_xe, 4 * (h + 1))
                v(eng.reciprocal(smx[:, 4 * h:4 * h + 4], smx[:, 4 * h:4 * h + 4]))
                eng.tensor_tensor(Px[h % 2], Px[h % 2],
                                  smx[:, 4 * h:4 * h + 4].unsqueeze(2).to_broadcast([P, NT, MEM]),
                                  ALU.mult).then_inc(s_xn, 1)

            with nc.Block() as block:
                @block.sync
                def _(eng):
                    load_up(eng, 0, 0, s_e[0:2])
                    load_down(eng, 0, 0, s_e[2])

                @block.tensor
                def _(eng):
                    for z in range(2):
                        eng.wait_ge(s_wo[z], 16)
                    for c in range(KD):
                        if c >= 4:
                            eng.wait_ge(s_or, c - 3)
                        for k in range(KD):
                            last = nc.tensor.matmul(B[c % 4][:, :], w_out[:, k, c * P:(c + 1) * P], hT[:, k, :],
                                                    start=k == 0, stop=k == KD - 1)
                        last.then_inc(s_o, 1)
                    norm_mean(eng, 1, nrm_acc)
                    norm_spread(eng, 1)
                    eng.wait_ge(s_wm, 32)
                    for c in range(2):
                        for k in range(KD):
                            if c == 0:
                                eng.wait_ge(s_h, KD + k + 1)
                            last = nc.tensor.matmul(B[c][:, :], wmq[:, k, c * P:(c + 1) * P], hT[:, k, :], start=k == 0,
                                                    stop=k == KD - 1)
                        last.then_inc(s_q0, 1)
                    for c in range(2):
                        eng.wait_ge(s_q1, c + 1)
                        for i in range(NT):
                            last = head_sums(B[2], 4 * c + i, qx_rs[:, c, i * P:(i + 1) * P], head_mean)
                    last.then_inc(s_q2, 1)
                    eng.wait_ge(s_q5, 1)
                    for c in range(2):
                        for i in range(NT):
                            j = 2 * (4 * c + i)
                            last = head_spread(B[2 + c][:, i * P:(i + 1) * P], xf[:, j:j + 2])
                        last.then_inc(s_q6, 1)
                    eng.wait_ge(s_q4, 2)
                    for h in range(HEADS):
                        rows = slice(64 * (h % 2), 64 * (h % 2) + 64)
                        if h >= 2:
                            eng.wait_ge(s_xe, 4 * (h - 1))
                        for i in range(NT):
                            last = nc.tensor.matmul(B[2 * (h % 2) + i // 2][:, (i % 2) * MEM:(i % 2 + 1) * MEM],
                                                    qx[rows, h // 2, i * P:(i + 1) * P], memKT[rows, h // 2, :],
                                                    start=True, stop=True)
                        last.then_inc(s_xs, 1)
                        if h >= 2:
                            flip_x(eng, h - 2)
                            pv_x(eng, h - 2)
                    for h in (HEADS - 2, HEADS - 1):
                        flip_x(eng, h)
                        pv_x(eng, h)
                    eng.wait_ge(s_xo, HEADS)
                    for c in range(KD):
                        if c >= 4:
                            eng.wait_ge(s_or, KD + c - 3)
                        for k in range(2):
                            last = nc.tensor.matmul(B[c % 4][:, :], wmo[:, k, c * P:(c + 1) * P], oX[:, k, :],
                                                    start=k == 0, stop=k == 1)
                        last.then_inc(s_o, 1)
                    norm_mean(eng, 2, nrm_acc)

                @block.scalar
                def _(eng):
                    a = ach.on(eng)
                    norm_squares(eng, 1, nrm_sq, grown=0)
                    norm_root(eng, 1)
                    for c in range(2):
                        eng.wait_ge(s_q0, c + 1)
                        eng.activation(qx_rs[:, c, :], B[c][:, :], ACT.Square).then_inc(s_q1, 1)
                    eng.wait_ge(s_q2, 1)
                    eng.activation(xf, B[2][:, 0:16], ACT.Sqrt, bias=epsc[:, 0:1]).then_inc(s_q3, 1)
                    for h in range(HEADS):
                        eng.wait_ge(s_xm, h + 1)
                        if h >= 2:
                            eng.wait_ge(s_xf, 2 * (h - 1))
                        for i in range(NT):
                            n = 4 * h + i
                            eng.activation(Px[h % 2][:, i, :],
                                           B[2 * (h % 2) + i // 2][:, (i % 2) * MEM:(i % 2 + 1) * MEM], ACT.Exp,
                                           scale=SCX, bias=mxx[:, n:n + 1], accum_out=smx[:, n:n + 1]
                                           ).then_inc(s_xe, 1)
                        if h:
                            copy_x(eng, h - 1)
                        if h >= 2:
                            out_x(eng, h - 2)
                    copy_x(eng, HEADS - 1)
                    out_x(eng, HEADS - 2)
                    out_x(eng, HEADS - 1)
                    norm_squares(eng, 2, nrm_sq, grown=KD)

                @block.vector
                def _(eng):
                    v = vch.on(eng)

                    def add_out(first):
                        for c in range(KD):
                            eng.wait_ge(s_o, first + c + 1)
                            eng.tensor_tensor(xT[:, c, :], xT[:, c, :], B[c % 4][:, :], ALU.add).then_inc(s_or, 1)
                            if c:
                                norm_add(eng, 1 + first // KD, c - 1, nrm_sq, nrm_acc)
                        norm_add(eng, 1 + first // KD, KD - 1, nrm_sq, nrm_acc)
                    add_out(0)
                    norm_scale(eng, 1, "g_mem")
                    for c in range(2):
                        if c == 0:
                            eng.wait_ge(s_q3, 1)
                            eng.reciprocal(xf, xf).then_inc(s_q5, 1)
                        eng.wait_ge(s_q6, c + 1)
                        eng.tensor_copy(qx_rs[:, c, :], B[2 + c][:, :]).then_inc(s_q7, 1)
                        eng.wait_ge(s_q7, c + 1)
                        eng.scalar_tensor_tensor(out=qx[:, c, :], in0=B[c][:, :], scalar=col("xq_g"),
                                                 in1=qx_rs[:, c, :], op0=ALU.mult, op1=ALU.mult).then_inc(s_q4, 1)
                    for h in range(HEADS):
                        eng.wait_ge(s_xs, h + 1)
                        for z in range(2):
                            last = eng.tensor_reduce(mxx[:, 4 * h + 2 * z:4 * h + 2 * z + 2],
                                                     B[2 * (h % 2) + z][:, :].rearrange("p (i m) -> p i m", i=2),
                                                     AX, ALU.max)
                        v(last)
                        eng.tensor_scalar(mxx[:, 4 * h:4 * h + 4], mxx[:, 4 * h:4 * h + 4], -SCX, None,
                                          ALU.mult).then_inc(s_xm, 1)
                        if h:
                            norm_x(eng, v, h - 1)
                    norm_x(eng, v, HEADS - 1)
                    add_out(KD)

            end_stage()
            htok = arena[:, 0:4096].rearrange("p (i n) -> p i n", i=NT)
            xr = [arena[:, 4096 + 512 * u:4608 + 512 * u] for u in range(2)]
            sel = [arena[:, 5120 + 256 * u:5376 + 256 * u].rearrange("p (i s) -> p i s", i=NT) for u in range(2)]
            xg = [arena[:, 5632 + 512 * u:6144 + 512 * u] for u in range(2)]
            hr = [arena[:, 6656 + 512 * u:7168 + 512 * u] for u in range(2)]
            sg = [arena[:, 7680 + 256 * u:7936 + 256 * u].rearrange("p (m s) -> p m s", m=HM) for u in range(2)]
            hid = [arena[:, 8192 + 256 * u:8448 + 256 * u].rearrange("p (m s) -> p m s", m=HM) for u in range(2)]
            ysb = [arena[:, 8704 + 512 * u:9216 + 512 * u] for u in range(2)]
            lg = arena[:, 9728:9872].rearrange("p (i n) -> p i n", i=NT)
            em, oh1, oh2, M, tmp = [arena[:, 9872 + 128 * z:10000 + 128 * z].rearrange("p (i n) -> p i n", i=NT)
                                    for z in range(5)]
            rankm = arena[:, 10512:10644].rearrange("p (e i) -> p e i", i=NT)
            rank = arena[:, 10644:10772].rearrange("p (i n) -> p i n", i=NT)
            gmax, gsum, m1, m2, ratio, gate1, gate2, idx, slot = [small[:, 4 * z:4 * z + 4] for z in range(9)]
            eg, goh, gt = [small[:, 64 + 16 * z:80 + 16 * z].rearrange("p (i n) -> p i n", i=NT) for z in range(3)]
            gates = em
            spread = xr[1]
            cntf = small[:, 128:160]
            slots_i = [smalli[:, 4 * k:4 * k + 4] for k in range(2)]
            passes_i, most_i = smalli[0:1, 16:48], smalli[0:1, 48:49]
            s_lg, s_ht, s_htc = sem("logits"), sem("h_flipped"), sem("h_token_major")
            s_gd, s_ge2, s_rt2, s_rk = sem("group_logits"), sem("group_exps"), sem("chosen"), sem("ranks")
            s_ed, s_ee = sem("expert_difference"), sem("expert_ratio")
            s_sel, s_g, s_xr, s_tx = sem("selection"), sem("gathered"), sem("gather_copied"), sem("gather_flipped")
            s_xg, s_mu, s_hr, s_th = sem("tokens_ready"), sem("up_done"), sem("up_copied"), sem("up_flipped")
            s_sg, s_hd, s_dn, s_ys = sem("silu_done"), sem("hidden_ready"), sem("down_done"), sem("rows_ready")
            s_yo = [sem(f"rows_written{u}") for u in range(2)]
            s_cb, s_cf = sem("combined"), sem("combine_flipped")

            def bc(ap, n):
                return ap.unsqueeze(2).to_broadcast([P, NT, n])

            def row(ap, n):
                return ap.unsqueeze(1).to_broadcast([P, NT, n])

            with nc.Block() as block:
                @block.sync
                def _(eng):
                    load_up(eng, 1, 1, s_e[3:5])
                    load_down(eng, 1, 1, s_e[5])

                @block.tensor
                def _(eng):
                    norm_spread(eng, 2)
                    for i in range(NT):
                        for k in range(KD):
                            if i == 0:
                                eng.wait_ge(s_h, 2 * KD + k + 1)
                            last = nc.tensor.matmul(B[0][:, i * 36:(i + 1) * 36], hT[:, k, i * P:(i + 1) * P],
                                                    wr[:, k, :], start=k == 0, stop=k == KD - 1)
                    last.then_inc(s_lg, 1)
                    for z in range(2 * NT):
                        if z >= 4:
                            eng.wait_ge(s_htc, z - 3)
                        for k in range(4):
                            kk = 4 * (z % 2) + k
                            last = nc.tensor.transpose(B[3 + z % 4][:, k * P:(k + 1) * P],
                                                       hT[:, kk, (z // 2) * P:(z // 2 + 1) * P], ident[:, :])
                        last.then_inc(s_ht, 1)
                    eng.wait_ge(s_rt2, 1)
                    for i in range(NT):
                        for j in range(i):
                            nc.tensor.matmul(B[1][:, i * NE:(i + 1) * NE], ones[:, :], M[:, j, :], start=j == 0,
                                             stop=False)
                        nc.tensor.matmul(B[1][:, i * NE:(i + 1) * NE], before[:, :], M[:, i, :], start=i == 0,
                                         stop=True)
                    for i in range(NT):
                        last = nc.tensor.matmul(B[2][:, 0:NE], ones[:, :], M[:, i, :], start=i == 0,
                                                stop=i == NT - 1)
                    last.then_inc(s_rk, 1)

                @block.scalar
                def _(eng):
                    norm_root(eng, 2)
                    for z in range(2 * NT):
                        eng.wait_ge(s_ht, z + 1)
                        eng.activation(htok[:, z // 2, 512 * (z % 2):512 * (z % 2) + 512], B[3 + z % 4][:, :],
                                       ACT.Copy).then_inc(s_htc, 1)
                    eng.wait_ge(s_gd, 1)
                    eng.activation(eg, eg, ACT.Exp).then_inc(s_ge2, 1)
                    eng.wait_ge(s_ed, 1)
                    eng.activation(ratio, ratio, ACT.Exp).then_inc(s_ee, 1)

                @block.vector
                def _(eng):
                    v = vch.on(eng)
                    norm_scale(eng, 2, "g_ffn")
                    eng.wait_ge(s_lg, 1)
                    v(eng.tensor_tensor(lg, B[0][:, 0:144].rearrange("p (i n) -> p i n", i=NT), row(brb[:, :], 36),
                                        ALU.add))

                    def first_max(src, n, best, out, t):
                        v(eng.tensor_reduce(best, src, AX, ALU.max))
                        v(eng.tensor_tensor(out, src, bc(best, n), ALU.is_ge))
                        v(eng.scalar_tensor_tensor(out=t, in0=out, scalar=-1000.0, in1=row(slot_iota[:, 0:n], n),
                                                   op0=ALU.mult, op1=ALU.add))
                        v(eng.tensor_reduce(idx, t, AX, ALU.min))
                        v(eng.tensor_tensor(out, t, bc(idx, n), ALU.is_equal))
                    first_max(lg[:, :, 0:NG], NG, gmax, goh, gt)
                    v(eng.tensor_tensor(eg, lg[:, :, 0:NG], bc(gmax, NG), ALU.subtract))
                    eng.sem_inc(s_gd, 1)
                    v(eng.tensor_scalar(gt, goh, BIG, -BIG, ALU.mult, ALU.add))
                    v(eng.tensor_tensor(em.rearrange("p i (g n) -> p i g n", g=NG),
                                        lg[:, :, NG:NG + NE].rearrange("p i (g n) -> p i g n", g=NG),
                                        gt.unsqueeze(3).to_broadcast([P, NT, NG, EPG]), ALU.add))
                    first_max(em, NE, m1, oh1, tmp)
                    v(eng.scalar_tensor_tensor(out=em, in0=oh1, scalar=-2 * BIG, in1=em, op0=ALU.mult, op1=ALU.add))
                    first_max(em, NE, m2, oh2, tmp)
                    v(eng.tensor_tensor(M, oh1, oh2, ALU.add))
                    eng.sem_inc(s_rt2, 1)
                    v(eng.tensor_tensor(ratio, m2, m1, ALU.subtract))
                    eng.sem_inc(s_ed, 1)
                    eng.wait_ge(s_ge2, 1)
                    v(eng.tensor_reduce(gsum, eg, AX, ALU.add))
                    eng.wait_ge(s_ee, 1)
                    v(eng.scalar_tensor_tensor(out=gate1, in0=ratio, scalar=1.0, in1=gsum, op0=ALU.add, op1=ALU.mult))
                    v(eng.reciprocal(gate1, gate1))
                    v(eng.tensor_tensor(gate2, gate1, ratio, ALU.mult))
                    eng.wait_ge(s_rk, 1)
                    v(eng.tensor_scalar(tmp, M, 1e5, -1e5, ALU.mult, ALU.add))
                    v(eng.tensor_copy(rank, B[1][:, 0:128].rearrange("p (i n) -> p i n", i=NT)))
                    v(eng.tensor_tensor(rankm[:, 0:NE, :].rearrange("p e i -> p i e"), rank, tmp, ALU.add))
                    v(eng.memset(rankm[:, NE, :], -1e5))
                    v(eng.tensor_tensor(gates, oh1, bc(gate1, NE), ALU.mult))
                    v(eng.tensor_tensor(tmp, oh2, bc(gate2, NE), ALU.mult))
                    v(eng.tensor_tensor(gates, gates, tmp, ALU.add))
                    for k, (oh, gate) in enumerate(((oh1, gate1), (oh2, gate2))):
                        v(eng.tensor_tensor(tmp, rank, oh, ALU.mult))
                        v(eng.tensor_reduce(slot, tmp, AX, ALU.add))
                        v(eng.tensor_scalar(idx, slot, float(CAP), None, ALU.is_lt))
                        v(eng.tensor_tensor(gate, gate, idx, ALU.mult))
                        v(eng.tensor_tensor(tmp, oh, row(slot0[:, :], NE), ALU.mult))
                        v(eng.tensor_reduce(idx, tmp, AX, ALU.add))
                        v(eng.scalar_tensor_tensor(out=slot, in0=slot, scalar=float(CAP - 1), in1=idx,
                                                   op0=ALU.min, op1=ALU.add))
                        v(eng.tensor_copy(slots_i[k], slot))
                    passes = cntf[0:1, :]
                    v(eng.memset(passes, 1.0))
                    for b in range(1, SEQ // CAP):
                        v(eng.scalar_tensor_tensor(out=passes, in0=B[2][0:1, 0:NE], scalar=float(b * CAP), in1=passes,
                                                   op0=ALU.is_gt, op1=ALU.add))
                    v(eng.tensor_copy(passes_i, passes))
                    v(eng.tensor_reduce(passes[:, 0:1], passes, AX, ALU.max))
                    v(eng.tensor_copy(most_i, passes[:, 0:1]))

            def pe_gather(u):
                for i in range(NT):
                    for half in range(2):
                        last = nc.tensor.matmul(B[u][CAP * half:CAP * half + CAP, :], sel[u][:, i, :],
                                                htok[:, i, 512 * half:512 * half + 512], start=i == 0,
                                                stop=i == NT - 1)
                return last

            def pe_flip(bank, src):
                for j in range(4):
                    last = nc.tensor.transpose(bank[:, j * P:(j + 1) * P], src[:, j * P:(j + 1) * P], ident[:, :])
                return last

            def pe_up(u):
                for k in range(KD):
                    o = (k % 4) * P + (k // 4) * CAP
                    for half, w in enumerate((w1v[u], w3v[u])):
                        last = nc.tensor.matmul(B[3 + 3 * u][CAP * half:CAP * half + CAP, :], xg[u][:, o:o + CAP],
                                                w[:, k, :], start=k == 0, stop=k == KD - 1)
                return last

            def pe_down(u):
                for m in range(HM):
                    for half in range(2):
                        last = nc.tensor.matmul(B[5 + 2 * u][CAP * half:CAP * half + CAP, :], hid[u][:, m, :],
                                                w2v[u][:, m, 512 * half:512 * half + 512], start=m == 0,
                                                stop=m == HM - 1)
                return last

            def up_half(half):
                return B[4][:, :].rearrange("p (m a s) -> p m a s", m=HM, a=2)[:, :, half, :]

            def expert_rows(e):
                return ys_d[bass.ds(e * CAP, CAP), :].rearrange("s (a n) -> a s n", a=2)

            def select(eng, u, ranks):
                return eng.tensor_tensor(sel[u], slot_iota[:, 0:CAP].unsqueeze(1).to_broadcast([P, NT, CAP]),
                                         ranks.rearrange("p a i -> p (a i)").unsqueeze(2).to_broadcast([P, NT, CAP]),
                                         ALU.is_equal)

            with nc.Block() as block:
                @block.sync
                def _(eng):
                    eng.sem_inc(s_yo[0], 16)
                    eng.sem_inc(s_yo[1], 16)

                    def store_rows(u, i):
                        eng.wait_ge(s_ys, 2 * i + (u + 3))
                        eng.dma_start(expert_rows(2 * i + u), ysb[u]).then_inc(s_yo[u], 16)
                    with eng.Fori(0, NE // 2 - 1) as i:
                        for u in range(2):
                            eng.wait_ge(s_mu, 2 * i + (u + 1))
                            load_up(eng, u, 2 * i + (u + 2), s_e[3 * u:3 * u + 2])
                            eng.wait_ge(s_dn, 2 * i + (u + 1))
                            load_down(eng, u, 2 * i + (u + 2), s_e[3 * u + 2])
                            store_rows(u, i)
                    for u in range(2):
                        store_rows(u, NE // 2 - 1)
                    for u in range(2):
                        eng.wait_ge(s_yo[u], 16 * (NE // 2 + 1))

                @block.tensor
                def _(eng):
                    eng.wait_ge(s_sel, 1)
                    pe_gather(0).then_inc(s_g, 1)
                    eng.wait_ge(s_xr, 1)
                    pe_flip(B[2], xr[0]).then_inc(s_tx, 1)
                    with eng.Fori(0, NE // 2) as i:
                        for u in range(2):
                            eng.wait_ge(s_e[3 * u], 16 * i + 16)
                            eng.wait_ge(s_e[3 * u + 1], 16 * i + 16)
                            eng.wait_ge(s_xg, 2 * i + (u + 1))
                            pe_up(u).then_inc(s_mu, 1)
                            eng.wait_ge(s_sel, 2 * i + (u + 2))
                            pe_gather(1 - u).then_inc(s_g, 1)
                            eng.wait_ge(s_hr, 2 * i + (u + 1))
                            pe_flip(B[4], hr[u]).then_inc(s_th, 1)
                            eng.wait_ge(s_xr, 2 * i + (u + 2))
                            pe_flip(B[2], xr[1 - u]).then_inc(s_tx, 1)
                            eng.wait_ge(s_e[3 * u + 2], 16 * i + 16)
                            eng.wait_ge(s_ys, 2 * i + (u + 1))
                            eng.wait_ge(s_hd, 2 * i + (u + 1))
                            pe_down(u).then_inc(s_dn, 1)

                @block.scalar
                def _(eng):
                    eng.wait_ge(s_g, 1)
                    eng.activation(xr[0], B[0][:, :], ACT.Copy).then_inc(s_xr, 1)
                    with eng.Fori(0, NE // 2) as i:
                        for u in range(2):
                            eng.wait_ge(s_mu, 2 * i + (u + 1))
                            eng.activation(hr[u], B[3 + 3 * u][:, :], ACT.Copy).then_inc(s_hr, 1)
                            eng.wait_ge(s_g, 2 * i + (u + 2))
                            eng.activation(xr[1 - u], B[1 - u][:, :], ACT.Copy).then_inc(s_xr, 1)
                            eng.wait_ge(s_th, 2 * i + (u + 1))
                            eng.activation(sg[u], up_half(0), ACT.Silu).then_inc(s_sg, 1)

                @block.vector
                def _(eng):
                    eng.sem_inc(s_ys, 2)
                    select(eng, 0, rankm[:, 0:1, :]).then_inc(s_sel, 1)
                    eng.wait_ge(s_tx, 1)
                    eng.tensor_copy(xg[0], B[2][:, :]).then_inc(s_xg, 1)
                    with eng.Fori(0, NE // 2) as i:
                        for u in range(2):
                            eng.wait_ge(s_g, 2 * i + (u + 1))
                            select(eng, 1 - u, rankm[:, bass.ds(2 * i + (u + 1), 1), :]).then_inc(s_sel, 1)
                            eng.wait_ge(s_sg, 2 * i + (u + 1))
                            eng.tensor_tensor(hid[u], sg[u], up_half(1), ALU.mult).then_inc(s_hd, 1)
                            eng.wait_ge(s_tx, 2 * i + (u + 2))
                            eng.tensor_copy(xg[1 - u], B[2][:, :]).then_inc(s_xg, 1)
                            eng.wait_ge(s_dn, 2 * i + (u + 1))
                            eng.wait_ge(s_yo[u], 16 * i + 16)
                            eng.tensor_copy(ysb[u], B[5 + 2 * u][:, :]).then_inc(s_ys, 1)

            o_sem = {x: sem("more_" + x) for x in ("w", "sel", "g", "xr", "tx", "xg", "up", "hr", "th", "sg", "hid",
                                                   "dn", "ys", "sp", "spt", "spc", "add")}
            most = nc.values_load(most_i, min_val=1, max_val=SEQ // CAP)
            with nc.If(most > 1):
                with nc.Fori(0, NE) as e:
                    passes = nc.values_load(smalli[0:1, bass.ds(16 + e, 1)], min_val=1, max_val=SEQ // CAP)
                    with nc.If(passes > 1):
                        with nc.Fori(1, passes) as b:
                            with nc.Block() as block:
                                @block.sync
                                def _(eng):
                                    load_up(eng, 0, e, (o_sem["w"], o_sem["w"]))
                                    load_down(eng, 0, e, o_sem["w"])
                                    eng.wait_ge(o_sem["w"], 48)

                                @block.tensor
                                def _(eng):
                                    eng.wait_ge(o_sem["sel"], 1)
                                    pe_gather(0).then_inc(o_sem["g"], 1)
                                    eng.wait_ge(o_sem["xr"], 1)
                                    pe_flip(B[2], xr[0]).then_inc(o_sem["tx"], 1)
                                    eng.wait_ge(o_sem["w"], 48)
                                    eng.wait_ge(o_sem["xg"], 1)
                                    pe_up(0).then_inc(o_sem["up"], 1)
                                    eng.wait_ge(o_sem["hr"], 1)
                                    pe_flip(B[4], hr[0]).then_inc(o_sem["th"], 1)
                                    eng.wait_ge(o_sem["hid"], 1)
                                    pe_down(0).then_inc(o_sem["dn"], 1)
                                    eng.wait_ge(o_sem["sp"], 1)
                                    pe_flip(B[1], hr[1]).then_inc(o_sem["spt"], 1)
                                    eng.wait_ge(o_sem["spc"], 1)
                                    eng.wait_ge(o_sem["ys"], 1)
                                    for k in range(KD):
                                        rows = slice(CAP * (k // 4), CAP * (k // 4) + CAP)
                                        nc.tensor.matmul(B[k][:, :], ysb[0][rows, (k % 4) * P:(k % 4 + 1) * P],
                                                         spread[rows, :], start=True,
                                                         stop=True).then_inc(o_sem["add"], 1)

                                @block.scalar
                                def _(eng):
                                    eng.wait_ge(o_sem["g"], 1)
                                    eng.activation(xr[0], B[0][:, :], ACT.Copy).then_inc(o_sem["xr"], 1)
                                    eng.wait_ge(o_sem["up"], 1)
                                    eng.activation(hr[0], B[3][:, :], ACT.Copy).then_inc(o_sem["hr"], 1)
                                    eng.wait_ge(o_sem["th"], 1)
                                    eng.activation(sg[0], up_half(0), ACT.Silu).then_inc(o_sem["sg"], 1)
                                    eng.wait_ge(o_sem["spt"], 1)
                                    eng.activation(spread, B[1][:, :], ACT.Copy).then_inc(o_sem["spc"], 1)

                                @block.vector
                                def _(eng):
                                    eng.tensor_tensor(
                                        sel[0],
                                        slot_iota[:, bass.ds(b * CAP, CAP)].unsqueeze(1).to_broadcast([P, NT, CAP]),
                                        rankm[:, bass.ds(e, 1), :].rearrange("p a i -> p (a i)").unsqueeze(2)
                                        .to_broadcast([P, NT, CAP]), ALU.is_equal).then_inc(o_sem["sel"], 1)
                                    eng.wait_ge(o_sem["sel"], 1)
                                    for half in range(2):
                                        last = eng.tensor_tensor(
                                            hr[1].rearrange("p (i a s) -> p i a s", i=NT, a=2)[:, :, half, :], sel[0],
                                            gates[:, :, bass.ds(e, 1)].to_broadcast([P, NT, CAP]), ALU.mult)
                                    last.then_inc(o_sem["sp"], 1)
                                    eng.wait_ge(o_sem["tx"], 1)
                                    eng.tensor_copy(xg[0], B[2][:, :]).then_inc(o_sem["xg"], 1)
                                    eng.wait_ge(o_sem["sg"], 1)
                                    eng.tensor_tensor(hid[0], sg[0], up_half(1), ALU.mult).then_inc(o_sem["hid"], 1)
                                    eng.wait_ge(o_sem["dn"], 1)
                                    eng.tensor_copy(ysb[0], B[5][:, :]).then_inc(o_sem["ys"], 1)
                                    for k in range(KD):
                                        eng.wait_ge(o_sem["add"], k + 1)
                                        eng.tensor_tensor(xT[:, k, :], xT[:, k, :], B[k][:, :], ALU.add)
                            clear(o_sem.values())
                            nc.all_engine_barrier()
                        for eng in (nc.sync, nc.gpsimd, nc.scalar, nc.vector, nc.tensor):
                            eng.nop()
                    for eng in (nc.sync, nc.gpsimd, nc.scalar, nc.vector, nc.tensor):
                        eng.nop()
                for eng in (nc.sync, nc.gpsimd, nc.scalar, nc.vector, nc.tensor):
                    eng.nop()

            def add_rows(eng, i):
                eng.wait_ge(s_cf, i + 1)
                for half in range(2):
                    x = xT[:, 4 * half:4 * half + 4, i * P:(i + 1) * P]
                    eng.tensor_tensor(x, x, B[2 * i + half][:, :].rearrange("p (k t) -> p k t", k=4), ALU.add)

            yg = [[ring_view(2 * k + i // 2, 2048 * (i % 2), 1024) for i in range(NT)] for k in range(2)]
            with nc.Block() as block:
                @block.gpsimd
                def _(eng):
                    for i in range(NT):
                        for k in range(2):
                            eng.indirect_dma_start(out=yg[k][i], out_offset=None, in_=ys_d,
                                                   in_offset=bass.IndirectOffsetOnAxis(ap=slots_i[k][:, i:i + 1],
                                                                                       axis=0)).then_inc(s_ygs[i], 16)

                @block.vector
                def _(eng):
                    v = vch.on(eng)
                    for i in range(NT):
                        eng.wait_ge(s_ygs[i], 32 * layer + 32)
                        v(eng.tensor_scalar(yg[0][i], yg[0][i], gate1[:, i:i + 1], None, ALU.mult))
                        eng.scalar_tensor_tensor(out=yg[0][i], in0=yg[1][i], scalar=gate2[:, i:i + 1], in1=yg[0][i],
                                                 op0=ALU.mult, op1=ALU.add).then_inc(s_cb, 1)
                        if i:
                            add_rows(eng, i - 1)
                    add_rows(eng, NT - 1)

                @block.tensor
                def _(eng):
                    for i in range(NT):
                        eng.wait_ge(s_cb, i + 1)
                        for half in range(2):
                            for k in range(4):
                                kk = 4 * half + k
                                last = nc.tensor.transpose(B[2 * i + half][:, k * P:(k + 1) * P],
                                                           yg[0][i][:, kk * P:(kk + 1) * P], ident[:, :])
                        last.then_inc(s_cf, 1)

            clear(layer_sems)
            end_stage()

        s_out = ctx.enter_context(nc.semaphore("out_written"))
        with nc.Block() as block:
            @block.sync
            def _(eng):
                eng.dma_start(out_d, xT[:, :, :]).then_inc(s_out, 16)
                eng.wait_ge(s_out, 16)


_F = np.float32


def pack(inputs):
    c = np.ascontiguousarray
    L = DEPTH

    def cols(a, n):
        return a.reshape(L, n, P).transpose(0, 2, 1)

    def zeros(*s):
        return np.zeros(s, _F)
    i = {k: np.asarray(v) for k, v in inputs.items()}
    mu = np.concatenate([i["shift_mu"], zeros(L, 15 * P - i["shift_mu"].shape[1])], 1)
    qn = i["mla_q_norm_g"]
    cq = np.stack([np.concatenate([zeros(L, 32), qn[:, :96]], 1), np.concatenate([qn[:, 96:], zeros(L, 32)], 1)], 2)
    pad32 = zeros(L, 32)
    colp = np.concatenate([
        cols(i["norm_mix_g"], 8), cols(i["norm_mem_g"], 8), cols(i["norm_ffn_g"], 8), cols(mu, 15),
        cols(i["rwkv_w0"], 4), cols(i["rwkv_a0"], 4), cols(i["rwkv_k_k"], 4), cols(i["rwkv_k_a"], 4),
        cols(i["rwkv_r_k"].reshape(L, 512), 4), cols(i["rwkv_ln_g"], 4), cols(i["rwkv_ln_b"], 4), cq,
        i["mla_kv_norm_g"][:, :, None], np.concatenate([i["mla_q_g"], pad32], 1)[:, :, None],
        np.concatenate([i["mla_k_g"], pad32], 1)[:, :, None], cols(i["gmlp_v_norm_g"], 2),
        np.concatenate([i["mem_q_g"], i["mem_q_g"]], 1)[:, :, None]], 2)
    memcol = np.concatenate([i["mem_norm_g"].reshape(8, P).T,
                             np.concatenate([i["mem_k_g"], i["mem_k_g"]])[:, None]], 1)
    wuq = i["mla_w_uq"]
    wuq = np.stack([np.concatenate([zeros(L, 32, 384), wuq[:, :96]], 1),
                    np.concatenate([wuq[:, 96:], zeros(L, 32, 384)], 1)], 2)
    wr = np.concatenate([i["moe_w_group"], i["moe_w_expert"]], 2).reshape(L, 8, P, NG + NE).transpose(0, 2, 1, 3)
    inv = np.power(_F(10000.0), -np.arange(HALF, dtype=_F) * _F(2.0) / _F(32)).astype(_F)
    gup = i["rwkv_g_up"]
    out = {
        "xT": i["x"][0].T.reshape(KD, P, SEQ).transpose(1, 0, 2),
        "memT": i["mem"][0].T.reshape(KD, P, MEM).transpose(1, 0, 2),
        "pos": i["positions"][0].reshape(NT, P).T,
        "inv": np.repeat(inv[None], P, 0),
        "colp": colp, "memcol": memcol, "w_in": i["w_in"],
        "lora": np.concatenate([i["rwkv_w_up"], i["rwkv_a_up"]], 1),
        "gup": gup[:, :P], "gup2": gup[:, P:], "wuq": wuq, "wukv": i["mla_w_ukv"],
        "wsT": i["gmlp_ws"].transpose(0, 3, 1, 2), "gb": i["gmlp_b"], "w_out": i["w_out"], "wkv": i["mem_w_kv"],
        "wmq": i["mem_w_q"], "wmo": i["mem_w_o"], "wr": wr,
        "br": np.concatenate([i["moe_b_group"], i["moe_b_expert"]], 1),
        "w1": i["moe_w1"].reshape(L * NE, D, DE), "w3": i["moe_w3"].reshape(L * NE, D, DE),
        "w2": i["moe_w2"].reshape(L * NE, DE, D),
    }
    return {k: c(a) for k, a in out.items()}


def kernel(**inputs):
    import concourse.bacc as _bacc
    from concourse.bass_utils import run_bass_kernel_spmd as _run

    nc = _bacc.Bacc("TRN2", target_bir_lowering=False, num_devices=1)
    arrays, args = {}, []
    for name, a in pack(inputs).items():
        arrays[f"in_{name}"] = a
        args.append(nc.dram_tensor(f"in_{name}", a.shape, mybir.dt.from_np(a.dtype), kind="ExternalInput").ap())
    out = nc.dram_tensor("out_xT", (P, KD, SEQ), F32, kind="ExternalOutput").ap()
    build(nc, *args, out)
    r = _run(nc, [arrays], core_ids=[0])
    got = r.results[0]["out_xT"]
    return np.ascontiguousarray(got.transpose(1, 0, 2).reshape(D, SEQ).T)[None]
```
